# Optimizing a Trainium2 kernel written in Bass

```python
import math
import jax, jax.numpy as jnp
from jax import lax
import numpy as np

D_MODEL = 2048
BATCH = 1
SEQ = 512
DEPTH = 1

A_HEADS = 16
A_KV_HEADS = 4
A_HEAD_DIM = 64
A_GROUP = A_HEADS // A_KV_HEADS
WINDOW = 128
BAND_BLOCK = 128
B_HEADS = 16
B_Q_LORA = 512
B_KV_LORA = 256
B_NOPE = 64
B_ROPE = 32
B_V = 64
ROPE_THETA = 10000.0
Q_BLOCK = 128
D_FF = 4 * D_MODEL
EPS = 1e-6
NEG_INF = -1e30

A_Q_W = A_HEADS * A_HEAD_DIM
A_KV_W = A_KV_HEADS * A_HEAD_DIM
A_OUT_W = A_HEADS * A_HEAD_DIM
B_OUT_W = B_HEADS * B_V
IN_SPLITS = (A_Q_W, A_KV_W, A_KV_W, B_Q_LORA, B_KV_LORA, B_ROPE, D_MODEL, D_MODEL)
IN_WIDTH = int(sum(IN_SPLITS))
IN_OFFSETS = tuple(int(v) for v in np.cumsum(IN_SPLITS)[:-1])

kernel_name = "gated_swa_mla_hybrid_encoder"

def rms_norm(x, g):
    xf = x.astype(jnp.float32)
    y = xf * lax.rsqrt(jnp.mean(xf * xf, axis=-1, keepdims=True) + EPS)
    return (y * g.astype(jnp.float32)).astype(x.dtype)

def alibi_slopes(n_heads):
    return jnp.exp2(-8.0 * (jnp.arange(n_heads, dtype=jnp.float32) + 1.0) / n_heads)

def apply_rope(x, pos):
    half = x.shape[-1] // 2
    inv = ROPE_THETA ** (-jnp.arange(half, dtype=jnp.float32) / half)
    ang = pos.astype(jnp.float32)[..., None] * inv
    cos = jnp.cos(ang)[:, :, None, :]
    sin = jnp.sin(ang)[:, :, None, :]
    x1 = x[..., :half].astype(jnp.float32)
    x2 = x[..., half:].astype(jnp.float32)
    out = jnp.concatenate([x1 * cos - x2 * sin, x2 * cos + x1 * sin], axis=-1)
    return out.astype(x.dtype)

def band_blocks(t, n_blocks):
    b = t.shape[0]
    pad = [(0, 0), (BAND_BLOCK, BAND_BLOCK)] + [(0, 0)] * (t.ndim - 2)
    tb = jnp.pad(t, pad).reshape(b, n_blocks + 2, BAND_BLOCK, *t.shape[2:])
    return jnp.concatenate([tb[:, :-2], tb[:, 1:-1], tb[:, 2:]], axis=2)

def windowed_gqa_sink(q, k, v, pos, sink):
    b, s = q.shape[0], q.shape[1]
    nb = s // BAND_BLOCK
    qb = q.reshape(b, nb, BAND_BLOCK, A_KV_HEADS, A_GROUP, A_HEAD_DIM)
    kb = band_blocks(k, nb)
    vb = band_blocks(v, nb)
    r = jnp.arange(BAND_BLOCK, dtype=jnp.int32)[:, None]
    c = jnp.arange(3 * BAND_BLOCK, dtype=jnp.int32)[None, :]
    in_win = jnp.abs(BAND_BLOCK + r - c) <= WINDOW
    kglob = (jnp.arange(nb, dtype=jnp.int32)[:, None, None] - 1) * BAND_BLOCK + c[None]
    mask = in_win[None] & (kglob >= 0) & (kglob < s)
    pq = pos.reshape(b, nb, BAND_BLOCK)
    pk = band_blocks(pos, nb)
    dist = jnp.abs(pq[..., :, None] - pk[..., None, :]).astype(jnp.float32)
    slopes = alibi_slopes(A_HEADS).reshape(A_KV_HEADS, A_GROUP)
    scale = A_HEAD_DIM ** -0.5
    scores = jnp.einsum('bnqhgd,bnchd->bnhgqc', qb, kb).astype(jnp.float32) * scale
    scores = scores - slopes[None, None, :, :, None, None] * dist[:, :, None, None]
    scores = jnp.where(mask[None, :, None, None], scores, NEG_INF)
    sk = sink.astype(jnp.float32).reshape(A_KV_HEADS, A_GROUP)[None, None, :, :, None, None]
    m = jnp.maximum(jnp.max(scores, axis=-1, keepdims=True), sk)
    p = jnp.exp(scores - m)
    denom = jnp.sum(p, axis=-1, keepdims=True) + jnp.exp(sk - m)
    probs = (p / denom).astype(v.dtype)
    out = jnp.einsum('bnhgqc,bnchd->bnqhgd', probs, vb)
    return out.reshape(b, s, A_OUT_W)

def mla_attention(c_q, c_kv, k_r, pos, g_q, g_kv, w_uq, w_uk, w_uv):
    b, s = c_q.shape[0], c_q.shape[1]
    c_q = rms_norm(c_q, g_q)
    c_kv = rms_norm(c_kv, g_kv)
    q = jnp.einsum('bsc,chd->bshd', c_q, w_uq)
    q_nope = q[..., :B_NOPE]
    q_rope = apply_rope(q[..., B_NOPE:], pos)
    k_nope = jnp.einsum('bsc,chd->bshd', c_kv, w_uk)
    val = jnp.einsum('bsc,chd->bshd', c_kv, w_uv)
    k_rope = apply_rope(k_r[:, :, None, :], pos)[:, :, 0]
    scale = (B_NOPE + B_ROPE) ** -0.5
    nb = s // Q_BLOCK
    qn = q_nope.reshape(b, nb, Q_BLOCK, B_HEADS, B_NOPE).transpose(1, 0, 2, 3, 4)
    qr = q_rope.reshape(b, nb, Q_BLOCK, B_HEADS, B_ROPE).transpose(1, 0, 2, 3, 4)

    def query_block(args):
        qn_b, qr_b = args
        sc = (jnp.einsum('bqhd,bkhd->bhqk', qn_b, k_nope)
              + jnp.einsum('bqhr,bkr->bhqk', qr_b, k_rope)).astype(jnp.float32) * scale
        p = jax.nn.softmax(sc, axis=-1).astype(val.dtype)
        return jnp.einsum('bhqk,bkhd->bqhd', p, val)

    o = lax.map(query_block, (qn, qr))
    return o.transpose(1, 0, 2, 3, 4).reshape(b, s, B_OUT_W)

def setup_inputs(seed: int = 0) -> dict:
    key = jax.random.key(seed)
    ks = jax.random.split(key, 20)

    def w(k, shape, fan_in):
        return jax.random.normal(k, shape, jnp.float32) * (fan_in ** -0.5)

    def gain(k, shape):
        return 1.0 + 0.02 * jax.random.normal(k, shape, jnp.float32)

    x = jax.random.normal(ks[0], (BATCH, SEQ, D_MODEL), jnp.float32)
    positions = jnp.broadcast_to(jnp.arange(SEQ, dtype=jnp.int32)[None, :], (BATCH, SEQ))
    return {
        "x": x,
        "positions": positions,
        "attn_norm_g": gain(ks[1], (DEPTH, D_MODEL)),
        "w_in": w(ks[2], (DEPTH, D_MODEL, IN_WIDTH), D_MODEL),
        "a_sink": 0.5 * jax.random.normal(ks[3], (DEPTH, A_HEADS), jnp.float32),
        "b_q_norm_g": gain(ks[4], (DEPTH, B_Q_LORA)),
        "b_kv_norm_g": gain(ks[5], (DEPTH, B_KV_LORA)),
        "b_w_uq": w(ks[6], (DEPTH, B_Q_LORA, B_HEADS, B_NOPE + B_ROPE), B_Q_LORA),
        "b_w_uk": w(ks[7], (DEPTH, B_KV_LORA, B_HEADS, B_NOPE), B_KV_LORA),
        "b_w_uv": w(ks[8], (DEPTH, B_KV_LORA, B_HEADS, B_V), B_KV_LORA),
        "w_branch_a": w(ks[9], (DEPTH, A_OUT_W, D_MODEL), A_OUT_W),
        "w_branch_b": w(ks[10], (DEPTH, B_OUT_W, D_MODEL), B_OUT_W),
        "w_out": w(ks[11], (DEPTH, D_MODEL, D_MODEL), D_MODEL),
        "mlp_norm_g": gain(ks[12], (DEPTH, D_MODEL)),
        "w_mlp_in": w(ks[13], (DEPTH, D_MODEL, D_FF), D_MODEL),
        "w_mlp_out": w(ks[14], (DEPTH, D_FF, D_MODEL), D_FF),
        "final_norm_g": gain(ks[15], (D_MODEL,)),
    }

def reference(x, positions, attn_norm_g, w_in, a_sink, b_q_norm_g, b_kv_norm_g,
              b_w_uq, b_w_uk, b_w_uv, w_branch_a, w_branch_b, w_out,
              mlp_norm_g, w_mlp_in, w_mlp_out, final_norm_g):
    b, s, _ = x.shape
    for l in range(DEPTH):
        h = rms_norm(x, attn_norm_g[l])
        proj = jnp.einsum('bsd,de->bse', h, w_in[l])
        qa, ka, va, c_q, c_kv, k_r, gate_a, gate_b = jnp.split(proj, IN_OFFSETS, axis=-1)
        o_a = windowed_gqa_sink(
            qa.reshape(b, s, A_HEADS, A_HEAD_DIM),
            ka.reshape(b, s, A_KV_HEADS, A_HEAD_DIM),
            va.reshape(b, s, A_KV_HEADS, A_HEAD_DIM),
            positions, a_sink[l])
        o_b = mla_attention(c_q, c_kv, k_r, positions, b_q_norm_g[l], b_kv_norm_g[l],
                            b_w_uq[l], b_w_uk[l], b_w_uv[l])
        merged = (jax.nn.sigmoid(gate_a) * jnp.einsum('bse,ed->bsd', o_a, w_branch_a[l])
                  + jax.nn.sigmoid(gate_b) * jnp.einsum('bse,ed->bsd', o_b, w_branch_b[l]))
        x = x + jnp.einsum('bsd,de->bse', merged, w_out[l])
        h2 = rms_norm(x, mlp_norm_g[l])
        u = jax.nn.relu(jnp.einsum('bsd,df->bsf', h2, w_mlp_in[l]))
        x = x + jnp.einsum('bsf,fd->bsd', u * u, w_mlp_out[l])
    return rms_norm(x, final_norm_g)


_drawn_inputs = setup_inputs


def setup_inputs(seed=0):
    import zlib

    import numpy as np

    out = dict(_drawn_inputs(seed))
    spreads = {}
    factors = {'attn_norm_g': 8.0,
     'a_sink': 6.923,
     'b_q_norm_g': 8.0,
     'b_kv_norm_g': 8.0,
     'mlp_norm_g': 9.434,
     'final_norm_g': 7.573}
    for name, (base, spread) in spreads.items():
        noise = np.random.default_rng([zlib.crc32(name.encode()), seed]).standard_normal(out[name].shape)
        drawn = base * np.exp(spread * noise) if base else spread * noise
        out[name] = __import__('jax').numpy.asarray(drawn.astype(out[name].dtype))
    for name, factor in factors.items():
        out[name] = (out[name] * factor).astype(out[name].dtype)
    return out
```

```python
from contextlib import ExitStack

import concourse.bass as bass
from concourse import mybir

F32 = mybir.dt.float32
F32R = mybir.dt.float32r
I32 = mybir.dt.int32
ALU = mybir.AluOpType
ACT = mybir.ActivationFunctionType
AX_X = mybir.AxisListType.X

P = 128
S = 512
D = 2048
KD = D // P
DFF = 4 * D
EPS = 1e-6
QB = S // P
HALF = 64
A_HEADS, A_KV, WINDOW = 16, 4, 128
B_HEADS, Q_LORA, KV_LORA, NOPE, ROPE = 16, 512, 256, 64, 32
KQ, KKV = Q_LORA // P, KV_LORA // P
GROUPS = B_HEADS // 4
A_SCALE = 0.125
B_SCALE = float((NOPE + ROPE) ** -0.5)
BLK = 2048
CH = 8
CHUNKS = DFF // (CH * P)

N_A, T_A = 4, 6
N_LAT, T_LAT = N_A + 40, T_A + 40
N_B, T_B = N_LAT + 7, T_LAT + 7
N_BR, T_BR = N_B + 2 * GROUPS, T_B + 7 * GROUPS
N_OUT, T_OUT = N_BR + 16, T_BR + 32
N_MLP, T_MLP = N_OUT + 16, T_OUT + 16
N_END, T_END = N_MLP + 16 * CHUNKS, T_MLP + 24 * CHUNKS

C_ONES, C_GATTN, C_GMLP, C_GFIN, C_GQ, C_GKV, C_SLOPE, C_SINK, C_INVF, C_SIGN, C_POS = (
    0, 128, 144, 160, 176, 180, 182, 198, 214, 215, 216)
C_IDENT = 220
A_ORDER = (0, 3, 1, 2)
A_BANK = ((0, 0), (1, 0), (2, 0), (0, 256))
C_ALL = C_IDENT + P

TWO_PI_PARTS = (6.283203125, -1.7821788787841797e-05, 3.9693904e-09)


def key_range(qb):
    return max(0, qb - 1) * P, min(QB, qb + 2) * P


def build(nc, xT_d, tab_d, pos_d, mask_d, w_d, out_d):
    gates_d = nc.dram_tensor("gates_scratch", (32, P, S), F32, kind="Internal").ap()

    KB = 1024
    BASE = 16512

    def at(name, kb, shape, dt):
        return nc.alloc_sbuf_tensor_at(name, shape, dt, offset=BASE + int(kb * KB))

    raw = at("raw", 0, [P, 2, BLK], F32)
    wsp = at("wsp", 16, [P, 2, 2, BLK], F32R)
    tab = at("tab", 48, [P, C_ALL], F32)
    rstd = at("rstd", 50, [P, S], F32)
    small = at("small", 52, [P, 64], F32)
    tmp = at("tmp", 52.5, [P, 2, S], F32)
    dist_t = at("dist_t", 154, [P, S], F32)
    otmp = at("otmp", 56.5, [HALF, S], F32)
    xg_h = at("xg_h", 60, [P, KD, S], F32R)
    xg_l = at("xg_l", 92, [P, KD, S], F32R)
    xT = at("xT", 124, [P, KD, S], F32)
    dist = at("dist", 124, [P, QB, 3 * P], F32)
    s_sb = at("s_sb", 130, [P, QB, 3 * P], F32)
    pA = at("pA", 136, [P, QB, 3 * P], F32)
    pTA_h = at("pTA_h", 142, [P, QB, 3 * P], F32R)
    pTA_l = at("pTA_l", 148, [P, QB, 3 * P], F32R)
    qf = at("qf", 154, [P, S], F32)
    kd_h = at("kd_h", 156, [P, A_KV, S], F32R)
    kd_l = at("kd_l", 164, [P, A_KV, S], F32R)
    va = at("va", 172, [P, QB, A_KV, 2, HALF], F32R)
    vc = at("vc", 180, [P, QB, 2, HALF], F32R)
    oA = at("oA", 182, [P, 8, S], F32)
    qs = at("qs", 198, [P, 2, S], F32R)
    pos_a = at("pos_a", 198, [P, S + QB], I32)
    gbuf = at("gbuf", 202, [P, 2, S], F32)
    cqf = at("cqf", 124, [P, KQ, S], F32)
    ckvf = at("ckvf", 132, [P, KKV, S], F32)
    cq_h = at("cq_h", 136, [P, KQ, S], F32R)
    cq_l = at("cq_l", 144, [P, KQ, S], F32R)
    ckv_h = at("ckv_h", 152, [P, KKV, S], F32R)
    ckv_l = at("ckv_l", 156, [P, KKV, S], F32R)
    cosb = at("cosb", 160, [P, S], F32)
    sinb = at("sinb", 162, [P, S], F32)
    oB = at("oB", 164, [P, 8, S], F32)
    sqL = at("sqL", 198, [P, 2, S], F32)
    lat_rstd = at("lat_rstd", 178, [P, S], F32)
    sumsq = at("sumsq", 180, [P, S], F32)
    rope_a = at("rope_a", 198, [P, S], F32)
    rope_b = at("rope_b", 200, [P, S], F32)
    rope_h = at("rope_h", 202, [P, S], F32R)
    rope_l = at("rope_l", 204, [P, S], F32R)
    q_h = at("q_h", 60, [P, 4, S], F32R)
    q_l = at("q_l", 68, [P, 4, S], F32R)
    k_h = at("k_h", 76, [P, 4, S], F32R)
    k_l = at("k_l", 84, [P, 4, S], F32R)
    vb = at("vb", 92, [P, QB, 4, 2, HALF], F32R)
    pB = at("pB", 100, [P, QB, S], F32)
    pTB_h = at("pTB_h", 108, [P, QB, S], F32R)
    pTB_l = at("pTB_l", 116, [P, QB, S], F32R)
    oA_h = at("oA_h", 60, [P, 8, S], F32R)
    oA_l = at("oA_l", 76, [P, 8, S], F32R)
    oB_h = at("oB_h", 92, [P, 8, S], F32R)
    oB_l = at("oB_l", 108, [P, 8, S], F32R)
    mg_h = at("mg_h", 124, [P, KD, S], F32R)
    mg_l = at("mg_l", 156, [P, KD, S], F32R)
    sg = at("sg", 188, [P, 2, 2, S], F32)
    gl = at("gl", 198, [P, 2, 2, S], F32)
    mt = at("mt", 196, [P, S], F32)
    x2 = at("x2", 60, [P, KD, S], F32)
    h2_h = at("h2_h", 92, [P, KD, S], F32R)
    h2_l = at("h2_l", 124, [P, KD, S], F32R)
    u_h = at("u_h", 156, [P, CH, S], F32R)
    u_l = at("u_l", 172, [P, CH, S], F32R)
    xin = at("xin", 188, [P, 2, S], F32)
    ssum = at("ssum", 192, [P, S], F32)
    sq = at("sq", 194, [P, 2, S], F32)
    ru = at("ru", 198, [P, S], F32)
    uu = at("uu", 200, [P, S], F32)
    outT = at("outT", 92, [P, KD, S], F32)
    pos_i = at("pos_i", 172, [P, S], I32)
    posf = at("posf", 174, [P, S], F32)
    ang = at("ang", 164, [P, S], F32)
    turns = at("turns", 166, [P, S], F32)
    t_hi = at("t_hi", 168, [P, S], F32)
    t_lo = at("t_lo", 170, [P, S], F32)

    with ExitStack() as ctx:
        bank = ctx.enter_context(nc.psum_tensor("bank", [P, 8, S], F32))

        def sem(name):
            return ctx.enter_context(nc.semaphore(name))

        raw_full = [sem("raw_full0"), sem("raw_full1")]
        hi_done, lo_done = sem("hi_done"), sem("lo_done")
        tile_full, tile_read = sem("tile_full"), sem("tile_read")
        tab_in = sem("tab_in")
        x_in = [sem(f"x_in{c}") for c in range(4)]
        mask_in, pos_in = sem("mask_in"), sem("pos_in")
        xh_done, xl_done = sem("xh_done"), sem("xl_done")
        sq_done, sq_added = sem("sq_done"), sem("sq_added")
        stat_full, stat_read, col_full = sem("stat_full"), sem("stat_read"), sem("col_full")
        sqrt_done, sin_done = sem("sqrt_done"), sem("sin_done")
        rstd_done = sem("rstd_done")
        chain, col_ready, ang_ready = sem("chain"), sem("col_ready"), sem("ang_ready")
        kv_hi, kv_ready = sem("kv_hi"), sem("kv_ready")
        v_half, v_hi, vc_ready = sem("v_half"), sem("v_hi"), sem("vc_ready")
        pad_set = sem("pad_set")
        q_hi, q_ready = sem("q_hi"), sem("q_ready")
        s_full, s_read = sem("s_full"), sem("s_read")
        neg_ready, dist_ready = sem("neg_ready"), sem("dist_ready")
        a_max, a_shift, a_exp, a_den, p_ready = (
            sem("a_max"), sem("a_shift"), sem("a_exp"), sem("a_den"), sem("p_ready"))
        t_full, pt_hi, pt_lo = sem("t_full"), sem("pt_hi"), sem("pt_lo")
        pv_full, pv_half, o_done = sem("pv_full"), sem("pv_half"), sem("o_done")
        gate_out = [sem("gate_out0"), sem("gate_out1")]
        lat_norm, lat_hi, lat_lo = sem("lat_norm"), sem("lat_hi"), sem("lat_lo")
        kr_ready, kr_split, kr_spread = sem("kr_ready"), sem("kr_split"), sem("kr_spread")
        zero_set = sem("zero_set")
        r_part = sem("r_part")
        b_hi, b_lo, r_sum, r_hi, r_lo, r_moved = (
            sem("b_hi"), sem("b_lo"), sem("r_sum"), sem("r_hi"), sem("r_lo"), sem("r_moved"))
        o_hi, o_lo = sem("o_hi"), sem("o_lo")
        gate_in = [sem("gate_inA"), sem("gate_inB")]
        gate_sig, merged, mg_hi, mg_lo = sem("gate_sig"), sem("merged"), sem("mg_hi"), sem("mg_lo")
        xin_in = sem("xin_in")
        h2_hi, h2_lo = sem("h2_hi"), sem("h2_lo")
        u_sq, u_hi, u_lo = sem("u_sq"), sem("u_hi"), sem("u_lo")
        fin_gain, fin_ready, stored = sem("fin_gain"), sem("fin_ready"), sem("stored")

        block = ctx.enter_context(nc.Block())
        ones = tab[:, C_ONES:C_ONES + P]
        ident = tab[:, C_IDENT:C_IDENT + P]

        @block.sync
        def _(sp):
            sp.dma_start(tab[:], tab_d).then_inc(tab_in, 16)
            sp.dma_start(xT[:, 0:4, :], xT_d[:, 0:4, :]).then_inc(x_in[0], 16)
            sp.dma_start(raw[:, 0, :], w_d[0]).then_inc(raw_full[0], 16)
            for c in range(1, 4):
                sp.dma_start(xT[:, 4 * c:4 * c + 4, :], xT_d[:, 4 * c:4 * c + 4, :]).then_inc(x_in[c], 16)
                if c == 1:
                    sp.dma_start(raw[:, 1, :], w_d[1]).then_inc(raw_full[1], 16)
            with sp.Fori(1, N_END // 2) as h:
                for slot in range(2):
                    sp.wait_ge(hi_done, h * 2 + slot - 1)
                    sp.wait_ge(lo_done, h * 2 + slot - 1)
                    sp.dma_start(raw[:, slot, :], w_d[bass.ds(h * 2 + slot, 1)].rearrange("a p k -> p (a k)")).then_inc(
                        raw_full[slot], 16)
            n = N_END - 1
            sp.wait_ge(hi_done, n - 1)
            sp.wait_ge(lo_done, n - 1)
            sp.dma_start(raw[:, n % 2, :], w_d[n]).then_inc(raw_full[n % 2], 16)
            for i in range(KD // 2):
                sp.wait_ge(fin_ready, 2 * i + 2)
                sp.dma_start(out_d[:, 2 * i:2 * i + 2, :], outT[:, 2 * i:2 * i + 2, :]).then_inc(stored, 16)
            sp.wait_ge(stored, 16 * (KD // 2))

        @block.gpsimd
        def _(pool):
            pool.dma_start(pos_a[:], pos_d).then_inc(pos_in, 16)
            pool.wait_ge(sq_done, KD)
            pool.wait_ge(xl_done, KD)
            pool.dma_start(dist[:], mask_d).then_inc(mask_in, 16)
            nc.gpsimd.memset(s_sb[:, 0, 2 * P:3 * P], -3e38).then_inc(pad_set, 1)
            nc.gpsimd.memset(s_sb[:, 3, 2 * P:3 * P], -3e38).then_inc(pad_set, 1)
            pool.wait_ge(tile_read, T_A)
            with pool.Fori(0, 4) as J:
                pool.wait_ge(pv_full, 1 + J * 4)
                nc.gpsimd.tensor_copy(vc[:].rearrange("p a b c -> p a (b c)"),
                                      va[:, :, bass.ds(J, 1), :, :].rearrange("p a g b c -> p a (g b c)")).then_inc(vc_ready, 1)
                for jj in range(2):
                    for i in range(4):
                        pool.wait_ge(tile_read, J * 10 + (T_A + 5 * jj + 1 + i + 1))
                        pool.dma_start(gates_d[bass.ds(J * 8 + 4 * jj + i, 1)].rearrange("a p k -> p (a k)"),
                                       gbuf[:, i % 2, :]).then_inc(gate_out[i % 2], 16)
            pool.wait_ge(gate_out[0], 16 * 16)
            pool.wait_ge(gate_out[1], 16 * 16)
            pool.wait_ge(pv_full, 1 + A_HEADS)
            pool.dma_start(pos_i[:], pos_d[:, 0:S]).then_inc(pos_in, 16)
            pool.wait_ge(tile_full, T_B)
            for t in (q_h, q_l, k_h, k_l):
                for e in (1, 3):
                    nc.gpsimd.memset(t[0:32, e, :].bitcast(F32), 0.0).then_inc(zero_set, 1)

            def rope_moves(g):
                if not (isinstance(g, int) and g == 0):
                    pool.wait_ge(s_full, 1 + g * 16 + 64)
                pool.wait_ge(r_lo, g + 1)
                pool.wait_ge(r_hi, g + 1)
                for e in range(4):
                    to = HALF if e % 2 == 0 else 32
                    for src, dst in ((rope_h, q_h), (rope_l, q_l)):
                        pool.dma_start(dst[to:to + 32, e, :], src[32 * e:32 * e + 32, :]).then_inc(r_moved, 16)
            for g in range(GROUPS):
                rope_moves(g)

            def gate_loads(p):
                for b in range(2):
                    if not (isinstance(p, int) and p == 0):
                        pool.wait_ge(gate_sig, p * 2 + b - 1)
                    pool.dma_start(gl[:, b], gates_d[bass.ds(p * 2 + 16 * b, 2)].rearrange("m p s -> p m s")).then_inc(
                        gate_in[b], 16)
            pool.wait_ge(r_moved, 16 * 8 * GROUPS)
            gate_loads(0)
            with pool.Fori(1, 8) as p:
                gate_loads(p)
            pool.wait_ge(merged, 16)
            pool.wait_ge(mg_lo, 1 + 16)
            with pool.Fori(0, 8) as p:
                pool.wait_ge(tile_read, p * 2 + T_OUT)
                pool.dma_start(xin[:], xT_d[:, bass.ds(p * 2, 2), :]).then_inc(xin_in, 16)

        @block.tensor
        def _(pe):
            for s in (pv_full, s_full, t_full):
                pe.sem_inc(s, 1)

            def split_ready(n):
                pe.wait_ge(hi_done, n + 1)
                pe.wait_ge(lo_done, n + 1)

            def mm3(out, w, sl, xh, xl, start, stop):
                wh, wl = wsp[:, sl, 0, w], wsp[:, sl, 1, w]
                nc.tensor.matmul(out, wh, xh, start=start, stop=False)
                nc.tensor.matmul(out, wh, xl, start=False, stop=False)
                return nc.tensor.matmul(out, wl, xh, start=False, stop=stop)

            def tile(b, sl, k0=0, k1=KD, xh=xg_h, xl=xg_l, kn=KD, off=0, width=P):
                for k in range(k0, k1):
                    c = off + width * k
                    last = mm3(bank[:, b, :], slice(c, c + P), sl, xh[:, k, :], xl[:, k, :], k == 0, k == kn - 1)
                return last

            pe.wait_ge(tab_in, 16)
            split_ready(0)
            for k in range(KD):
                pe.wait_ge(xh_done, k + 1)
                pe.wait_ge(xl_done, k + 1)
                last = mm3(bank[:, 0, :], slice(P * k, P * k + P), 0, xg_h[:, k, :], xg_l[:, k, :], k == 0, k == KD - 1)
            last.then_inc(tile_full, 1)
            split_ready(1)
            tile(1, 1).then_inc(tile_full, 1)
            for b in range(2):
                split_ready(2 + b)
                for tt in range(QB):
                    out = bank[:, 2 + tt, 0:256]
                    tok = slice(P * tt, P * tt + P)
                    for k in range(8):
                        wh, wl = (wsp[:, b, i, 256 * k:256 * k + 256] for i in range(2))
                        xh, xl = xg_h[:, 8 * b + k, tok], xg_l[:, 8 * b + k, tok]
                        nc.tensor.matmul(out, xh, wh, start=(b == 0 and k == 0), stop=False)
                        nc.tensor.matmul(out, xh, wl, start=False, stop=False)
                        last = nc.tensor.matmul(out, xl, wh, start=False, stop=(b == 1 and k == 7))
                    if b == 1:
                        last.then_inc(tile_full, 1)
                if b == 0:
                    last.then_inc(v_half, 1)
                    pe.wait_ge(sq_added, KD)
                    nc.tensor.matmul(bank[:, 7, :], ones, tmp[:, 0, :], start=True, stop=True).then_inc(stat_full, 1)
            pe.wait_ge(rstd_done, 1)
            for tt in range(QB):
                last = nc.tensor.matmul(bank[:, 7, tt:tt + 1], rstd[0:1, P * tt:P * tt + P], tab[0:1, C_ONES:C_ONES + 1],
                                        start=True, stop=True)
            last.then_inc(col_full, 1)

            def a_scores(J, jj, e):
                h = 2 * jj + e
                for qb in A_ORDER:
                    k0, k1 = key_range(qb)
                    b, c = A_BANK[qb]
                    out = bank[:, b, c:c + k1 - k0]
                    lhs = qs[:, e, P * qb:P * qb + P]
                    if qb == 0:
                        pe.wait_ge(q_ready, J * 4 + 2 * jj + 2)
                        pe.wait_ge(s_read, 1 + J * 16 + 4 * h)
                    nc.tensor.matmul(out, lhs, kd_h[:, bass.ds(J, 1), k0:k1].rearrange("p a k -> p (a k)"), start=True, stop=False)
                    nc.tensor.matmul(out, lhs, kd_l[:, bass.ds(J, 1), k0:k1].rearrange("p a k -> p (a k)"),
                                     start=False, stop=True).then_inc(s_full, 1)

            def a_turn(J, h, kbs):
                for kb in kbs:
                    if kb == 0:
                        pe.wait_ge(p_ready, J * 16 + 4 * h + 4)
                    pe.wait_ge(pt_lo, 1 + J * 16 + max(4 * h + kb - 1, 0))
                    q0, q1 = max(0, kb - 1), min(QB, kb + 2)
                    for qb in range(q0, q1):
                        c = P * kb - key_range(qb)[0]
                        last = nc.tensor.transpose(bank[:, 4 + kb % 2, P * (qb - q0):P * (qb - q0) + P],
                                                   pA[:, qb, c:c + P], ident)
                    last.then_inc(t_full, 1)

            def a_values(J, h, kbs):
                for kb in kbs:
                    if kb == 0:
                        pe.wait_ge(vc_ready, J + 1)
                        pe.wait_ge(o_done, 1 + J * 4 + h)
                    pe.wait_ge(pt_lo, 1 + J * 16 + 4 * h + kb + 1)
                    q0, q1 = key_range(kb)
                    n = q1 - q0
                    nc.tensor.matmul(bank[:, 6, q0:q1], vc[:, kb].rearrange("p a d -> p (a d)"), pTA_h[:, kb, 0:n],
                                     start=(kb == 0), stop=False, skip_group_check=True)
                    last = nc.tensor.matmul(bank[0:HALF, 6, q0:q1], vc[:, kb, 0, :], pTA_l[:, kb, 0:n],
                                            start=False, stop=(kb == QB - 1), skip_group_check=True)
                if kbs[-1] == QB - 1:
                    last.then_inc(pv_full, 1)

            pe.wait_ge(kv_hi, 3 * A_KV)
            with pe.Fori(0, 4) as J:
                for jj in range(2):
                    h0, h1 = 2 * jj, 2 * jj + 1

                    def piece(i, k0, k1):
                        b, sl = (3, 7)[(5 * jj + i) % 2], (5 * jj + i) % 2
                        if k0 == 0:
                            split_ready(J * 10 + (N_A + 5 * jj + i))
                            pe.wait_ge(tile_read, J * 10 + (T_A + 5 * jj + i - 1))
                        last = tile(b, sl, k0, k1)
                        if k1 == KD:
                            last.then_inc(tile_full, 1)
                    piece(0, 0, KD)
                    piece(1, 0, KD)
                    a_scores(J, jj, 0)
                    piece(2, 0, KD)
                    a_turn(J, h0, (0, 1))
                    piece(3, 0, 8)
                    a_values(J, h0, (0, 1))
                    a_turn(J, h0, (2, 3))
                    a_scores(J, jj, 1)
                    piece(3, 8, KD)
                    a_values(J, h0, (2, 3))
                    piece(4, 0, 8)
                    a_turn(J, h1, (0, 1))
                    piece(4, 8, 11)
                    a_values(J, h1, (0, 1))
                    a_turn(J, h1, (2, 3))
                    piece(4, 11, 14)
                    a_values(J, h1, (2, 3))
                    piece(4, 14, KD)

            pe.wait_ge(s_read, 1 + 4 * A_HEADS)
            pe.wait_ge(pt_lo, 1 + 4 * A_HEADS)
            pe.wait_ge(tile_read, T_A + 39)
            for m in range(KQ + KKV):
                split_ready(N_LAT + m)
                if m == 3:
                    pe.wait_ge(tile_read, T_LAT)
                tile(m, (N_LAT + m) % 2).then_inc(tile_full, 1)
                if m == KQ:
                    pe.wait_ge(sq_added, KD + KQ)
                    nc.tensor.matmul(bank[:, 7, :], ones, sumsq[:], start=True, stop=True).then_inc(stat_full, 1)
            split_ready(N_LAT + 6)
            pe.wait_ge(o_done, 1 + A_HEADS)
            for k in range(KD):
                last = mm3(bank[0:ROPE, 6, :], slice(ROPE * k, ROPE * k + ROPE), 0, xg_h[:, k, :], xg_l[:, k, :],
                           k == 0, k == KD - 1)
            last.then_inc(tile_full, 1)
            pe.wait_ge(sq_added, KD + KQ + KKV)
            pe.wait_ge(stat_read, 2)
            nc.tensor.matmul(bank[:, 7, :], ones, sumsq[:], start=True, stop=True).then_inc(stat_full, 1)

            def b_queries(g, part):
                t, sl = 7 * g + (T_B + part), N_B % 2
                if part == 0:
                    split_ready(2 * g + N_B)
                    pe.wait_ge(lat_lo, KQ)
                if part == 1:
                    pe.wait_ge(o_done, 1 + 4 * g + (A_HEADS - 1)) if not (isinstance(g, int) and g == 0) else None
                if part == 2:
                    pe.wait_ge(tile_read, 7 * g + (T_B + 1))
                tile((7, 6, 7)[part], sl, 0, KQ, cq_h, cq_l, KQ, P * part, 3 * P).then_inc(tile_full, 1)

            def b_keys(g):
                sl = (N_B + 1) % 2
                split_ready(2 * g + N_B + 1)
                pe.wait_ge(lat_lo, KQ + KKV)
                for i in range(2):
                    tile(i, sl, 0, KKV, ckv_h, ckv_l, KKV, P * i, 2 * P).then_inc(tile_full, 1)

            def b_values_in(g):
                sl = (N_B + 1) % 2
                for i in range(2):
                    for j in range(2):
                        tok = slice(P * (2 * i + j), P * (2 * i + j) + P)
                        out = bank[:, 2 + i, 256 * j:256 * j + 256]
                        for k in range(KKV):
                            wh, wl = (wsp[:, sl, v, 512 + 256 * k:768 + 256 * k] for v in range(2))
                            nc.tensor.matmul(out, ckv_h[:, k, tok], wh, start=(k == 0), stop=False)
                            nc.tensor.matmul(out, ckv_h[:, k, tok], wl, start=False, stop=False)
                            last = nc.tensor.matmul(out, ckv_l[:, k, tok], wh, start=False, stop=(k == KKV - 1))
                    last.then_inc(tile_full, 1)

            def b_scores(g, e):
                rows = slice(0, NOPE + ROPE) if e % 2 == 0 else slice(0, P)
                for qb in range(QB):
                    if e == 0 and qb == 0:
                        pe.wait_ge(b_lo, 4 * g + 4)
                        pe.wait_ge(r_moved, 128 * g + 128)
                        pe.wait_ge(tile_read, 7 * g + (T_B + 5))
                    if e == 0 and qb == 2:
                        pe.wait_ge(tile_read, 7 * g + (T_B + 7))
                    if e > 0:
                        pe.wait_ge(a_exp, 1 + 16 * g + (5 * A_HEADS + 4 * e - 4 + qb + 1))
                    q = slice(P * qb, P * qb + P)
                    nc.tensor.matmul(bank[:, qb, :], q_h[rows, e, q], k_h[rows, e, :], start=True, stop=False)
                    nc.tensor.matmul(bank[:, qb, :], q_h[rows, e, q], k_l[rows, e, :], start=False, stop=False)
                    nc.tensor.matmul(bank[:, qb, :], q_l[rows, e, q], k_h[rows, e, :], start=False, stop=True).then_inc(
                        s_full, 1)

            def b_turn(g, e, kbs):
                for kb in kbs:
                    if kb == 0:
                        pe.wait_ge(p_ready, 16 * g + (4 * A_HEADS + 4 * e + 4))
                    pe.wait_ge(pt_lo, 1 + 16 * g + (4 * A_HEADS + 4 * e + kb - 1))
                    for qb in range(QB):
                        last = nc.tensor.transpose(bank[:, 4 + kb % 2, P * qb:P * qb + P], pB[:, qb, P * kb:P * kb + P], ident)
                    last.then_inc(t_full, 1)

            def b_values(g, e, kbs):
                for kb in kbs:
                    if kb == 0:
                        pe.wait_ge(o_done, 1 + 4 * g + (A_HEADS + e))
                    pe.wait_ge(pt_lo, 1 + 16 * g + (4 * A_HEADS + 4 * e + kb + 1))
                    nc.tensor.matmul(bank[:, 6, :], vb[:, kb, e].rearrange("p a d -> p (a d)"), pTB_h[:, kb, :],
                                     start=(kb == 0), stop=False, skip_group_check=True)
                    last = nc.tensor.matmul(bank[0:HALF, 6, :], vb[:, kb, e, 0, :], pTB_l[:, kb, :],
                                            start=False, stop=(kb == QB - 1), skip_group_check=True)
                if kbs[-1] == QB - 1:
                    last.then_inc(pv_full, 1)

            def b_group(g, more):
                b_scores(g, 0)
                for e in range(3):
                    b_turn(g, e, (0, 1))
                    b_scores(g, e + 1)
                    b_values(g, e, (0, 1))
                    b_turn(g, e, (2, 3))
                    b_values(g, e, (2, 3))
                if more:
                    b_queries(g + 1, 0)
                    b_queries(g + 1, 1)
                    b_turn(g, 3, (0, 1))
                    b_queries(g + 1, 2)
                    pe.wait_ge(tile_read, 7 * g + (T_B + 7 + 2))
                    b_values(g, 3, (0, 1))
                    b_turn(g, 3, (2, 3))
                    pe.wait_ge(a_exp, 1 + 16 * g + (5 * A_HEADS + 16))
                    b_keys(g + 1)
                    b_values(g, 3, (2, 3))
                    b_values_in(g + 1)
                else:
                    b_turn(g, 3, (0, 1))
                    b_values(g, 3, (0, 1))
                    b_turn(g, 3, (2, 3))
                    b_values(g, 3, (2, 3))

            pe.wait_ge(stat_read, 3)
            pe.wait_ge(tile_read, T_B)
            for part in range(3):
                b_queries(0, part)
            b_keys(0)
            b_values_in(0)
            pe.wait_ge(zero_set, 8)
            pe.wait_ge(kr_spread, 8)
            with pe.Fori(0, GROUPS - 1) as g:
                b_group(g, True)
            b_group(GROUPS - 1, False)

            def branch_pair(p, first):
                for b, (oh, ol) in enumerate(((oA_h, oA_l), (oB_h, oB_l))):
                    split_ready(2 * p + N_BR + b)
                    for i in range(2):
                        pe.wait_ge(tile_read, 4 * p + (T_BR + 2 * b + i - 3))
                        for k in range(8):
                            if first and i == 0:
                                pe.wait_ge(o_lo, 8 * b + k + 1)
                            c = 256 * k + P * i
                            last = mm3(bank[:, 2 * b + i, :], slice(c, c + P), (N_BR + b) % 2, oh[:, k, :], ol[:, k, :],
                                       k == 0, k == 7)
                        last.then_inc(tile_full, 1)

            pe.wait_ge(tile_read, T_BR)
            pe.wait_ge(a_exp, 1 + 5 * A_HEADS + 4 * B_HEADS)
            branch_pair(0, True)
            with pe.Fori(1, 8) as p:
                branch_pair(p, False)

            def out_pair(p, first):
                for i in range(2):
                    split_ready(2 * p + N_OUT + i)
                    pe.wait_ge(tile_read, 2 * p + (T_OUT + i - 1))
                    for k in range(KD):
                        if first and i == 0:
                            pe.wait_ge(mg_lo, 1 + k + 1)
                        last = mm3(bank[:, 4 + i, :], slice(P * k, P * k + P), (N_OUT + i) % 2, mg_h[:, k, :], mg_l[:, k, :],
                                   k == 0, k == KD - 1)
                    last.then_inc(tile_full, 1)

            out_pair(0, True)
            with pe.Fori(1, 8) as p:
                out_pair(p, False)

            def up_pair(c, q, first):
                for i in range(2):
                    split_ready(16 * c + 2 * q + (N_MLP + i))
                    pe.wait_ge(tile_read, 24 * c + 2 * q + (T_MLP + i - 1))
                    for k in range(KD):
                        if first and i == 0:
                            pe.wait_ge(h2_lo, k + 1)
                        last = mm3(bank[:, i, :], slice(P * k, P * k + P), (N_MLP + i) % 2, h2_h[:, k, :], h2_l[:, k, :],
                                   k == 0, k == KD - 1)
                    last.then_inc(tile_full, 1)
                    if first and i == 0:
                        nc.tensor.matmul(bank[:, 7, :], ones, ssum[:], start=True, stop=True).then_inc(stat_full, 1)

            def down_pair(c, q):
                for i in range(4):
                    b, j = i // 2, i % 2
                    if j == 0:
                        split_ready(16 * c + 2 * q + (N_MLP + CH + b))
                    pe.wait_ge(tile_read, 24 * c + 4 * q + (T_MLP + CH + i - 3))
                    for k in range(CH):
                        if i == 0 and k in (0, CH - 1):
                            pe.wait_ge(u_lo, CH * c + (CH - 1 if k == 0 else CH))
                        col = 256 * k + P * j
                        last = mm3(bank[:, 2 + i, :], slice(col, col + P), (N_MLP + b) % 2, u_h[:, k, :], u_l[:, k, :],
                                   k == 0, k == CH - 1)
                    last.then_inc(tile_full, 1)

            up_pair(0, 0, True)
            with pe.Fori(1, 4) as q:
                up_pair(0, q, False)
            with pe.Fori(0, 4) as q:
                down_pair(0, q)
            with pe.Fori(1, CHUNKS) as c:
                with pe.Fori(0, 4) as q:
                    up_pair(c, q, False)
                with pe.Fori(0, 4) as q:
                    down_pair(c, q)
            pe.wait_ge(sq_added, KD + KQ + KKV + 2 * KD)
            nc.tensor.matmul(bank[:, 7, :], ones, ssum[:], start=True, stop=True).then_inc(stat_full, 1)

        @block.scalar
        def _(act):
            def hi(n, sl, hlf, done, width=BLK):
                act.wait_ge(raw_full[sl], hlf)
                if done is not None:
                    act.wait_ge(tile_full, done)
                nc.scalar.copy(wsp[:, sl, 0, 0:width], raw[:, sl, 0:width]).then_inc(hi_done, 1)

            def hi_at(base_n, per, i, done, width=BLK):
                n = base_n + i
                hi(None, n % 2, per * 8 + 16 * (n // 2 + 1), done, width)

            act.sem_inc(a_exp, 1)
            act.wait_ge(tab_in, 16)
            hi(0, 0, 16, None)
            for k in range(KD):
                act.wait_ge(x_in[k // 4], 16)
                nc.scalar.activation(xg_h[:, k, :], xT[:, k, :], ACT.Copy,
                                     scale=tab[:, C_GATTN + k:C_GATTN + k + 1]).then_inc(xh_done, 1)
                if k == 7:
                    hi(1, 1, 16, None)
            for k in range(KD):
                if k >= 2:
                    act.wait_ge(sq_added, k - 1)
                nc.scalar.square(gbuf[:, k % 2, :], xT[:, k, :]).then_inc(sq_done, 1)
                if k == 7:
                    hi(2, 0, 32, 1)
            hi(3, 1, 32, 2)

            def sqrt_of(i):
                act.wait_ge(stat_read, i)
                nc.scalar.sqrt(tmp[:, 1, :], tmp[:, 0, :]).then_inc(sqrt_done, 1)
            sqrt_of(1)
            for g in range(A_KV):
                r = slice(HALF * (g % 2), HALF * (g % 2) + HALF)
                o = slice(HALF * (1 - g % 2), HALF * (1 - g % 2) + HALF)
                act.wait_ge(tile_read, g // 2 + 1)
                nc.scalar.copy(kd_h[r, g, :], gbuf[r, g // 2, :]).then_inc(kv_hi, 1)
            for g in range(A_KV):
                r = slice(HALF * (g % 2), HALF * (g % 2) + HALF)
                o = slice(HALF * (1 - g % 2), HALF * (1 - g % 2) + HALF)
                act.wait_ge(kv_ready, g + 1)
                act.wait_ge(kv_hi, g + 1)
                nc.scalar.copy(kd_h[o, g, :], kd_h[r, g, :].bitcast(F32)).then_inc(kv_hi, 1)
                nc.scalar.copy(kd_l[o, g, :], kd_l[r, g, :].bitcast(F32)).then_inc(kv_hi, 1)
            act.wait_ge(v_half, 1)
            hi(4, 0, 48, None)
            act.wait_ge(col_ready, 1)
            for tt in range(QB):
                act.wait_ge(tile_full, 3 + tt)
                nc.scalar.activation(va[:, tt, :, 0, :], bank[:, 2 + tt, 0:256].rearrange("p (g d) -> p g d", g=A_KV), ACT.Copy,
                                     scale=small[:, tt:tt + 1]).then_inc(v_hi, 1)
            hi(5, 1, 48, T_A)

            def softmax_a(J, h):
                act.wait_ge(a_shift, J * 4 + h + 1)
                act.wait_ge(t_full, 1 + J * 16 + 4 * h)
                for qb in range(QB):
                    k0, k1 = key_range(qb)
                    nc.scalar.activation(pA[:, qb, 0:k1 - k0], s_sb[:, qb, 0:k1 - k0], ACT.Exp, scale=A_SCALE,
                                         bias=small[:, 8 + qb:9 + qb], accum_out=small[:, 12 + qb:13 + qb]).then_inc(a_exp, 1)
                nc.scalar.activation(small[:, 16:20], small[:, 8:12], ACT.Exp,
                                     bias=tab[:, bass.ds(J * 4 + (C_SINK + h), 1)]).then_inc(a_exp, 1)

            def turned_hi(base, h, kbs, src_n, dst):
                for kb in kbs:
                    act.wait_ge(t_full, 1 + base + (4 * h + kb + 1))
                    n = src_n(kb)
                    nc.scalar.copy(dst[:, kb, 0:n], bank[:, 4 + kb % 2, 0:n]).then_inc(pt_hi, 1)

            def a_n(kb):
                return key_range(kb)[1] - key_range(kb)[0]

            def turned_a(J, h, kbs):
                if kbs[0] == 0:
                    act.wait_ge(pv_full, 1 + J * 4 + h)
                turned_hi(J * 16, h, kbs, a_n, pTA_h)

            def half_out(count):
                act.wait_ge(pv_full, 1 + count + 1)
                act.wait_ge(o_done, 1 + count)
                nc.scalar.copy(otmp[:], bank[HALF:P, 6, :]).then_inc(pv_half, 1)

            with act.Fori(0, 4) as J:
                for jj in range(2):
                    def next_hi(i):
                        hi_at(N_A, J * 10, 5 * jj + i + 2, J * 10 + (T_A + 5 * jj + i + 1))
                    h0, h1 = 2 * jj, 2 * jj + 1
                    act.wait_ge(tile_read, J * 10 + (T_A + 5 * jj + 1))
                    act.wait_ge(s_full, 1 + J * 16 + 8 * jj)
                    nc.scalar.copy(qs[0:HALF, 0, :], qf[0:HALF, :]).then_inc(q_hi, 1)
                    nc.scalar.copy(qs[HALF:P, 1, :], qf[HALF:P, :]).then_inc(q_hi, 1)
                    next_hi(0)
                    next_hi(1)
                    softmax_a(J, h0)
                    next_hi(2)
                    turned_a(J, h0, (0, 1))
                    turned_a(J, h0, (2, 3))
                    softmax_a(J, h1)
                    next_hi(3)
                    half_out(J * 4 + h0)
                    turned_a(J, h1, (0, 1))
                    turned_a(J, h1, (2, 3))
                    half_out(J * 4 + h1)
                    next_hi(4)

            for m in range(KQ + KKV):
                act.wait_ge(tile_read, T_LAT + m + 1)
                if m >= 2:
                    act.wait_ge(sq_added, KD + m - 1)
                src = cqf[:, m, :] if m < KQ else ckvf[:, m - KQ, :]
                nc.scalar.square(sqL[:, m % 2, :], src).then_inc(sq_done, 1)
                hi_at(N_LAT, 0, m + 2, T_LAT + m + 1)
                if m == KQ:
                    sqrt_of(2)
                    for k in range(KQ):
                        act.wait_ge(lat_norm, k + 1)
                        nc.scalar.activation(cq_h[:, k, :], cqf[:, k, :], ACT.Copy,
                                             scale=tab[:, C_GQ + k:C_GQ + k + 1]).then_inc(lat_hi, 1)
            act.wait_ge(ang_ready, 1)
            nc.scalar.activation(t_hi[:], ang[:], ACT.Sin, scale=0.5).then_inc(sin_done, 1)
            nc.scalar.activation(t_lo[:], turns[:], ACT.Sin).then_inc(sin_done, 1)
            hi_at(N_LAT, 0, 8, T_LAT + 7)
            act.wait_ge(kr_ready, 1)
            act.wait_ge(gate_out[0], 16 * 16)
            act.wait_ge(gate_out[1], 16 * 16)
            nc.scalar.copy(rope_h[0:ROPE, :], rope_a[0:ROPE, :]).then_inc(kr_split, 1)
            act.wait_ge(kr_split, 2)
            for e in range(4):
                to = HALF if e % 2 == 0 else 32
                nc.scalar.copy(k_h[to:to + ROPE, e, :], rope_h[0:ROPE, :].bitcast(F32)).then_inc(kr_spread, 1)
                nc.scalar.copy(k_l[to:to + ROPE, e, :], rope_l[0:ROPE, :].bitcast(F32)).then_inc(kr_spread, 1)
            sqrt_of(3)
            for k in range(KKV):
                act.wait_ge(lat_norm, KQ + k + 1)
                nc.scalar.activation(ckv_h[:, k, :], ckvf[:, k, :], ACT.Copy,
                                     scale=tab[:, C_GKV + k:C_GKV + k + 1]).then_inc(lat_hi, 1)

            def pair_hi(g, which, i):
                t = 7 * g + (T_B + (i if which == 0 else 3 + i))
                b = (7, 6)[i] if which == 0 else i
                dst = (q_h, k_h)[which]
                act.wait_ge(tile_full, t + 1)
                for e in range(2):
                    r = slice(HALF * e, HALF * e + HALF)
                    nc.scalar.copy(dst[r, 2 * i + e, :], bank[r, b, :]).then_inc(b_hi, 1)

            def rope_hi(g):
                act.wait_ge(r_sum, g + 1)
                nc.scalar.copy(rope_h[:], rope_a[:]).then_inc(r_hi, 1)

            def values_hi(g):
                for i in range(2):
                    act.wait_ge(tile_full, 7 * g + (T_B + 6 + i))
                    nc.scalar.copy(vb[:, 2 * i:2 * i + 2, :, 0, :].rearrange("p t e d -> p (t e) d"),
                                   bank[:, 2 + i, :].rearrange("p (a d) -> p a d", d=HALF)).then_inc(v_hi, 1)

            def softmax_b(g, e):
                act.wait_ge(a_shift, 4 * g + (A_HEADS + e + 1))
                act.wait_ge(t_full, 1 + 16 * g + (4 * A_HEADS + 4 * e))
                for qb in range(QB):
                    nc.scalar.activation(pB[:, qb, :], bank[:, qb, :], ACT.Exp, scale=B_SCALE,
                                         bias=small[:, 8 + qb:9 + qb], accum_out=small[:, 12 + qb:13 + qb]).then_inc(a_exp, 1)

            def turned_b(g, e, kbs):
                if kbs[0] == 0:
                    act.wait_ge(pv_full, 1 + 4 * g + (A_HEADS + e))
                turned_hi(16 * g + 4 * A_HEADS, e, kbs, lambda kb: S, pTB_h)

            def b_group(g, more):
                softmax_b(g, 0)
                for e in range(3):
                    turned_b(g, e, (0, 1))
                    turned_b(g, e, (2, 3))
                    softmax_b(g, e + 1)
                    half_out(4 * g + (A_HEADS + e))
                    if e < 2:
                        w = ((1536, 1024)[e] if more else BLK)
                        hi_at(N_B, 2 * g, 2 + e, 7 * g + (T_B + (3, 7)[e]), w)
                if more:
                    act.wait_ge(s_full, 1 + 16 * g + (4 * A_HEADS + 16))
                    pair_hi(g + 1, 0, 0)
                    pair_hi(g + 1, 0, 1)
                    turned_b(g, 3, (0, 1))
                    rope_hi_wait(g + 1)
                    turned_b(g, 3, (2, 3))
                    pair_hi(g + 1, 1, 0)
                    pair_hi(g + 1, 1, 1)
                    half_out(4 * g + (A_HEADS + 3))
                    act.wait_ge(pv_full, 1 + 4 * g + (A_HEADS + 4))
                    values_hi(g + 1)
                else:
                    turned_b(g, 3, (0, 1))
                    turned_b(g, 3, (2, 3))
                    half_out(4 * g + (A_HEADS + 3))

            def rope_hi_wait(g):
                act.wait_ge(r_moved, 128 * g)
                rope_hi(g)

            act.wait_ge(zero_set, 8)
            for i in range(2):
                pair_hi(0, 0, i)
            rope_hi(0)
            for i in range(2):
                pair_hi(0, 1, i)
            values_hi(0)
            with act.Fori(0, GROUPS - 1) as g:
                b_group(g, True)
            b_group(GROUPS - 1, False)

            for k in range(8):
                act.wait_ge(o_done, 1 + A_HEADS) if k == 0 else None
                nc.scalar.copy(oA_h[:, k, :], oA[:, k, :]).then_inc(o_hi, 1)
            for k in range(8):
                act.wait_ge(o_done, 1 + A_HEADS + 2 * k + 2)
                nc.scalar.copy(oB_h[:, k, :], oB[:, k, :]).then_inc(o_hi, 1)

            def sig(p, b):
                act.wait_ge(gate_in[b], 16 * p + 16)
                act.wait_ge(tile_read, 4 * p + (T_BR - 2 + 2 * b))
                nc.scalar.activation(sg[:, b], gl[:, b], ACT.Sigmoid).then_inc(gate_sig, 1)

            act.wait_ge(o_lo, 8)
            with act.Fori(0, 8) as p:
                sig(p, 0)
                sig(p, 1)
                hi_at(N_BR, 2 * p, 2, 4 * p + (T_BR + 2))
                for i in range(2):
                    act.wait_ge(merged, 2 * p + (i + 1))
                    nc.scalar.copy(mg_h[:, bass.ds(2 * p + i, 1), :], tmp[:, i:i + 1, :]).then_inc(mg_hi, 1)
                hi_at(N_BR, 2 * p, 3, 4 * p + (T_BR + 4))

            with act.Fori(0, 8) as p:
                for i in range(2):
                    act.wait_ge(tile_read, 2 * p + (T_OUT + i + 1))
                    act.wait_ge(sq_added, 2 * p + (KD + KQ + KKV + i - 1))
                    nc.scalar.activation(h2_h[:, bass.ds(2 * p + i, 1), :].rearrange("p a s -> p (a s)"),
                                         x2[:, bass.ds(2 * p + i, 1), :].rearrange("p a s -> p (a s)"), ACT.Copy,
                                         scale=tab[:, bass.ds(2 * p + (C_GMLP + i), 1)]).then_inc(h2_hi, 1)
                    nc.scalar.square(sq[:, i, :].rearrange("p (a s) -> p a s", a=1), x2[:, bass.ds(2 * p + i, 1), :]).then_inc(sq_done, 1)
                    hi_at(N_OUT, 2 * p, 2 + i, 2 * p + (T_OUT + i + 1))

            def up(c, q):
                for i in range(2):
                    act.wait_ge(u_sq, CH * c + 2 * q + (i + 1))
                    nc.scalar.copy(u_h[:, bass.ds(2 * q + i, 1), :], uu[:].rearrange("p (a s) -> p a s", a=1)).then_inc(u_hi, 1)
                    hi_at(N_MLP, 16 * c + 2 * q, 2 + i, 24 * c + 2 * q + (T_MLP + i + 1))

            def down(c, q, last=False):
                for b in range(2):
                    if last:
                        for j in range(2):
                            m = 4 * q + 2 * b + j
                            act.wait_ge(tile_read, T_END - KD + m + 1)
                            act.wait_ge(sq_added, KD + KQ + KKV + KD + m - 1)
                            nc.scalar.square(sq[:, j, :], x2[:, m, :]).then_inc(sq_done, 1)
                            nc.scalar.activation(outT[:, m, :], x2[:, m, :], ACT.Copy,
                                                 scale=tab[:, C_GFIN + m:C_GFIN + m + 1]).then_inc(fin_gain, 1)
                    if not (last and q == 3):
                        hi_at(N_MLP + CH, 16 * c + 2 * q, 2 + b, 24 * c + 4 * q + (T_MLP + CH + 2 * b + 2))

            sqrt_of(4)
            with act.Fori(0, CHUNKS - 1) as c:
                with act.Fori(0, 4) as q:
                    up(c, q)
                with act.Fori(0, 4) as q:
                    down(c, q)
            with act.Fori(0, 4) as q:
                up(CHUNKS - 1, q)
            for q in range(4):
                down(CHUNKS - 1, q, True)
            sqrt_of(5)

        @block.vector
        def _(dve):
            V = nc.vector
            links = [0]

            def link(ins):
                links[0] += 1
                ins.then_inc(chain, 1)
                dve.wait_ge(chain, links[0])

            def lo_at(base_n, per, i, width=BLK):
                n = base_n + i
                dve.wait_ge(hi_done, per + (n + 1))
                V.tensor_tensor(wsp[:, n % 2, 1, 0:width], raw[:, n % 2, 0:width], wsp[:, n % 2, 0, 0:width].bitcast(F32),
                                ALU.subtract).then_inc(lo_done, 1)

            def rms(i, count, dst):
                dve.wait_ge(stat_full, i)
                V.tensor_scalar(tmp[:, 0, :], bank[:, 7, :], 1.0 / count, EPS, ALU.mult, ALU.add).then_inc(stat_read, 1)
                dve.wait_ge(sqrt_done, i)
                link(V.reciprocal(dst, tmp[:, 1, :]))
                link(V.tensor_tensor(tmp[:, 1, :], dst, dst, ALU.mult))
                dve.wait_ge(stat_read, i)
                link(V.tensor_tensor(tmp[:, 1, :], tmp[:, 1, :], tmp[:, 0, :], ALU.mult))
                link(V.tensor_scalar(tmp[:, 1, :], tmp[:, 1, :], -0.5, 1.5, ALU.mult, ALU.add))
                V.tensor_tensor(dst, dst, tmp[:, 1, :], ALU.mult).then_inc(rstd_done, 1)
                dve.wait_ge(rstd_done, i)

            def add_square(total, src, count, first):
                dve.wait_ge(sq_done, count)
                if first:
                    V.tensor_copy(total, src).then_inc(sq_added, 1)
                else:
                    dve.wait_ge(sq_added, count - 1)
                    V.tensor_tensor(total, total, src, ALU.add).then_inc(sq_added, 1)

            for s in (s_read, pt_lo, o_done, mg_lo):
                dve.sem_inc(s, 1)
            dve.wait_ge(tab_in, 16)
            lo_at(0, 0, 0)
            for k in range(KD):
                dve.wait_ge(xh_done, k + 1)
                V.scalar_tensor_tensor(xg_l[:, k, :], xT[:, k, :], tab[:, C_GATTN + k:C_GATTN + k + 1],
                                       xg_h[:, k, :].bitcast(F32), ALU.mult, ALU.subtract).then_inc(xl_done, 1)
                if k == 9:
                    lo_at(0, 0, 1)
            for k in range(KD):
                add_square(tmp[:, 0, :], gbuf[:, k % 2, :], k + 1, k == 0)
                if k == 9:
                    lo_at(0, 0, 2)
            dve.wait_ge(pos_in, 16)
            link(V.tensor_copy(small[:, 28:32], pos_a[:, S:S + QB]))
            V.tensor_scalar(small[:, 32:48], tab[:, C_SINK:C_SINK + A_HEADS], -1.0, None, ALU.mult).then_inc(neg_ready, 1)
            dve.wait_ge(mask_in, 16)
            for qb in range(QB):
                k0, k1 = key_range(qb)
                n = k1 - k0
                link(V.tensor_scalar(dist_t[:, 0:n], pos_a[:, k0:k1], small[:, 28 + qb:29 + qb], None, ALU.subtract))
                link(V.scalar_tensor_tensor(dist_t[:, 0:n], dist_t[:, 0:n], -1.0, dist_t[:, 0:n], ALU.mult, ALU.max))
                link(V.tensor_tensor(dist[:, qb, 0:n], dist[:, qb, 0:n], dist_t[:, 0:n], ALU.add))
            lo_at(0, 0, 3)
            rms(1, D, rstd[:])
            for i in range(2):
                dve.wait_ge(tile_full, i + 1)
                V.tensor_tensor(gbuf[:, i, :], bank[:, i, :], rstd[:], ALU.mult).then_inc(tile_read, 1)
            for g in range(A_KV):
                r = slice(HALF * (g % 2), HALF * (g % 2) + HALF)
                dve.wait_ge(kv_hi, g + 1)
                dve.wait_ge(tile_read, g // 2 + 1)
                V.tensor_tensor(kd_l[r, g, :], gbuf[r, g // 2, :], kd_h[r, g, :].bitcast(F32), ALU.subtract).then_inc(kv_ready, 1)
            lo_at(0, 0, 4)
            dve.wait_ge(col_full, 1)
            V.tensor_copy(small[:, 0:QB], bank[:, 7, 0:QB]).then_inc(col_ready, 1)
            dve.wait_ge(col_ready, 1)
            for tt in range(QB):
                dve.wait_ge(v_hi, tt + 1)
                V.scalar_tensor_tensor(va[:, tt, :, 1, :], bank[:, 2 + tt, 0:256].rearrange("p (g d) -> p g d", g=A_KV),
                                       small[:, tt:tt + 1], va[:, tt, :, 0, :].bitcast(F32), ALU.mult, ALU.subtract).then_inc(
                    tile_read, 1)
            lo_at(0, 0, 5)

            def gate_tile(J, jj, i):
                t = 5 * jj + i
                dve.wait_ge(tile_full, J * 10 + (T_A + t + 1))
                if jj or i > 2:
                    dve.wait_ge(gate_out[(i - 1) % 2], J * 64 + 16 * (2 * jj + (i - 1) // 2))
                V.tensor_tensor(gbuf[:, (i - 1) % 2, :], bank[:, (3, 7)[t % 2], :], rstd[:], ALU.mult).then_inc(tile_read, 1)

            def maximum(before, h):
                dve.wait_ge(s_read, 1 + before * 4 + (4 * h + 4))
                V.tensor_reduce(small[:, 4:8], s_sb[:], AX_X, ALU.max).then_inc(a_max, 1)
                dve.wait_ge(a_max, before + (h + 1))

            def biased(J, h):
                if h == 0:
                    dve.wait_ge(pad_set, 2)
                for n, qb in enumerate(A_ORDER):
                    dve.wait_ge(s_full, 1 + J * 16 + (4 * h + max(n + 1, 2)))
                    if n == 0:
                        dve.wait_ge(a_exp, 1 + J * 20 + 5 * h)
                    k0, k1 = key_range(qb)
                    b, c = A_BANK[qb]
                    V.scalar_tensor_tensor(s_sb[:, qb, 0:k1 - k0], dist[:, qb, 0:k1 - k0],
                                           tab[:, bass.ds(J * 4 + (C_SLOPE + h), 1)], bank[:, b, c:c + k1 - k0],
                                           ALU.mult, ALU.add).then_inc(s_read, 1)
                maximum(J * 4, h)
                V.tensor_scalar(small[:, 8:12], small[:, 4:8], -A_SCALE, small[:, bass.ds(J * 4 + (32 + h), 1)],
                                ALU.mult, ALU.min).then_inc(a_shift, 1)

            def normalise_a(J, h):
                dve.wait_ge(a_exp, 1 + J * 20 + (5 * h + 5))
                V.tensor_tensor(small[:, 20:24], small[:, 12:16], small[:, 16:20], ALU.add).then_inc(a_den, 1)
                dve.wait_ge(a_den, J * 8 + (2 * h + 1))
                V.reciprocal(small[:, 24:28], small[:, 20:24]).then_inc(a_den, 1)
                dve.wait_ge(a_den, J * 8 + (2 * h + 2))
                for qb in range(QB):
                    n = key_range(qb)[1] - key_range(qb)[0]
                    V.tensor_scalar(pA[:, qb, 0:n], pA[:, qb, 0:n], small[:, 24 + qb:25 + qb], None, ALU.mult).then_inc(p_ready, 1)

            def turned_lo(base, h, kbs, width, hi_t, lo_t):
                for kb in kbs:
                    dve.wait_ge(pt_hi, base + (4 * h + kb + 1))
                    n = width(kb)
                    V.tensor_tensor(lo_t[:, kb, 0:n], bank[:, 4 + kb % 2, 0:n], hi_t[:, kb, 0:n].bitcast(F32),
                                    ALU.subtract).then_inc(pt_lo, 1)

            def a_n(kb):
                return key_range(kb)[1] - key_range(kb)[0]

            def out_sum(dst, count, e):
                dve.wait_ge(pv_half, count + 1)
                V.tensor_tensor(dst, bank[0:HALF, 6, :], otmp[:], ALU.add).then_inc(o_done, 1)

            dve.wait_ge(neg_ready, 1)
            with dve.Fori(0, 4) as J:
                for jj in range(2):
                    h0, h1 = 2 * jj, 2 * jj + 1
                    dve.wait_ge(tile_full, J * 10 + (T_A + 5 * jj + 1))
                    V.tensor_tensor(qf[:], bank[:, (3, 7)[5 * jj % 2], :], rstd[:], ALU.mult).then_inc(tile_read, 1)
                    dve.wait_ge(q_hi, J * 4 + (2 * jj + 2))
                    dve.wait_ge(tile_read, J * 10 + (T_A + 5 * jj + 1))
                    V.tensor_tensor(qs[HALF:P, 0, :], qf[0:HALF, :], qs[0:HALF, 0, :].bitcast(F32), ALU.subtract).then_inc(q_ready, 1)
                    V.tensor_tensor(qs[0:HALF, 1, :], qf[HALF:P, :], qs[HALF:P, 1, :].bitcast(F32), ALU.subtract).then_inc(q_ready, 1)

                    def next_lo(i):
                        lo_at(N_A, J * 10, 5 * jj + i + 2)

                    def out_a(h):
                        out_sum(oA[HALF * (h % 2):HALF * (h % 2) + HALF, bass.ds(J * 2 + h // 2, 1), :].rearrange("p a s -> p (a s)"),
                                J * 4 + h, h)
                    next_lo(0)
                    gate_tile(J, jj, 1)
                    biased(J, h0)
                    next_lo(1)
                    normalise_a(J, h0)
                    gate_tile(J, jj, 2)
                    turned_lo(J * 16, h0, (0, 1), a_n, pTA_h, pTA_l)
                    next_lo(2)
                    turned_lo(J * 16, h0, (2, 3), a_n, pTA_h, pTA_l)
                    biased(J, h1)
                    gate_tile(J, jj, 3)
                    normalise_a(J, h1)
                    out_a(h0)
                    next_lo(3)
                    turned_lo(J * 16, h1, (0, 1), a_n, pTA_h, pTA_l)
                    turned_lo(J * 16, h1, (2, 3), a_n, pTA_h, pTA_l)
                    out_a(h1)
                    gate_tile(J, jj, 4)
                    next_lo(4)
                for b in range(2):
                    dve.wait_ge(gate_out[b], J * 64 + 64)

            def angles():
                magic = 1.5 * 2.0 ** 23
                dve.wait_ge(pos_in, 32)
                link(V.tensor_copy(posf[:], pos_i[:]))
                link(V.tensor_scalar(ang[:], posf[:], tab[:, C_INVF:C_INVF + 1], None, ALU.mult))
                link(V.tensor_scalar(turns[:], ang[:], 0.15915494309189535, magic, ALU.mult, ALU.add))
                link(V.tensor_scalar(turns[:], turns[:], magic, None, ALU.subtract))
                link(V.tensor_scalar(t_hi[:], turns[:], magic * 2048, None, ALU.add))
                link(V.tensor_scalar(t_hi[:], t_hi[:], magic * 2048, None, ALU.subtract))
                link(V.tensor_tensor(t_lo[:], turns[:], t_hi[:], ALU.subtract))
                for part in TWO_PI_PARTS:
                    for t in (t_hi, t_lo):
                        link(V.scalar_tensor_tensor(ang[:], t[:], -part, ang[:], ALU.mult, ALU.add))
                link(V.scalar_tensor_tensor(turns[:], ang[:], -1.0, ang[:], ALU.mult, ALU.max))
                V.tensor_scalar(turns[:], turns[:], -0.5, 1.5707963267948966, ALU.mult, ALU.add).then_inc(ang_ready, 1)

            for m in range(KQ + KKV):
                dve.wait_ge(tile_full, T_LAT + m + 1)
                dst = cqf[:, m, :] if m < KQ else ckvf[:, m - KQ, :]
                V.tensor_tensor(dst, bank[:, m, :], rstd[:], ALU.mult).then_inc(tile_read, 1)
                lo_at(N_LAT, 0, m + 2)
                if m == 1:
                    angles()
                if m == KQ:
                    rms(2, Q_LORA, lat_rstd[:])
                    for k in range(KQ):
                        V.tensor_tensor(cqf[:, k, :], cqf[:, k, :], lat_rstd[:], ALU.mult).then_inc(lat_norm, 1)
                    for k in range(KQ):
                        dve.wait_ge(lat_hi, k + 1)
                        V.scalar_tensor_tensor(cq_l[:, k, :], cqf[:, k, :], tab[:, C_GQ + k:C_GQ + k + 1],
                                               cq_h[:, k, :].bitcast(F32), ALU.mult, ALU.subtract).then_inc(lat_lo, 1)
                add_square(sumsq[:], sqL[:, m % 2, :], KD + m + 1, m in (0, KQ))
            dve.wait_ge(sin_done, 2)
            link(V.tensor_tensor(cosb[:], t_hi[:], t_hi[:], ALU.mult))
            link(V.tensor_scalar(cosb[:], cosb[:], -2.0, 1.0, ALU.mult, ALU.add))
            link(V.tensor_tensor(sinb[:], t_hi[:], t_lo[:], ALU.mult))
            link(V.tensor_scalar(sinb[:], sinb[:], tab[:, C_SIGN:C_SIGN + 1], 2.0, ALU.mult, ALU.mult))
            dve.wait_ge(tile_full, T_B)
            r0 = slice(0, ROPE)
            V.tensor_tensor(rope_a[r0, :], bank[r0, 6, :], rstd[r0, :], ALU.mult).then_inc(tile_read, 1)
            lo_at(N_LAT, 0, 8)
            dve.wait_ge(tile_read, T_B)
            swap = [(i + 16) % 32 for i in range(32)]
            link(V.stream_shuffle(rope_b[r0, :], rope_a[r0, :], swap))
            link(V.tensor_tensor(rope_b[r0, :], rope_b[r0, :], sinb[r0, :], ALU.mult))
            link(V.tensor_tensor(rope_a[r0, :], rope_a[r0, :], cosb[r0, :], ALU.mult))
            V.tensor_tensor(rope_a[r0, :], rope_a[r0, :], rope_b[r0, :], ALU.add).then_inc(kr_ready, 1)
            dve.wait_ge(kr_split, 1)
            V.tensor_tensor(rope_l[r0, :], rope_a[r0, :], rope_h[r0, :].bitcast(F32), ALU.subtract).then_inc(kr_split, 1)
            rms(3, KV_LORA, lat_rstd[:])
            for k in range(KKV):
                V.tensor_tensor(ckvf[:, k, :], ckvf[:, k, :], lat_rstd[:], ALU.mult).then_inc(lat_norm, 1)
            for k in range(KKV):
                dve.wait_ge(lat_hi, KQ + k + 1)
                V.scalar_tensor_tensor(ckv_l[:, k, :], ckvf[:, k, :], tab[:, C_GKV + k:C_GKV + k + 1],
                                       ckv_h[:, k, :].bitcast(F32), ALU.mult, ALU.subtract).then_inc(lat_lo, 1)

            def pair_lo(g, which, i):
                b = (7, 6)[i] if which == 0 else i
                hi_t, lo_t = ((q_h, q_l), (k_h, k_l))[which]
                dve.wait_ge(b_hi, 8 * g + (4 * which + 2 * i + 2))
                for e in range(2):
                    r = slice(HALF * e, HALF * e + HALF)
                    V.tensor_tensor(lo_t[r, 2 * i + e, :], bank[r, b, :], hi_t[r, 2 * i + e, :].bitcast(F32),
                                    ALU.subtract).then_inc((b_lo, tile_read)[e], 1)

            def rotate(g):
                dve.wait_ge(tile_full, 7 * g + (T_B + 3))
                if not (isinstance(g, int) and g == 0):
                    dve.wait_ge(r_moved, 128 * g)
                V.tensor_tensor(rope_a[:], bank[:, 7, :], cosb[:], ALU.mult).then_inc(r_part, 1)
                V.stream_shuffle(rope_b[:], bank[:, 7, :], swap).then_inc(tile_read, 1)
                dve.wait_ge(tile_read, 7 * g + (T_B + 3))
                V.tensor_tensor(rope_b[:], rope_b[:], sinb[:], ALU.mult).then_inc(r_part, 1)
                dve.wait_ge(r_part, 2 * g + 2)
                V.tensor_tensor(rope_a[:], rope_a[:], rope_b[:], ALU.add).then_inc(r_sum, 1)

            def rotate_lo(g):
                dve.wait_ge(r_hi, g + 1)
                V.tensor_tensor(rope_l[:], rope_a[:], rope_h[:].bitcast(F32), ALU.subtract).then_inc(r_lo, 1)

            def values_lo(g):
                for i in range(2):
                    dve.wait_ge(v_hi, 2 * g + (QB + i + 1))
                    V.tensor_tensor(vb[:, 2 * i:2 * i + 2, :, 1, :].rearrange("p t e d -> p (t e) d"),
                                    bank[:, 2 + i, :].rearrange("p (a d) -> p a d", d=HALF),
                                    vb[:, 2 * i:2 * i + 2, :, 0, :].rearrange("p t e d -> p (t e) d").bitcast(F32),
                                    ALU.subtract).then_inc(tile_read, 1)

            def maximum_b(g, e):
                dve.wait_ge(s_full, 1 + 16 * g + (4 * A_HEADS + 4 * e + 4))
                V.tensor_reduce(small[:, 4:8], bank[:, 0:QB, :], AX_X, ALU.max).then_inc(a_max, 1)
                dve.wait_ge(a_max, 4 * g + (A_HEADS + e + 1))
                V.tensor_scalar(small[:, 8:12], small[:, 4:8], -B_SCALE, None, ALU.mult).then_inc(a_shift, 1)

            def normalise_b(g, e):
                dve.wait_ge(a_exp, 1 + 16 * g + (5 * A_HEADS + 4 * e + 4))
                V.reciprocal(small[:, 24:28], small[:, 12:16]).then_inc(a_den, 1)
                dve.wait_ge(a_den, 4 * g + (2 * A_HEADS + e + 1))
                for qb in range(QB):
                    V.tensor_scalar(pB[:, qb, :], pB[:, qb, :], small[:, 24 + qb:25 + qb], None, ALU.mult).then_inc(p_ready, 1)

            def lo_b(g, e, kbs):
                turned_lo(16 * g + 4 * A_HEADS, e, kbs, lambda kb: S, pTB_h, pTB_l)

            def out_b(g, e):
                r = slice(HALF * (e % 2), HALF * (e % 2) + HALF)
                if isinstance(g, int):
                    dst = oB[r, 2 * g + e // 2, :]
                else:
                    dst = oB[r, bass.ds(2 * g + e // 2, 1), :].rearrange("p a s -> p (a s)")
                out_sum(dst, 4 * g + (A_HEADS + e), e)

            def b_group(g, more):
                maximum_b(g, 0)
                for e in range(3):
                    normalise_b(g, e)
                    lo_b(g, e, (0, 1))
                    maximum_b(g, e + 1)
                    lo_b(g, e, (2, 3))
                    out_b(g, e)
                    if e < 2:
                        lo_at(N_B, 2 * g, 2 + e, (1536, 1024)[e] if more else BLK)
                normalise_b(g, 3)
                if more:
                    pair_lo(g + 1, 0, 0)
                    pair_lo(g + 1, 0, 1)
                    lo_b(g, 3, (0, 1))
                    rotate(g + 1)
                    lo_b(g, 3, (2, 3))
                    rotate_lo(g + 1)
                    pair_lo(g + 1, 1, 0)
                    pair_lo(g + 1, 1, 1)
                    out_b(g, 3)
                    values_lo(g + 1)
                else:
                    lo_b(g, 3, (0, 1))
                    lo_b(g, 3, (2, 3))
                    out_b(g, 3)

            pair_lo(0, 0, 0)
            pair_lo(0, 0, 1)
            rotate(0)
            rotate_lo(0)
            pair_lo(0, 1, 0)
            pair_lo(0, 1, 1)
            values_lo(0)
            with dve.Fori(0, GROUPS - 1) as g:
                b_group(g, True)
            b_group(GROUPS - 1, False)

            for b, (o, oh, ol) in enumerate(((oA, oA_h, oA_l), (oB, oB_h, oB_l))):
                for k in range(8):
                    dve.wait_ge(o_hi, 8 * b + k + 1)
                    V.tensor_tensor(ol[:, k, :], o[:, k, :], oh[:, k, :].bitcast(F32), ALU.subtract).then_inc(o_lo, 1)
            with dve.Fori(0, 8) as p:
                for i in range(2):
                    dve.wait_ge(tile_full, 4 * p + (T_BR + i + 1))
                    dve.wait_ge(gate_sig, 2 * p + 1)
                    dve.wait_ge(mg_lo, 1 + 2 * p)
                    V.tensor_tensor(tmp[:, i, :], bank[:, i, :], sg[:, 0, i, :], ALU.mult).then_inc(tile_read, 1)
                lo_at(N_BR, 2 * p, 2)
                for i in range(2):
                    dve.wait_ge(tile_full, 4 * p + (T_BR + i + 3))
                    dve.wait_ge(gate_sig, 2 * p + 2)
                    V.tensor_tensor(mt[:], bank[:, 2 + i, :], sg[:, 1, i, :], ALU.mult).then_inc(tile_read, 1)
                    dve.wait_ge(tile_read, 4 * p + (T_BR + i + 3))
                    V.tensor_tensor(tmp[:, i, :], tmp[:, i, :], mt[:], ALU.add).then_inc(merged, 1)
                    dve.wait_ge(merged, 2 * p + (i + 1))
                    dve.wait_ge(mg_hi, 2 * p + (i + 1))
                    V.tensor_tensor(mg_l[:, bass.ds(2 * p + i, 1), :], tmp[:, i:i + 1, :],
                                    mg_h[:, bass.ds(2 * p + i, 1), :].bitcast(F32), ALU.subtract).then_inc(mg_lo, 1)
                lo_at(N_BR, 2 * p, 3)

            link(V.memset(ssum[:], 0.0))
            with dve.Fori(0, 8) as p:
                for i in range(2):
                    dve.wait_ge(tile_full, 2 * p + (T_OUT + i + 1))
                    if i == 0:
                        dve.wait_ge(xin_in, 16 * p + 16)
                    V.tensor_tensor(x2[:, bass.ds(2 * p + i, 1), :], bank[:, 4 + i:5 + i, :], xin[:, i:i + 1, :],
                                    ALU.add).then_inc(tile_read, 1)
                    lo_at(N_OUT, 2 * p, 2 + i)
                    dve.wait_ge(sq_done, 2 * p + (KD + KQ + KKV + i + 1))
                    dve.wait_ge(sq_added, 2 * p + (KD + KQ + KKV + i))
                    V.tensor_tensor(ssum[:], ssum[:], sq[:, i, :], ALU.add).then_inc(sq_added, 1)
            for k in range(KD):
                dve.wait_ge(tile_full, T_MLP)
                dve.wait_ge(h2_hi, k + 1)
                V.scalar_tensor_tensor(h2_l[:, k, :], x2[:, k, :], tab[:, C_GMLP + k:C_GMLP + k + 1],
                                       h2_h[:, k, :].bitcast(F32), ALU.mult, ALU.subtract).then_inc(h2_lo, 1)
            rms(4, D, rstd[:])

            def up(c, q):
                for i in range(2):
                    n = CH * c + 2 * q + (i + 1)
                    dve.wait_ge(tile_full, 24 * c + 2 * q + (T_MLP + i + 1))
                    V.scalar_tensor_tensor(ru[:], bank[:, i, :], 0.0, rstd[:], ALU.max, ALU.mult).then_inc(tile_read, 1)
                    dve.wait_ge(tile_read, 24 * c + 2 * q + (T_MLP + i + 1))
                    V.tensor_tensor(uu[:], ru[:], ru[:], ALU.mult).then_inc(u_sq, 1)
                    dve.wait_ge(u_sq, n)
                    dve.wait_ge(u_hi, n)
                    V.tensor_tensor(u_l[:, bass.ds(2 * q + i, 1), :], uu[:].rearrange("p (a s) -> p a s", a=1),
                                    u_h[:, bass.ds(2 * q + i, 1), :].bitcast(F32), ALU.subtract).then_inc(u_lo, 1)
                    lo_at(N_MLP, 16 * c + 2 * q, 2 + i)

            def down(c, q, last=False):
                for b in range(2):
                    for j in range(2):
                        i = 2 * b + j
                        dve.wait_ge(tile_full, 24 * c + 4 * q + (T_MLP + CH + i + 1))
                        at_m = x2[:, bass.ds(4 * q + i, 1), :]
                        V.tensor_tensor(at_m, bank[:, 2 + i:3 + i, :], at_m, ALU.add).then_inc(tile_read, 1)
                    if not (last and q == 3):
                        lo_at(N_MLP + CH, 16 * c + 2 * q, 2 + b)
                    if last:
                        for j in range(2):
                            m = 4 * q + 2 * b + j
                            add_square(ssum[:], sq[:, j, :], 2 * KD + KQ + KKV + m + 1, m == 0)

            with dve.Fori(0, CHUNKS - 1) as c:
                with dve.Fori(0, 4) as q:
                    up(c, q)
                with dve.Fori(0, 4) as q:
                    down(c, q)
            with dve.Fori(0, 4) as q:
                up(CHUNKS - 1, q)
            for q in range(4):
                down(CHUNKS - 1, q, True)
            rms(5, D, rstd[:])
            for m in range(KD):
                dve.wait_ge(fin_gain, m + 1)
                V.tensor_tensor(outT[:, m, :], outT[:, m, :], rstd[:], ALU.mult).then_inc(fin_ready, 1)


def layout(inputs):
    import numpy as np
    f = np.float32

    def rows(w, width):
        return w.reshape(w.shape[0] // P, P, w.shape[1] // width, width)

    w_in = np.asarray(inputs["w_in"])[0]
    cuts = np.cumsum([1024, 256, 256, Q_LORA, KV_LORA, ROPE, D])
    qa, ka, va, cq, ckv, kr, ga, gb = np.split(w_in, cuts, axis=1)
    W = np.zeros((N_END, P, BLK), f)

    def cols(w):
        return rows(w, P).transpose(2, 1, 0, 3).reshape(-1, P, BLK)

    W[0:2] = cols(ka)
    W[2:4] = va.reshape(2, 8, P, 256).transpose(0, 2, 1, 3).reshape(2, P, BLK)
    a = W[N_A:N_LAT].reshape(8, 5, P, BLK)
    a[:, 0] = cols(qa)
    a[:, 1:] = np.concatenate([cols(ga), cols(gb)]).reshape(8, 4, P, BLK)
    W[N_LAT:N_LAT + 4] = cols(cq)
    W[N_LAT + 4:N_LAT + 6] = cols(ckv)
    W[N_LAT + 6][:, :KD * ROPE] = kr.reshape(KD, P, ROPE).transpose(1, 0, 2).reshape(P, -1)
    uq, uk, uv = (np.asarray(inputs[n])[0] for n in ("b_w_uq", "b_w_uk", "b_w_uv"))
    for g in range(GROUPS):
        hs = slice(4 * g, 4 * g + 4)
        q = uq[:, hs].reshape(KQ, P, 4, NOPE + ROPE)
        q = np.concatenate([q[..., :NOPE].reshape(KQ, P, -1), q[..., NOPE:].reshape(KQ, P, -1)], axis=2)
        W[N_B + 2 * g][:, :KQ * 384] = q.transpose(1, 0, 2).reshape(P, -1)
        for i, u in enumerate((uk, uv)):
            W[N_B + 2 * g + 1][:, 512 * i:512 * i + 512] = u[:, hs].reshape(KKV, P, 256).transpose(1, 0, 2).reshape(P, -1)

    def halves(w):
        k, m = w.shape
        return w.reshape(k // 1024, 8, P, m // 256, 256).transpose(0, 3, 2, 1, 4).reshape(k // 1024, m // 256, P, BLK)

    br = W[N_BR:N_OUT].reshape(8, 2, P, BLK)
    br[:, 0] = halves(np.asarray(inputs["w_branch_a"])[0])[0]
    br[:, 1] = halves(np.asarray(inputs["w_branch_b"])[0])[0]
    W[N_OUT:N_MLP] = cols(np.asarray(inputs["w_out"])[0])
    mlp = W[N_MLP:].reshape(CHUNKS, 2, 8, P, BLK)
    mlp[:, 0] = cols(np.asarray(inputs["w_mlp_in"])[0]).reshape(CHUNKS, 8, P, BLK)
    mlp[:, 1] = halves(np.asarray(inputs["w_mlp_out"])[0])

    tab = np.zeros((P, C_ALL), f)
    tab[:, C_ONES:C_ONES + P] = 1.0
    tab[:, C_IDENT:C_IDENT + P] = np.eye(P, dtype=f)
    for c, n in ((C_GATTN, "attn_norm_g"), (C_GMLP, "mlp_norm_g"), (C_GFIN, "final_norm_g"), (C_GQ, "b_q_norm_g"),
                 (C_GKV, "b_kv_norm_g")):
        g = np.asarray(inputs[n]).reshape(-1, P).T
        tab[:, c:c + g.shape[1]] = g
    tab[:, C_SLOPE:C_SLOPE + A_HEADS] = -np.exp2(-8.0 * (np.arange(A_HEADS) + 1.0) / A_HEADS).astype(f) / A_SCALE
    tab[:, C_SINK:C_SINK + A_HEADS] = np.asarray(inputs["a_sink"])
    p = np.arange(P)
    tab[:, C_INVF] = (f(10000.0) ** (-(np.arange(16, dtype=f)) / f(16)))[p % 16]
    tab[:, C_SIGN] = np.where(p % ROPE < ROPE // 2, -1.0, 1.0)
    mask = np.zeros((P, QB, 3 * P), f)
    for qb in range(QB):
        k0, k1 = key_range(qb)
        d = np.abs(P * qb + np.arange(P)[:, None] - np.arange(k0, k1)[None])
        mask[:, qb, :k1 - k0] = np.where(d <= WINDOW, 0.0, 1e30)
    pos = np.asarray(inputs["positions"])[0]
    pos = np.concatenate([np.broadcast_to(pos, (P, S)), pos.reshape(QB, P).T], axis=1)
    xT = np.asarray(inputs["x"])[0].T.reshape(KD, P, S).transpose(1, 0, 2)
    return {"xT": xT, "tab": tab, "pos": pos, "mask": mask, "w": W}


def kernel(**inputs):
    import numpy as np
    import concourse.bacc as bacc
    from concourse.bass_utils import run_bass_kernel_spmd

    nc = bacc.Bacc("TRN2", target_bir_lowering=False, num_devices=1)
    arrays, args = {}, []
    for name, a in layout(inputs).items():
        a = np.ascontiguousarray(a)
        arrays["in_" + name] = a
        args.append(nc.dram_tensor("in_" + name, a.shape, mybir.dt.from_np(a.dtype), kind="ExternalInput").ap())
    args.append(nc.dram_tensor("out_t", (P, KD, S), F32, kind="ExternalOutput").ap())
    build(nc, *args)
    r = run_bass_kernel_spmd(nc, [arrays], core_ids=[0])
    return np.ascontiguousarray(r.results[0]["out_t"].transpose(2, 1, 0).reshape(1, S, D))
```

```python
from contextlib import ExitStack

import concourse.bass as bass
from concourse import mybir

F32 = mybir.dt.float32
F32R = mybir.dt.float32r
I32 = mybir.dt.int32
ALU = mybir.AluOpType
ACT = mybir.ActivationFunctionType
AX_X = mybir.AxisListType.X

P = 128
S = 512
D = 2048
KD = D // P
DFF = 4 * D
EPS = 1e-6
QB = S // P
HALF = 64
A_HEADS, A_KV, WINDOW = 16, 4, 128
B_HEADS, Q_LORA, KV_LORA, NOPE, ROPE = 16, 512, 256, 64, 32
KQ, KKV = Q_LORA // P, KV_LORA // P
GROUPS = B_HEADS // 4
A_SCALE = 0.125
B_SCALE = float((NOPE + ROPE) ** -0.5)
BLK = 2048
CH = 8
CHUNKS = DFF // (CH * P)

N_A, T_A = 4, 6
N_LAT, T_LAT = N_A + 40, T_A + 40
N_B, T_B = N_LAT + 7, T_LAT + 7
N_BR, T_BR = N_B + 2 * GROUPS, T_B + 7 * GROUPS
N_OUT, T_OUT = N_BR + 16, T_BR + 32
N_MLP, T_MLP = N_OUT + 16, T_OUT + 16
N_END, T_END = N_MLP + 16 * CHUNKS, T_MLP + 24 * CHUNKS

C_ONES, C_GATTN, C_GMLP, C_GFIN, C_GQ, C_GKV, C_SLOPE, C_SINK, C_INVF, C_SIGN, C_POS = (
    0, 128, 144, 160, 176, 180, 182, 198, 214, 215, 216)
C_IDENT = 220
A_ORDER = (0, 3, 1, 2)
A_BANK = ((0, 0), (1, 0), (2, 0), (0, 256))
C_ALL = C_IDENT + P

TWO_PI_PARTS = (6.283203125, -1.7821788787841797e-05, 3.9693904e-09)

FIRST_ORDER = ("q0", "q1", "r", "k0", "k1", "v0", "v1")
NEXT_ORDER = ("q0", "r", "k0", "q1", "k1", "v0", "v1")
FIRST_BANK = (0, 1, 7, 2, 3, 4, 5)
FILL_1 = ("q0", "r", "q1", "k1")
FILL_2 = (None, "k0", None, "v0")


def place(kind, g):
    if isinstance(g, int) and g == 0:
        return FIRST_ORDER.index(kind) + 1, FIRST_BANK[FIRST_ORDER.index(kind)]
    return NEXT_ORDER.index(kind) + 1, 7


def key_range(qb):
    return max(0, qb - 1) * P, min(QB, qb + 2) * P


def build(nc, xT_d, tab_d, pos_d, mask_d, w_d, out_d):
    gates_d = nc.dram_tensor("gates_scratch", (32, P, S), F32, kind="Internal").ap()

    KB = 1024
    BASE = 16512

    def at(name, kb, shape, dt):
        return nc.alloc_sbuf_tensor_at(name, shape, dt, offset=BASE + int(kb * KB))

    raw = at("raw", 0, [P, 2, BLK], F32)
    wsp = at("wsp", 16, [P, 2, 2, BLK], F32R)
    tab = at("tab", 48, [P, C_ALL], F32)
    rstd = at("rstd", 50, [P, S], F32)
    small = at("small", 52, [P, 64], F32)
    tmp = at("tmp", 52.5, [P, 2, S], F32)
    dist_t = at("dist_t", 154, [P, S], F32)
    otmp = at("otmp", 56.5, [HALF, S], F32)
    xg_h = at("xg_h", 60, [P, KD, S], F32R)
    xg_l = at("xg_l", 92, [P, KD, S], F32R)
    xT = at("xT", 124, [P, KD, S], F32)
    dist = at("dist", 124, [P, QB, 3 * P], F32)
    s_sb = at("s_sb", 130, [P, QB, 3 * P], F32)
    pA = at("pA", 136, [P, QB, 3 * P], F32)
    pTA_h = at("pTA_h", 142, [P, QB, 3 * P], F32R)
    pTA_l = at("pTA_l", 148, [P, QB, 3 * P], F32R)
    qf = at("qf", 154, [P, S], F32)
    kd_h = at("kd_h", 156, [P, A_KV, S], F32R)
    kd_l = at("kd_l", 164, [P, A_KV, S], F32R)
    va = at("va", 172, [P, QB, A_KV, 2, HALF], F32R)
    vc = at("vc", 180, [P, QB, 2, HALF], F32R)
    oA = at("oA", 182, [P, 8, S], F32)
    qs = at("qs", 198, [P, 2, S], F32R)
    pos_a = at("pos_a", 198, [P, S + QB], I32)
    gbuf = at("gbuf", 202, [P, 2, S], F32)
    cqf = at("cqf", 124, [P, KQ, S], F32)
    ckvf = at("ckvf", 132, [P, KKV, S], F32)
    cq_h = at("cq_h", 136, [P, KQ, S], F32R)
    cq_l = at("cq_l", 144, [P, KQ, S], F32R)
    ckv_h = at("ckv_h", 152, [P, KKV, S], F32R)
    ckv_l = at("ckv_l", 156, [P, KKV, S], F32R)
    cosb = at("cosb", 160, [P, S], F32)
    sinb = at("sinb", 162, [P, S], F32)
    oB = at("oB", 164, [P, 8, S], F32)
    sqL = at("sqL", 198, [P, 2, S], F32)
    lat_rstd = at("lat_rstd", 178, [P, S], F32)
    sumsq = at("sumsq", 180, [P, S], F32)
    rope_a = at("rope_a", 198, [P, S], F32)
    rope_b = at("rope_b", 200, [P, S], F32)
    rope_h = at("rope_h", 202, [P, S], F32R)
    rope_l = at("rope_l", 204, [P, S], F32R)
    q_h = at("q_h", 60, [P, 4, S], F32R)
    q_l = at("q_l", 68, [P, 4, S], F32R)
    k_h = at("k_h", 76, [P, 4, S], F32R)
    k_l = at("k_l", 84, [P, 4, S], F32R)
    vb = at("vb", 92, [P, 2, QB, 2, 2, HALF], F32R)
    pB = [at("pB0", 100, [P, QB, S], F32), at("pB1", 124, [P, QB, S], F32)]
    pTB_h = at("pTB_h", 108, [P, QB, S], F32R)
    pTB_l = at("pTB_l", 116, [P, QB, S], F32R)
    oA_h = at("oA_h", 60, [P, 8, S], F32R)
    oA_l = at("oA_l", 76, [P, 8, S], F32R)
    oB_h = at("oB_h", 92, [P, 8, S], F32R)
    oB_l = at("oB_l", 108, [P, 8, S], F32R)
    mg_h = at("mg_h", 124, [P, KD, S], F32R)
    mg_l = at("mg_l", 156, [P, KD, S], F32R)
    sg = at("sg", 188, [P, 2, 2, S], F32)
    gl = at("gl", 198, [P, 2, 2, S], F32)
    mt = at("mt", 196, [P, S], F32)
    x2 = at("x2", 60, [P, KD, S], F32)
    h2_h = at("h2_h", 92, [P, KD, S], F32R)
    h2_l = at("h2_l", 124, [P, KD, S], F32R)
    u_h = at("u_h", 156, [P, CH, S], F32R)
    u_l = at("u_l", 172, [P, CH, S], F32R)
    xin = at("xin", 188, [P, 2, S], F32)
    ssum = at("ssum", 192, [P, S], F32)
    sq = at("sq", 194, [P, 2, S], F32)
    ru = at("ru", 198, [P, S], F32)
    uu = at("uu", 200, [P, S], F32)
    outT = at("outT", 92, [P, KD, S], F32)
    pos_i = at("pos_i", 172, [P, S], I32)
    posf = at("posf", 174, [P, S], F32)
    ang = at("ang", 164, [P, S], F32)
    turns = at("turns", 166, [P, S], F32)
    t_hi = at("t_hi", 168, [P, S], F32)
    t_lo = at("t_lo", 170, [P, S], F32)

    with ExitStack() as ctx:
        bank = ctx.enter_context(nc.psum_tensor("bank", [P, 8, S], F32))

        def sem(name):
            return ctx.enter_context(nc.semaphore(name))

        raw_full = [sem("raw_full0"), sem("raw_full1")]
        hi_done, lo_done = sem("hi_done"), sem("lo_done")
        tile_full, tile_read = sem("tile_full"), sem("tile_read")
        tab_in = sem("tab_in")
        x_in = [sem(f"x_in{c}") for c in range(4)]
        mask_in, pos_in = sem("mask_in"), sem("pos_in")
        xh_done, xl_done = sem("xh_done"), sem("xl_done")
        sq_done, sq_added = sem("sq_done"), sem("sq_added")
        stat_full, stat_read, col_full = sem("stat_full"), sem("stat_read"), sem("col_full")
        sqrt_done, sin_done = sem("sqrt_done"), sem("sin_done")
        rstd_done = sem("rstd_done")
        chain, col_ready, ang_ready = sem("chain"), sem("col_ready"), sem("ang_ready")
        kv_hi, kv_ready = sem("kv_hi"), sem("kv_ready")
        v_half, v_hi, vc_ready = sem("v_half"), sem("v_hi"), sem("vc_ready")
        pad_set = sem("pad_set")
        q_hi, q_ready = sem("q_hi"), sem("q_ready")
        s_full, s_read = sem("s_full"), sem("s_read")
        neg_ready, dist_ready = sem("neg_ready"), sem("dist_ready")
        a_max, a_shift, a_exp, a_den, p_ready, p_ready2 = (
            sem("a_max"), sem("a_shift"), sem("a_exp"), sem("a_den"), sem("p_ready"), sem("p_ready2"))
        t_full, pt_hi, pt_lo = sem("t_full"), sem("pt_hi"), sem("pt_lo")
        pv_full, pv_half, o_done = sem("pv_full"), sem("pv_half"), sem("o_done")
        gate_out = [sem("gate_out0"), sem("gate_out1")]
        lat_norm, lat_hi, lat_lo = sem("lat_norm"), sem("lat_hi"), sem("lat_lo")
        kr_ready, kr_split, kr_spread = sem("kr_ready"), sem("kr_split"), sem("kr_spread")
        zero_set = sem("zero_set")
        r_part = sem("r_part")
        b_hi, b_lo, r_sum, r_hi, r_lo = sem("b_hi"), sem("b_lo"), sem("r_sum"), sem("r_hi"), sem("r_lo")
        r_moved = [sem("r_moved0"), sem("r_moved1")]
        o_hi, o_lo = sem("o_hi"), sem("o_lo")
        gate_in = [sem("gate_inA"), sem("gate_inB")]
        gate_sig, merged, mg_hi, mg_lo = sem("gate_sig"), sem("merged"), sem("mg_hi"), sem("mg_lo")
        xin_in = sem("xin_in")
        h2_hi, h2_lo = sem("h2_hi"), sem("h2_lo")
        u_sq, u_hi, u_lo = sem("u_sq"), sem("u_hi"), sem("u_lo")
        fin_gain, fin_ready, stored = sem("fin_gain"), sem("fin_ready"), sem("stored")

        block = ctx.enter_context(nc.Block())
        ones = tab[:, C_ONES:C_ONES + P]
        ident = tab[:, C_IDENT:C_IDENT + P]

        @block.sync
        def _(sp):
            sp.dma_start(tab[:], tab_d).then_inc(tab_in, 16)
            sp.dma_start(xT[:, 0:4, :], xT_d[:, 0:4, :]).then_inc(x_in[0], 16)
            sp.dma_start(raw[:, 0, :], w_d[0]).then_inc(raw_full[0], 16)
            for c in range(1, 4):
                sp.dma_start(xT[:, 4 * c:4 * c + 4, :], xT_d[:, 4 * c:4 * c + 4, :]).then_inc(x_in[c], 16)
                if c == 1:
                    sp.dma_start(raw[:, 1, :], w_d[1]).then_inc(raw_full[1], 16)
            with sp.Fori(1, N_END // 2) as h:
                for slot in range(2):
                    sp.wait_ge(hi_done, h * 2 + slot - 1)
                    sp.wait_ge(lo_done, h * 2 + slot - 1)
                    sp.dma_start(raw[:, slot, :], w_d[bass.ds(h * 2 + slot, 1)].rearrange("a p k -> p (a k)")).then_inc(
                        raw_full[slot], 16)
            n = N_END - 1
            sp.wait_ge(hi_done, n - 1)
            sp.wait_ge(lo_done, n - 1)
            sp.dma_start(raw[:, n % 2, :], w_d[n]).then_inc(raw_full[n % 2], 16)
            for i in range(KD // 2):
                sp.wait_ge(fin_ready, 2 * i + 2)
                sp.dma_start(out_d[:, 2 * i:2 * i + 2, :], outT[:, 2 * i:2 * i + 2, :]).then_inc(stored, 16)
            sp.wait_ge(stored, 16 * (KD // 2))

        @block.gpsimd
        def _(pool):
            pool.dma_start(pos_a[:], pos_d).then_inc(pos_in, 16)
            pool.wait_ge(sq_done, KD)
            pool.wait_ge(xl_done, KD)
            pool.dma_start(dist[:], mask_d).then_inc(mask_in, 16)
            nc.gpsimd.memset(s_sb[:, 0, 2 * P:3 * P], -3e38).then_inc(pad_set, 1)
            nc.gpsimd.memset(s_sb[:, 3, 2 * P:3 * P], -3e38).then_inc(pad_set, 1)
            pool.wait_ge(tile_read, T_A)
            with pool.Fori(0, 4) as J:
                pool.wait_ge(pv_full, 1 + J * 4)
                nc.gpsimd.tensor_copy(vc[:].rearrange("p a b c -> p a (b c)"),
                                      va[:, :, bass.ds(J, 1), :, :].rearrange("p a g b c -> p a (g b c)")).then_inc(vc_ready, 1)
                for jj in range(2):
                    for i in range(4):
                        pool.wait_ge(tile_read, J * 10 + (T_A + 5 * jj + 1 + i + 1))
                        pool.dma_start(gates_d[bass.ds(J * 8 + 4 * jj + i, 1)].rearrange("a p k -> p (a k)"),
                                       gbuf[:, i % 2, :]).then_inc(gate_out[i % 2], 16)
            pool.wait_ge(gate_out[0], 16 * 16)
            pool.wait_ge(gate_out[1], 16 * 16)
            pool.wait_ge(pv_full, 1 + A_HEADS)
            pool.dma_start(pos_i[:], pos_d[:, 0:S]).then_inc(pos_in, 16)
            pool.wait_ge(tile_full, T_B)
            for t in (q_h, q_l, k_h, k_l):
                for e in (1, 3):
                    nc.gpsimd.memset(t[0:32, e, :].bitcast(F32), 0.0).then_inc(zero_set, 1)

            def rope_moves(g, pairs):
                pool.wait_ge(r_lo, g + 1)
                pool.wait_ge(r_hi, g + 1)
                for i in pairs:
                    if g > 0:
                        pool.wait_ge(s_full, 1 + 4 * A_HEADS + 16 * (g - 1) + 8 * (i + 1))
                    for e in (2 * i, 2 * i + 1):
                        to = HALF if e % 2 == 0 else 32
                        for src, dst in ((rope_h, q_h), (rope_l, q_l)):
                            pool.dma_start(dst[to:to + 32, e, :], src[32 * e:32 * e + 32, :]).then_inc(r_moved[i], 16)
            def normalise_half(h):
                pool.wait_ge(a_den, 2 * A_HEADS + h + 1)
                for qb in range(2, QB):
                    nc.gpsimd.tensor_scalar(pB[h % 2][:, qb, :], pB[h % 2][:, qb, :], small[:, 24 + qb:25 + qb], None,
                                            ALU.mult).then_inc(p_ready2, 1)

            def block_lo(n, width):
                pool.wait_ge(hi_done, n + 1)
                pool.wait_ge(lo_done, n)
                nc.gpsimd.tensor_tensor(wsp[:, n % 2, 1, 0:width], raw[:, n % 2, 0:width],
                                        wsp[:, n % 2, 0, 0:width].bitcast(F32), ALU.subtract).then_inc(lo_done, 1)

            rope_moves(0, (0, 1))
            normalise_half(0)
            for g in range(GROUPS):
                for e in range(4):
                    if 4 * g + e + 1 < B_HEADS:
                        normalise_half(4 * g + e + 1)
                    if e == 0:
                        block_lo(N_B + 2 * g + 3, 1024 if g < GROUPS - 1 else BLK)
                    if g < GROUPS - 1:
                        if e == 1:
                            rope_moves(g + 1, (0,))
                        if e == 2:
                            rope_moves(g + 1, (1,))
                        if e == 3:
                            block_lo(N_B + 2 * g + 4, BLK)

            def gate_loads(p):
                for b in range(2):
                    if not (isinstance(p, int) and p == 0):
                        pool.wait_ge(gate_sig, p * 2 + b - 1)
                    pool.dma_start(gl[:, b], gates_d[bass.ds(p * 2 + 16 * b, 2)].rearrange("m p s -> p m s")).then_inc(
                        gate_in[b], 16)
            for i in range(2):
                pool.wait_ge(r_moved[i], 64 * GROUPS)
            gate_loads(0)
            with pool.Fori(1, 8) as p:
                gate_loads(p)
            pool.wait_ge(merged, 16)
            pool.wait_ge(mg_lo, 1 + 16)
            with pool.Fori(0, 8) as p:
                pool.wait_ge(tile_read, p * 2 + T_OUT)
                pool.dma_start(xin[:], xT_d[:, bass.ds(p * 2, 2), :]).then_inc(xin_in, 16)

        @block.tensor
        def _(pe):
            for s in (pv_full, s_full, t_full):
                pe.sem_inc(s, 1)

            def split_ready(n):
                pe.wait_ge(hi_done, n + 1)
                pe.wait_ge(lo_done, n + 1)

            def mm3(out, w, sl, xh, xl, start, stop):
                wh, wl = wsp[:, sl, 0, w], wsp[:, sl, 1, w]
                nc.tensor.matmul(out, wh, xh, start=start, stop=False)
                nc.tensor.matmul(out, wh, xl, start=False, stop=False)
                return nc.tensor.matmul(out, wl, xh, start=False, stop=stop)

            def tile(b, sl, k0=0, k1=KD, xh=xg_h, xl=xg_l, kn=KD, off=0, width=P):
                for k in range(k0, k1):
                    c = off + width * k
                    last = mm3(bank[:, b, :], slice(c, c + P), sl, xh[:, k, :], xl[:, k, :], k == 0, k == kn - 1)
                return last

            pe.wait_ge(tab_in, 16)
            split_ready(0)
            for k in range(KD):
                pe.wait_ge(xh_done, k + 1)
                pe.wait_ge(xl_done, k + 1)
                last = mm3(bank[:, 0, :], slice(P * k, P * k + P), 0, xg_h[:, k, :], xg_l[:, k, :], k == 0, k == KD - 1)
            last.then_inc(tile_full, 1)
            split_ready(1)
            tile(1, 1).then_inc(tile_full, 1)
            for b in range(2):
                split_ready(2 + b)
                for tt in range(QB):
                    out = bank[:, 2 + tt, 0:256]
                    tok = slice(P * tt, P * tt + P)
                    for k in range(8):
                        wh, wl = (wsp[:, b, i, 256 * k:256 * k + 256] for i in range(2))
                        xh, xl = xg_h[:, 8 * b + k, tok], xg_l[:, 8 * b + k, tok]
                        nc.tensor.matmul(out, xh, wh, start=(b == 0 and k == 0), stop=False)
                        nc.tensor.matmul(out, xh, wl, start=False, stop=False)
                        last = nc.tensor.matmul(out, xl, wh, start=False, stop=(b == 1 and k == 7))
                    if b == 1:
                        last.then_inc(tile_full, 1)
                if b == 0:
                    last.then_inc(v_half, 1)
                    pe.wait_ge(sq_added, KD)
                    nc.tensor.matmul(bank[:, 7, :], ones, tmp[:, 0, :], start=True, stop=True).then_inc(stat_full, 1)
            pe.wait_ge(rstd_done, 1)
            for tt in range(QB):
                last = nc.tensor.matmul(bank[:, 7, tt:tt + 1], rstd[0:1, P * tt:P * tt + P], tab[0:1, C_ONES:C_ONES + 1],
                                        start=True, stop=True)
            last.then_inc(col_full, 1)

            def a_scores(J, jj, e):
                h = 2 * jj + e
                for qb in A_ORDER:
                    k0, k1 = key_range(qb)
                    b, c = A_BANK[qb]
                    out = bank[:, b, c:c + k1 - k0]
                    lhs = qs[:, e, P * qb:P * qb + P]
                    if qb == 0:
                        pe.wait_ge(q_ready, J * 4 + 2 * jj + 2)
                        pe.wait_ge(s_read, 1 + J * 16 + 4 * h)
                    nc.tensor.matmul(out, lhs, kd_h[:, bass.ds(J, 1), k0:k1].rearrange("p a k -> p (a k)"), start=True, stop=False)
                    nc.tensor.matmul(out, lhs, kd_l[:, bass.ds(J, 1), k0:k1].rearrange("p a k -> p (a k)"),
                                     start=False, stop=True).then_inc(s_full, 1)

            def a_turn(J, h, kbs):
                for kb in kbs:
                    if kb == 0:
                        pe.wait_ge(p_ready, J * 16 + 4 * h + 4)
                    pe.wait_ge(pt_lo, 1 + J * 16 + max(4 * h + kb - 1, 0))
                    q0, q1 = max(0, kb - 1), min(QB, kb + 2)
                    for qb in range(q0, q1):
                        c = P * kb - key_range(qb)[0]
                        last = nc.tensor.transpose(bank[:, 4 + kb % 2, P * (qb - q0):P * (qb - q0) + P],
                                                   pA[:, qb, c:c + P], ident)
                    last.then_inc(t_full, 1)

            def a_values(J, h, kbs):
                for kb in kbs:
                    if kb == 0:
                        pe.wait_ge(vc_ready, J + 1)
                        pe.wait_ge(o_done, 1 + J * 4 + h)
                    pe.wait_ge(pt_lo, 1 + J * 16 + 4 * h + kb + 1)
                    q0, q1 = key_range(kb)
                    n = q1 - q0
                    nc.tensor.matmul(bank[:, 6, q0:q1], vc[:, kb].rearrange("p a d -> p (a d)"), pTA_h[:, kb, 0:n],
                                     start=(kb == 0), stop=False, skip_group_check=True)
                    last = nc.tensor.matmul(bank[0:HALF, 6, q0:q1], vc[:, kb, 0, :], pTA_l[:, kb, 0:n],
                                            start=False, stop=(kb == QB - 1), skip_group_check=True)
                if kbs[-1] == QB - 1:
                    last.then_inc(pv_full, 1)

            pe.wait_ge(kv_hi, 3 * A_KV)
            with pe.Fori(0, 4) as J:
                for jj in range(2):
                    h0, h1 = 2 * jj, 2 * jj + 1

                    def piece(i, k0, k1):
                        b, sl = (3, 7)[(5 * jj + i) % 2], (5 * jj + i) % 2
                        if k0 == 0:
                            split_ready(J * 10 + (N_A + 5 * jj + i))
                            pe.wait_ge(tile_read, J * 10 + (T_A + 5 * jj + i - 1))
                        last = tile(b, sl, k0, k1)
                        if k1 == KD:
                            last.then_inc(tile_full, 1)
                    piece(0, 0, KD)
                    piece(1, 0, KD)
                    a_scores(J, jj, 0)
                    piece(2, 0, KD)
                    a_turn(J, h0, (0, 1))
                    piece(3, 0, 8)
                    a_values(J, h0, (0, 1))
                    a_turn(J, h0, (2, 3))
                    a_scores(J, jj, 1)
                    piece(3, 8, KD)
                    a_values(J, h0, (2, 3))
                    piece(4, 0, 8)
                    a_turn(J, h1, (0, 1))
                    piece(4, 8, 11)
                    a_values(J, h1, (0, 1))
                    a_turn(J, h1, (2, 3))
                    piece(4, 11, 14)
                    a_values(J, h1, (2, 3))
                    piece(4, 14, KD)

            pe.wait_ge(s_read, 1 + 4 * A_HEADS)
            pe.wait_ge(pt_lo, 1 + 4 * A_HEADS)
            pe.wait_ge(tile_read, T_A + 39)
            for m in range(KQ + KKV):
                split_ready(N_LAT + m)
                if m == 3:
                    pe.wait_ge(tile_read, T_LAT)
                tile(m, (N_LAT + m) % 2).then_inc(tile_full, 1)
                if m == KQ:
                    pe.wait_ge(sq_added, KD + KQ)
                    nc.tensor.matmul(bank[:, 7, :], ones, sumsq[:], start=True, stop=True).then_inc(stat_full, 1)
            split_ready(N_LAT + 6)
            pe.wait_ge(o_done, 1 + A_HEADS)
            for k in range(KD):
                last = mm3(bank[0:ROPE, 6, :], slice(ROPE * k, ROPE * k + ROPE), 0, xg_h[:, k, :], xg_l[:, k, :],
                           k == 0, k == KD - 1)
            last.then_inc(tile_full, 1)
            pe.wait_ge(sq_added, KD + KQ + KKV)
            pe.wait_ge(stat_read, 2)
            nc.tensor.matmul(bank[:, 7, :], ones, sumsq[:], start=True, stop=True).then_inc(stat_full, 1)

            def b_project(kind, g):
                n, b = place(kind, g)
                first = isinstance(g, int)
                if kind == "q0":
                    split_ready(2 * g + N_B)
                if kind == "k0":
                    split_ready(2 * g + N_B + 1)
                if first:
                    pe.wait_ge(lat_lo, KQ if kind[0] in "qr" else KQ + KKV)
                else:
                    pe.wait_ge(tile_read, 7 * g + (T_B + n - 1))
                if kind[0] in "qr":
                    part = ("q0", "q1", "r").index(kind)
                    last = tile(b, N_B % 2, 0, KQ, cq_h, cq_l, KQ, P * part, 3 * P)
                elif kind[0] == "k":
                    last = tile(b, (N_B + 1) % 2, 0, KKV, ckv_h, ckv_l, KKV, P * int(kind[1]), 2 * P)
                else:
                    for tt in range(QB):
                        tok = slice(P * tt, P * tt + P)
                        for k in range(KKV):
                            c = 512 + 256 * k + P * int(kind[1])
                            wh, wl = (wsp[:, (N_B + 1) % 2, v, c:c + P] for v in range(2))
                            nc.tensor.matmul(bank[:, b, tok], ckv_h[:, k, tok], wh, start=(k == 0), stop=False)
                            nc.tensor.matmul(bank[:, b, tok], ckv_h[:, k, tok], wl, start=False, stop=False)
                            last = nc.tensor.matmul(bank[:, b, tok], ckv_l[:, k, tok], wh, start=False, stop=(k == KKV - 1))
                last.then_inc(tile_full, 1)

            def b_scores(g, e):
                first = isinstance(g, int) and g == 0
                rows = slice(0, NOPE + ROPE) if e % 2 == 0 else slice(0, P)
                if e % 2 == 0:
                    pe.wait_ge(b_lo, 4 * g + (2 * (e // 2) + 2))
                    pe.wait_ge(tile_read, 7 * g + (T_B + place("k0k1"[e:e + 2], g)[0]))
                    pe.wait_ge(r_moved[e // 2], 64 * g + 64)
                for qb in range(QB):
                    if not (first and e == 0):
                        pe.wait_ge(a_exp, 16 * g + (1 + 5 * A_HEADS + 4 * e - 4 + qb + 1))
                    q = slice(P * qb, P * qb + P)
                    nc.tensor.matmul(bank[:, qb, :], q_h[rows, e, q], k_h[rows, e, :], start=True, stop=False)
                    nc.tensor.matmul(bank[:, qb, :], q_h[rows, e, q], k_l[rows, e, :], start=False, stop=False)
                    nc.tensor.matmul(bank[:, qb, :], q_l[rows, e, q], k_h[rows, e, :], start=False, stop=True).then_inc(
                        s_full, 1)

            def b_turn(g, e, kbs):
                for kb in kbs:
                    if kb == 0:
                        pe.wait_ge(p_ready, 8 * g + (4 * A_HEADS + 2 * e + 2))
                        pe.wait_ge(p_ready2, 8 * g + (2 * e + 2))
                    pe.wait_ge(pt_lo, 1 + 16 * g + (4 * A_HEADS + 4 * e + kb - 1))
                    for qb in range(QB):
                        last = nc.tensor.transpose(bank[:, 4 + kb % 2, P * qb:P * qb + P], pB[e % 2][:, qb, P * kb:P * kb + P], ident)
                    last.then_inc(t_full, 1)

            def b_values(g, e):
                pe.wait_ge(o_done, 4 * g + (1 + A_HEADS + e))
                if e % 2 == 0:
                    pe.wait_ge(tile_read, 7 * g + (T_B + place("v0v1"[e:e + 2], g)[0]))
                for kb in range(QB):
                    pe.wait_ge(pt_lo, 16 * g + (1 + 4 * A_HEADS + 4 * e + kb + 1))
                    v = vb[:, e // 2, kb, e % 2]
                    nc.tensor.matmul(bank[:, 6, :], v.rearrange("p a d -> p (a d)"), pTB_h[:, kb, :],
                                     start=(kb == 0), stop=False, skip_group_check=True)
                    last = nc.tensor.matmul(bank[0:HALF, 6, :], v[:, 0, :], pTB_l[:, kb, :],
                                            start=False, stop=(kb == QB - 1), skip_group_check=True)
                last.then_inc(pv_full, 1)

            def b_group(g, more):
                for e in range(4):
                    if e < 3:
                        b_scores(g, e + 1)
                    elif more:
                        b_scores(g + 1, 0)
                    if e > 0:
                        b_values(g, e - 1)
                    b_turn(g, e, (0, 1))
                    if more:
                        b_project(FILL_1[e], g + 1)
                    b_turn(g, e, (2, 3))
                    if more and FILL_2[e]:
                        b_project(FILL_2[e], g + 1)
                b_values(g, 3)
                if more:
                    b_project("v1", g + 1)

            pe.wait_ge(stat_read, 3)
            pe.wait_ge(tile_read, T_B)
            for kind in FIRST_ORDER:
                b_project(kind, 0)
            pe.wait_ge(zero_set, 8)
            pe.wait_ge(kr_spread, 8)
            pe.wait_ge(tile_read, T_B + 7)
            b_scores(0, 0)
            with pe.Fori(0, GROUPS - 1) as g:
                b_group(g, True)
            b_group(GROUPS - 1, False)

            def branch_pair(p, first):
                for b, (oh, ol) in enumerate(((oA_h, oA_l), (oB_h, oB_l))):
                    split_ready(2 * p + N_BR + b)
                    for i in range(2):
                        pe.wait_ge(tile_read, 4 * p + (T_BR + 2 * b + i - 3))
                        for k in range(8):
                            if first and i == 0:
                                pe.wait_ge(o_lo, 8 * b + k + 1)
                            c = 256 * k + P * i
                            last = mm3(bank[:, 2 * b + i, :], slice(c, c + P), (N_BR + b) % 2, oh[:, k, :], ol[:, k, :],
                                       k == 0, k == 7)
                        last.then_inc(tile_full, 1)

            pe.wait_ge(tile_read, T_BR)
            pe.wait_ge(a_exp, 1 + 5 * A_HEADS + 4 * B_HEADS)
            branch_pair(0, True)
            with pe.Fori(1, 8) as p:
                branch_pair(p, False)

            def out_pair(p, first):
                for i in range(2):
                    split_ready(2 * p + N_OUT + i)
                    pe.wait_ge(tile_read, 2 * p + (T_OUT + i - 1))
                    for k in range(KD):
                        if first and i == 0:
                            pe.wait_ge(mg_lo, 1 + k + 1)
                        last = mm3(bank[:, 4 + i, :], slice(P * k, P * k + P), (N_OUT + i) % 2, mg_h[:, k, :], mg_l[:, k, :],
                                   k == 0, k == KD - 1)
                    last.then_inc(tile_full, 1)

            out_pair(0, True)
            with pe.Fori(1, 8) as p:
                out_pair(p, False)

            def up_pair(c, q, first):
                for i in range(2):
                    split_ready(16 * c + 2 * q + (N_MLP + i))
                    pe.wait_ge(tile_read, 24 * c + 2 * q + (T_MLP + i - 1))
                    for k in range(KD):
                        if first and i == 0:
                            pe.wait_ge(h2_lo, k + 1)
                        last = mm3(bank[:, i, :], slice(P * k, P * k + P), (N_MLP + i) % 2, h2_h[:, k, :], h2_l[:, k, :],
                                   k == 0, k == KD - 1)
                    last.then_inc(tile_full, 1)
                    if first and i == 0:
                        nc.tensor.matmul(bank[:, 7, :], ones, ssum[:], start=True, stop=True).then_inc(stat_full, 1)

            def down_pair(c, q):
                for i in range(4):
                    b, j = i // 2, i % 2
                    if j == 0:
                        split_ready(16 * c + 2 * q + (N_MLP + CH + b))
                    pe.wait_ge(tile_read, 24 * c + 4 * q + (T_MLP + CH + i - 3))
                    for k in range(CH):
                        if i == 0 and k in (0, CH - 1):
                            pe.wait_ge(u_lo, CH * c + (CH - 1 if k == 0 else CH))
                        col = 256 * k + P * j
                        last = mm3(bank[:, 2 + i, :], slice(col, col + P), (N_MLP + b) % 2, u_h[:, k, :], u_l[:, k, :],
                                   k == 0, k == CH - 1)
                    last.then_inc(tile_full, 1)

            up_pair(0, 0, True)
            with pe.Fori(1, 4) as q:
                up_pair(0, q, False)
            with pe.Fori(0, 4) as q:
                down_pair(0, q)
            with pe.Fori(1, CHUNKS) as c:
                with pe.Fori(0, 4) as q:
                    up_pair(c, q, False)
                with pe.Fori(0, 4) as q:
                    down_pair(c, q)
            pe.wait_ge(sq_added, KD + KQ + KKV + 2 * KD)
            nc.tensor.matmul(bank[:, 7, :], ones, ssum[:], start=True, stop=True).then_inc(stat_full, 1)

        @block.scalar
        def _(act):
            def hi(n, sl, hlf, done, width=BLK):
                act.wait_ge(raw_full[sl], hlf)
                if done is not None:
                    act.wait_ge(tile_full, done)
                nc.scalar.copy(wsp[:, sl, 0, 0:width], raw[:, sl, 0:width]).then_inc(hi_done, 1)

            def hi_at(base_n, per, i, done, width=BLK):
                n = base_n + i
                hi(None, n % 2, per * 8 + 16 * (n // 2 + 1), done, width)

            act.sem_inc(a_exp, 1)
            act.wait_ge(tab_in, 16)
            hi(0, 0, 16, None)
            for k in range(KD):
                act.wait_ge(x_in[k // 4], 16)
                nc.scalar.activation(xg_h[:, k, :], xT[:, k, :], ACT.Copy,
                                     scale=tab[:, C_GATTN + k:C_GATTN + k + 1]).then_inc(xh_done, 1)
                if k == 7:
                    hi(1, 1, 16, None)
            for k in range(KD):
                if k >= 2:
                    act.wait_ge(sq_added, k - 1)
                nc.scalar.square(gbuf[:, k % 2, :], xT[:, k, :]).then_inc(sq_done, 1)
                if k == 7:
                    hi(2, 0, 32, 1)
            hi(3, 1, 32, 2)

            def sqrt_of(i):
                act.wait_ge(stat_read, i)
                nc.scalar.sqrt(tmp[:, 1, :], tmp[:, 0, :]).then_inc(sqrt_done, 1)
            sqrt_of(1)
            for g in range(A_KV):
                r = slice(HALF * (g % 2), HALF * (g % 2) + HALF)
                o = slice(HALF * (1 - g % 2), HALF * (1 - g % 2) + HALF)
                act.wait_ge(tile_read, g // 2 + 1)
                nc.scalar.copy(kd_h[r, g, :], gbuf[r, g // 2, :]).then_inc(kv_hi, 1)
            for g in range(A_KV):
                r = slice(HALF * (g % 2), HALF * (g % 2) + HALF)
                o = slice(HALF * (1 - g % 2), HALF * (1 - g % 2) + HALF)
                act.wait_ge(kv_ready, g + 1)
                act.wait_ge(kv_hi, g + 1)
                nc.scalar.copy(kd_h[o, g, :], kd_h[r, g, :].bitcast(F32)).then_inc(kv_hi, 1)
                nc.scalar.copy(kd_l[o, g, :], kd_l[r, g, :].bitcast(F32)).then_inc(kv_hi, 1)
            act.wait_ge(v_half, 1)
            hi(4, 0, 48, None)
            act.wait_ge(col_ready, 1)
            for tt in range(QB):
                act.wait_ge(tile_full, 3 + tt)
                nc.scalar.activation(va[:, tt, :, 0, :], bank[:, 2 + tt, 0:256].rearrange("p (g d) -> p g d", g=A_KV), ACT.Copy,
                                     scale=small[:, tt:tt + 1]).then_inc(v_hi, 1)
            hi(5, 1, 48, T_A)

            def softmax_a(J, h):
                act.wait_ge(a_shift, J * 4 + h + 1)
                act.wait_ge(t_full, 1 + J * 16 + 4 * h)
                for qb in range(QB):
                    k0, k1 = key_range(qb)
                    nc.scalar.activation(pA[:, qb, 0:k1 - k0], s_sb[:, qb, 0:k1 - k0], ACT.Exp, scale=A_SCALE,
                                         bias=small[:, 8 + qb:9 + qb], accum_out=small[:, 12 + qb:13 + qb]).then_inc(a_exp, 1)
                nc.scalar.activation(small[:, 16:20], small[:, 8:12], ACT.Exp,
                                     bias=tab[:, bass.ds(J * 4 + (C_SINK + h), 1)]).then_inc(a_exp, 1)

            def turned_hi(base, h, kbs, src_n, dst):
                for kb in kbs:
                    act.wait_ge(t_full, 1 + base + (4 * h + kb + 1))
                    n = src_n(kb)
                    nc.scalar.copy(dst[:, kb, 0:n], bank[:, 4 + kb % 2, 0:n]).then_inc(pt_hi, 1)

            def a_n(kb):
                return key_range(kb)[1] - key_range(kb)[0]

            def turned_a(J, h, kbs):
                if kbs[0] == 0:
                    act.wait_ge(pv_full, 1 + J * 4 + h)
                turned_hi(J * 16, h, kbs, a_n, pTA_h)

            def half_out(count):
                act.wait_ge(pv_full, 1 + count + 1)
                act.wait_ge(o_done, 1 + count)
                nc.scalar.copy(otmp[:], bank[HALF:P, 6, :]).then_inc(pv_half, 1)

            with act.Fori(0, 4) as J:
                for jj in range(2):
                    def next_hi(i):
                        hi_at(N_A, J * 10, 5 * jj + i + 2, J * 10 + (T_A + 5 * jj + i + 1))
                    h0, h1 = 2 * jj, 2 * jj + 1
                    act.wait_ge(tile_read, J * 10 + (T_A + 5 * jj + 1))
                    act.wait_ge(s_full, 1 + J * 16 + 8 * jj)
                    nc.scalar.copy(qs[0:HALF, 0, :], qf[0:HALF, :]).then_inc(q_hi, 1)
                    nc.scalar.copy(qs[HALF:P, 1, :], qf[HALF:P, :]).then_inc(q_hi, 1)
                    next_hi(0)
                    next_hi(1)
                    softmax_a(J, h0)
                    next_hi(2)
                    turned_a(J, h0, (0, 1))
                    turned_a(J, h0, (2, 3))
                    softmax_a(J, h1)
                    next_hi(3)
                    half_out(J * 4 + h0)
                    turned_a(J, h1, (0, 1))
                    turned_a(J, h1, (2, 3))
                    half_out(J * 4 + h1)
                    next_hi(4)

            for m in range(KQ + KKV):
                act.wait_ge(tile_read, T_LAT + m + 1)
                if m >= 2:
                    act.wait_ge(sq_added, KD + m - 1)
                src = cqf[:, m, :] if m < KQ else ckvf[:, m - KQ, :]
                nc.scalar.square(sqL[:, m % 2, :], src).then_inc(sq_done, 1)
                hi_at(N_LAT, 0, m + 2, T_LAT + m + 1)
                if m == KQ:
                    sqrt_of(2)
                    for k in range(KQ):
                        act.wait_ge(lat_norm, k + 1)
                        nc.scalar.activation(cq_h[:, k, :], cqf[:, k, :], ACT.Copy,
                                             scale=tab[:, C_GQ + k:C_GQ + k + 1]).then_inc(lat_hi, 1)
            act.wait_ge(ang_ready, 1)
            nc.scalar.activation(t_hi[:], ang[:], ACT.Sin, scale=0.5).then_inc(sin_done, 1)
            nc.scalar.activation(t_lo[:], turns[:], ACT.Sin).then_inc(sin_done, 1)
            hi_at(N_LAT, 0, 8, T_LAT + 7)
            act.wait_ge(kr_ready, 1)
            act.wait_ge(gate_out[0], 16 * 16)
            act.wait_ge(gate_out[1], 16 * 16)
            nc.scalar.copy(rope_h[0:ROPE, :], rope_a[0:ROPE, :]).then_inc(kr_split, 1)
            act.wait_ge(kr_split, 2)
            for e in range(4):
                to = HALF if e % 2 == 0 else 32
                nc.scalar.copy(k_h[to:to + ROPE, e, :], rope_h[0:ROPE, :].bitcast(F32)).then_inc(kr_spread, 1)
                nc.scalar.copy(k_l[to:to + ROPE, e, :], rope_l[0:ROPE, :].bitcast(F32)).then_inc(kr_spread, 1)
            sqrt_of(3)
            for k in range(KKV):
                act.wait_ge(lat_norm, KQ + k + 1)
                nc.scalar.activation(ckv_h[:, k, :], ckvf[:, k, :], ACT.Copy,
                                     scale=tab[:, C_GKV + k:C_GKV + k + 1]).then_inc(lat_hi, 1)

            def project_hi(kind, g):
                n, b = place(kind, g)
                act.wait_ge(tile_full, 7 * g + (T_B + n))
                i = int(kind[1])
                if kind[0] == "v":
                    if not isinstance(g, int):
                        act.wait_ge(pv_full, 4 * g + (1 + A_HEADS - 4 + 2 * i + 2))
                    nc.scalar.copy(vb[:, i, :, :, 0, :].rearrange("p t e d -> p (t e) d"),
                                   bank[:, b, :].rearrange("p (a d) -> p a d", d=HALF)).then_inc(v_hi, 1)
                    return
                if not isinstance(g, int):
                    act.wait_ge(s_full, 16 * g + (1 + 4 * A_HEADS - 16 + 8 * i + 8))
                for e in range(2):
                    r = slice(HALF * e, HALF * e + HALF)
                    nc.scalar.copy((q_h if kind[0] == "q" else k_h)[r, 2 * i + e, :], bank[r, b, :]).then_inc(b_hi, 1)

            def rope_hi(g):
                act.wait_ge(r_sum, g + 1)
                nc.scalar.copy(rope_h[:], rope_a[:]).then_inc(r_hi, 1)

            def softmax_b(g, e):
                act.wait_ge(a_shift, 4 * g + (A_HEADS + e + 1))
                act.wait_ge(t_full, 16 * g + (1 + 4 * A_HEADS + 4 * e - 4))
                for qb in range(QB):
                    nc.scalar.activation(pB[e % 2][:, qb, :], bank[:, qb, :], ACT.Exp, scale=B_SCALE,
                                         bias=small[:, 8 + qb:9 + qb], accum_out=small[:, 12 + qb:13 + qb]).then_inc(a_exp, 1)

            def turned_b(g, e, kbs):
                if kbs[0] == 0:
                    act.wait_ge(pv_full, 4 * g + (1 + A_HEADS + e))
                turned_hi(16 * g + 4 * A_HEADS, e, kbs, lambda kb: S, pTB_h)

            def b_group(g, more):
                for e in range(4):
                    if e > 0:
                        half_out(4 * g + (A_HEADS + e - 1))
                    turned_b(g, e, (0, 1))
                    if e < 3:
                        softmax_b(g, e + 1)
                    elif more:
                        softmax_b(g + 1, 0)
                    if more and FILL_1[e] != "r":
                        project_hi(FILL_1[e], g + 1)
                    turned_b(g, e, (2, 3))
                    if more and e == 1:
                        rope_hi(g + 1)
                    if more and FILL_2[e]:
                        project_hi(FILL_2[e], g + 1)
                    if e == 0:
                        hi_at(N_B, 2 * g, 3, 7 * g + (T_B + 7), 1024 if more else BLK)
                    if more and e == 3:
                        hi_at(N_B, 2 * g, 4, 7 * g + (T_B + 7 + 4))
                half_out(4 * g + (A_HEADS + 3))
                if more:
                    project_hi("v1", g + 1)

            act.wait_ge(zero_set, 8)
            for kind in FIRST_ORDER:
                if kind == "r":
                    rope_hi(0)
                    hi_at(N_B, 0, 2, T_B + 3, 1536)
                else:
                    project_hi(kind, 0)
            softmax_b(0, 0)
            with act.Fori(0, GROUPS - 1) as g:
                b_group(g, True)
            b_group(GROUPS - 1, False)

            for k in range(8):
                act.wait_ge(o_done, 1 + A_HEADS) if k == 0 else None
                nc.scalar.copy(oA_h[:, k, :], oA[:, k, :]).then_inc(o_hi, 1)
            for k in range(8):
                act.wait_ge(o_done, 1 + A_HEADS + 2 * k + 2)
                nc.scalar.copy(oB_h[:, k, :], oB[:, k, :]).then_inc(o_hi, 1)

            def sig(p, b):
                act.wait_ge(gate_in[b], 16 * p + 16)
                act.wait_ge(tile_read, 4 * p + (T_BR - 2 + 2 * b))
                nc.scalar.activation(sg[:, b], gl[:, b], ACT.Sigmoid).then_inc(gate_sig, 1)

            act.wait_ge(o_lo, 8)
            with act.Fori(0, 8) as p:
                sig(p, 0)
                sig(p, 1)
                hi_at(N_BR, 2 * p, 2, 4 * p + (T_BR + 2))
                for i in range(2):
                    act.wait_ge(merged, 2 * p + (i + 1))
                    nc.scalar.copy(mg_h[:, bass.ds(2 * p + i, 1), :], tmp[:, i:i + 1, :]).then_inc(mg_hi, 1)
                hi_at(N_BR, 2 * p, 3, 4 * p + (T_BR + 4))

            with act.Fori(0, 8) as p:
                for i in range(2):
                    act.wait_ge(tile_read, 2 * p + (T_OUT + i + 1))
                    act.wait_ge(sq_added, 2 * p + (KD + KQ + KKV + i - 1))
                    nc.scalar.activation(h2_h[:, bass.ds(2 * p + i, 1), :].rearrange("p a s -> p (a s)"),
                                         x2[:, bass.ds(2 * p + i, 1), :].rearrange("p a s -> p (a s)"), ACT.Copy,
                                         scale=tab[:, bass.ds(2 * p + (C_GMLP + i), 1)]).then_inc(h2_hi, 1)
                    nc.scalar.square(sq[:, i, :].rearrange("p (a s) -> p a s", a=1), x2[:, bass.ds(2 * p + i, 1), :]).then_inc(sq_done, 1)
                    hi_at(N_OUT, 2 * p, 2 + i, 2 * p + (T_OUT + i + 1))

            def up(c, q):
                for i in range(2):
                    act.wait_ge(u_sq, CH * c + 2 * q + (i + 1))
                    nc.scalar.copy(u_h[:, bass.ds(2 * q + i, 1), :], uu[:].rearrange("p (a s) -> p a s", a=1)).then_inc(u_hi, 1)
                    hi_at(N_MLP, 16 * c + 2 * q, 2 + i, 24 * c + 2 * q + (T_MLP + i + 1))

            def down(c, q, last=False):
                for b in range(2):
                    if last:
                        for j in range(2):
                            m = 4 * q + 2 * b + j
                            act.wait_ge(tile_read, T_END - KD + m + 1)
                            act.wait_ge(sq_added, KD + KQ + KKV + KD + m - 1)
                            nc.scalar.square(sq[:, j, :], x2[:, m, :]).then_inc(sq_done, 1)
                            nc.scalar.activation(outT[:, m, :], x2[:, m, :], ACT.Copy,
                                                 scale=tab[:, C_GFIN + m:C_GFIN + m + 1]).then_inc(fin_gain, 1)
                    if not (last and q == 3):
                        hi_at(N_MLP + CH, 16 * c + 2 * q, 2 + b, 24 * c + 4 * q + (T_MLP + CH + 2 * b + 2))

            sqrt_of(4)
            with act.Fori(0, CHUNKS - 1) as c:
                with act.Fori(0, 4) as q:
                    up(c, q)
                with act.Fori(0, 4) as q:
                    down(c, q)
            with act.Fori(0, 4) as q:
                up(CHUNKS - 1, q)
            for q in range(4):
                down(CHUNKS - 1, q, True)
            sqrt_of(5)

        @block.vector
        def _(dve):
            V = nc.vector
            links = [0]

            def link(ins):
                links[0] += 1
                ins.then_inc(chain, 1)
                dve.wait_ge(chain, links[0])

            def lo_at(base_n, per, i, width=BLK):
                n = base_n + i
                dve.wait_ge(hi_done, per + (n + 1))
                dve.wait_ge(lo_done, per + n) if n > 0 else None
                V.tensor_tensor(wsp[:, n % 2, 1, 0:width], raw[:, n % 2, 0:width], wsp[:, n % 2, 0, 0:width].bitcast(F32),
                                ALU.subtract).then_inc(lo_done, 1)

            def rms(i, count, dst):
                dve.wait_ge(stat_full, i)
                V.tensor_scalar(tmp[:, 0, :], bank[:, 7, :], 1.0 / count, EPS, ALU.mult, ALU.add).then_inc(stat_read, 1)
                dve.wait_ge(sqrt_done, i)
                link(V.reciprocal(dst, tmp[:, 1, :]))
                link(V.tensor_tensor(tmp[:, 1, :], dst, dst, ALU.mult))
                dve.wait_ge(stat_read, i)
                link(V.tensor_tensor(tmp[:, 1, :], tmp[:, 1, :], tmp[:, 0, :], ALU.mult))
                link(V.tensor_scalar(tmp[:, 1, :], tmp[:, 1, :], -0.5, 1.5, ALU.mult, ALU.add))
                V.tensor_tensor(dst, dst, tmp[:, 1, :], ALU.mult).then_inc(rstd_done, 1)
                dve.wait_ge(rstd_done, i)

            def add_square(total, src, count, first):
                dve.wait_ge(sq_done, count)
                if first:
                    V.tensor_copy(total, src).then_inc(sq_added, 1)
                else:
                    dve.wait_ge(sq_added, count - 1)
                    V.tensor_tensor(total, total, src, ALU.add).then_inc(sq_added, 1)

            for s in (s_read, pt_lo, o_done, mg_lo):
                dve.sem_inc(s, 1)
            dve.wait_ge(tab_in, 16)
            lo_at(0, 0, 0)
            for k in range(KD):
                dve.wait_ge(xh_done, k + 1)
                V.scalar_tensor_tensor(xg_l[:, k, :], xT[:, k, :], tab[:, C_GATTN + k:C_GATTN + k + 1],
                                       xg_h[:, k, :].bitcast(F32), ALU.mult, ALU.subtract).then_inc(xl_done, 1)
                if k == 9:
                    lo_at(0, 0, 1)
            for k in range(KD):
                add_square(tmp[:, 0, :], gbuf[:, k % 2, :], k + 1, k == 0)
                if k == 9:
                    lo_at(0, 0, 2)
            dve.wait_ge(pos_in, 16)
            link(V.tensor_copy(small[:, 28:32], pos_a[:, S:S + QB]))
            V.tensor_scalar(small[:, 32:48], tab[:, C_SINK:C_SINK + A_HEADS], -1.0, None, ALU.mult).then_inc(neg_ready, 1)
            dve.wait_ge(mask_in, 16)
            for qb in range(QB):
                k0, k1 = key_range(qb)
                n = k1 - k0
                link(V.tensor_scalar(dist_t[:, 0:n], pos_a[:, k0:k1], small[:, 28 + qb:29 + qb], None, ALU.subtract))
                link(V.scalar_tensor_tensor(dist_t[:, 0:n], dist_t[:, 0:n], -1.0, dist_t[:, 0:n], ALU.mult, ALU.max))
                link(V.tensor_tensor(dist[:, qb, 0:n], dist[:, qb, 0:n], dist_t[:, 0:n], ALU.add))
            lo_at(0, 0, 3)
            rms(1, D, rstd[:])
            for i in range(2):
                dve.wait_ge(tile_full, i + 1)
                V.tensor_tensor(gbuf[:, i, :], bank[:, i, :], rstd[:], ALU.mult).then_inc(tile_read, 1)
            for g in range(A_KV):
                r = slice(HALF * (g % 2), HALF * (g % 2) + HALF)
                dve.wait_ge(kv_hi, g + 1)
                dve.wait_ge(tile_read, g // 2 + 1)
                V.tensor_tensor(kd_l[r, g, :], gbuf[r, g // 2, :], kd_h[r, g, :].bitcast(F32), ALU.subtract).then_inc(kv_ready, 1)
            lo_at(0, 0, 4)
            dve.wait_ge(col_full, 1)
            V.tensor_copy(small[:, 0:QB], bank[:, 7, 0:QB]).then_inc(col_ready, 1)
            dve.wait_ge(col_ready, 1)
            for tt in range(QB):
                dve.wait_ge(v_hi, tt + 1)
                V.scalar_tensor_tensor(va[:, tt, :, 1, :], bank[:, 2 + tt, 0:256].rearrange("p (g d) -> p g d", g=A_KV),
                                       small[:, tt:tt + 1], va[:, tt, :, 0, :].bitcast(F32), ALU.mult, ALU.subtract).then_inc(
                    tile_read, 1)
            lo_at(0, 0, 5)

            def gate_tile(J, jj, i):
                t = 5 * jj + i
                dve.wait_ge(tile_full, J * 10 + (T_A + t + 1))
                if jj or i > 2:
                    dve.wait_ge(gate_out[(i - 1) % 2], J * 64 + 16 * (2 * jj + (i - 1) // 2))
                V.tensor_tensor(gbuf[:, (i - 1) % 2, :], bank[:, (3, 7)[t % 2], :], rstd[:], ALU.mult).then_inc(tile_read, 1)

            def maximum(before, h):
                dve.wait_ge(s_read, 1 + before * 4 + (4 * h + 4))
                V.tensor_reduce(small[:, 4:8], s_sb[:], AX_X, ALU.max).then_inc(a_max, 1)
                dve.wait_ge(a_max, before + (h + 1))

            def biased(J, h):
                if h == 0:
                    dve.wait_ge(pad_set, 2)
                for n, qb in enumerate(A_ORDER):
                    dve.wait_ge(s_full, 1 + J * 16 + (4 * h + max(n + 1, 2)))
                    if n == 0:
                        dve.wait_ge(a_exp, 1 + J * 20 + 5 * h)
                    k0, k1 = key_range(qb)
                    b, c = A_BANK[qb]
                    V.scalar_tensor_tensor(s_sb[:, qb, 0:k1 - k0], dist[:, qb, 0:k1 - k0],
                                           tab[:, bass.ds(J * 4 + (C_SLOPE + h), 1)], bank[:, b, c:c + k1 - k0],
                                           ALU.mult, ALU.add).then_inc(s_read, 1)
                maximum(J * 4, h)
                V.tensor_scalar(small[:, 8:12], small[:, 4:8], -A_SCALE, small[:, bass.ds(J * 4 + (32 + h), 1)],
                                ALU.mult, ALU.min).then_inc(a_shift, 1)

            def normalise_a(J, h):
                dve.wait_ge(a_exp, 1 + J * 20 + (5 * h + 5))
                V.tensor_tensor(small[:, 20:24], small[:, 12:16], small[:, 16:20], ALU.add).then_inc(a_den, 1)
                dve.wait_ge(a_den, J * 8 + (2 * h + 1))
                V.reciprocal(small[:, 24:28], small[:, 20:24]).then_inc(a_den, 1)
                dve.wait_ge(a_den, J * 8 + (2 * h + 2))
                for qb in range(QB):
                    n = key_range(qb)[1] - key_range(qb)[0]
                    V.tensor_scalar(pA[:, qb, 0:n], pA[:, qb, 0:n], small[:, 24 + qb:25 + qb], None, ALU.mult).then_inc(p_ready, 1)

            def turned_lo(base, h, kbs, width, hi_t, lo_t):
                for kb in kbs:
                    dve.wait_ge(pt_hi, base + (4 * h + kb + 1))
                    n = width(kb)
                    V.tensor_tensor(lo_t[:, kb, 0:n], bank[:, 4 + kb % 2, 0:n], hi_t[:, kb, 0:n].bitcast(F32),
                                    ALU.subtract).then_inc(pt_lo, 1)

            def a_n(kb):
                return key_range(kb)[1] - key_range(kb)[0]

            def out_sum(dst, count, e):
                dve.wait_ge(pv_half, count + 1)
                V.tensor_tensor(dst, bank[0:HALF, 6, :], otmp[:], ALU.add).then_inc(o_done, 1)

            dve.wait_ge(neg_ready, 1)
            with dve.Fori(0, 4) as J:
                for jj in range(2):
                    h0, h1 = 2 * jj, 2 * jj + 1
                    dve.wait_ge(tile_full, J * 10 + (T_A + 5 * jj + 1))
                    V.tensor_tensor(qf[:], bank[:, (3, 7)[5 * jj % 2], :], rstd[:], ALU.mult).then_inc(tile_read, 1)
                    dve.wait_ge(q_hi, J * 4 + (2 * jj + 2))
                    dve.wait_ge(tile_read, J * 10 + (T_A + 5 * jj + 1))
                    V.tensor_tensor(qs[HALF:P, 0, :], qf[0:HALF, :], qs[0:HALF, 0, :].bitcast(F32), ALU.subtract).then_inc(q_ready, 1)
                    V.tensor_tensor(qs[0:HALF, 1, :], qf[HALF:P, :], qs[HALF:P, 1, :].bitcast(F32), ALU.subtract).then_inc(q_ready, 1)

                    def next_lo(i):
                        lo_at(N_A, J * 10, 5 * jj + i + 2)

                    def out_a(h):
                        out_sum(oA[HALF * (h % 2):HALF * (h % 2) + HALF, bass.ds(J * 2 + h // 2, 1), :].rearrange("p a s -> p (a s)"),
                                J * 4 + h, h)
                    next_lo(0)
                    gate_tile(J, jj, 1)
                    biased(J, h0)
                    next_lo(1)
                    normalise_a(J, h0)
                    gate_tile(J, jj, 2)
                    turned_lo(J * 16, h0, (0, 1), a_n, pTA_h, pTA_l)
                    next_lo(2)
                    turned_lo(J * 16, h0, (2, 3), a_n, pTA_h, pTA_l)
                    biased(J, h1)
                    gate_tile(J, jj, 3)
                    normalise_a(J, h1)
                    out_a(h0)
                    next_lo(3)
                    turned_lo(J * 16, h1, (0, 1), a_n, pTA_h, pTA_l)
                    turned_lo(J * 16, h1, (2, 3), a_n, pTA_h, pTA_l)
                    out_a(h1)
                    gate_tile(J, jj, 4)
                    next_lo(4)
                for b in range(2):
                    dve.wait_ge(gate_out[b], J * 64 + 64)

            def angles():
                magic = 1.5 * 2.0 ** 23
                dve.wait_ge(pos_in, 32)
                link(V.tensor_copy(posf[:], pos_i[:]))
                link(V.tensor_scalar(ang[:], posf[:], tab[:, C_INVF:C_INVF + 1], None, ALU.mult))
                link(V.tensor_scalar(turns[:], ang[:], 0.15915494309189535, magic, ALU.mult, ALU.add))
                link(V.tensor_scalar(turns[:], turns[:], magic, None, ALU.subtract))
                link(V.tensor_scalar(t_hi[:], turns[:], magic * 2048, None, ALU.add))
                link(V.tensor_scalar(t_hi[:], t_hi[:], magic * 2048, None, ALU.subtract))
                link(V.tensor_tensor(t_lo[:], turns[:], t_hi[:], ALU.subtract))
                for part in TWO_PI_PARTS:
                    for t in (t_hi, t_lo):
                        link(V.scalar_tensor_tensor(ang[:], t[:], -part, ang[:], ALU.mult, ALU.add))
                link(V.scalar_tensor_tensor(turns[:], ang[:], -1.0, ang[:], ALU.mult, ALU.max))
                V.tensor_scalar(turns[:], turns[:], -0.5, 1.5707963267948966, ALU.mult, ALU.add).then_inc(ang_ready, 1)

            for m in range(KQ + KKV):
                dve.wait_ge(tile_full, T_LAT + m + 1)
                dst = cqf[:, m, :] if m < KQ else ckvf[:, m - KQ, :]
                V.tensor_tensor(dst, bank[:, m, :], rstd[:], ALU.mult).then_inc(tile_read, 1)
                lo_at(N_LAT, 0, m + 2)
                if m == 1:
                    angles()
                if m == KQ:
                    rms(2, Q_LORA, lat_rstd[:])
                    for k in range(KQ):
                        V.tensor_tensor(cqf[:, k, :], cqf[:, k, :], lat_rstd[:], ALU.mult).then_inc(lat_norm, 1)
                    for k in range(KQ):
                        dve.wait_ge(lat_hi, k + 1)
                        V.scalar_tensor_tensor(cq_l[:, k, :], cqf[:, k, :], tab[:, C_GQ + k:C_GQ + k + 1],
                                               cq_h[:, k, :].bitcast(F32), ALU.mult, ALU.subtract).then_inc(lat_lo, 1)
                add_square(sumsq[:], sqL[:, m % 2, :], KD + m + 1, m in (0, KQ))
            dve.wait_ge(sin_done, 2)
            link(V.tensor_tensor(cosb[:], t_hi[:], t_hi[:], ALU.mult))
            link(V.tensor_scalar(cosb[:], cosb[:], -2.0, 1.0, ALU.mult, ALU.add))
            link(V.tensor_tensor(sinb[:], t_hi[:], t_lo[:], ALU.mult))
            link(V.tensor_scalar(sinb[:], sinb[:], tab[:, C_SIGN:C_SIGN + 1], 2.0, ALU.mult, ALU.mult))
            dve.wait_ge(tile_full, T_B)
            r0 = slice(0, ROPE)
            V.tensor_tensor(rope_a[r0, :], bank[r0, 6, :], rstd[r0, :], ALU.mult).then_inc(tile_read, 1)
            lo_at(N_LAT, 0, 8)
            dve.wait_ge(tile_read, T_B)
            swap = [(i + 16) % 32 for i in range(32)]
            link(V.stream_shuffle(rope_b[r0, :], rope_a[r0, :], swap))
            link(V.tensor_tensor(rope_b[r0, :], rope_b[r0, :], sinb[r0, :], ALU.mult))
            link(V.tensor_tensor(rope_a[r0, :], rope_a[r0, :], cosb[r0, :], ALU.mult))
            V.tensor_tensor(rope_a[r0, :], rope_a[r0, :], rope_b[r0, :], ALU.add).then_inc(kr_ready, 1)
            dve.wait_ge(kr_split, 1)
            V.tensor_tensor(rope_l[r0, :], rope_a[r0, :], rope_h[r0, :].bitcast(F32), ALU.subtract).then_inc(kr_split, 1)
            rms(3, KV_LORA, lat_rstd[:])
            for k in range(KKV):
                V.tensor_tensor(ckvf[:, k, :], ckvf[:, k, :], lat_rstd[:], ALU.mult).then_inc(lat_norm, 1)
            for k in range(KKV):
                dve.wait_ge(lat_hi, KQ + k + 1)
                V.scalar_tensor_tensor(ckv_l[:, k, :], ckvf[:, k, :], tab[:, C_GKV + k:C_GKV + k + 1],
                                       ckv_h[:, k, :].bitcast(F32), ALU.mult, ALU.subtract).then_inc(lat_lo, 1)

            def project_lo(kind, g):
                n, b = place(kind, g)
                i = int(kind[1])
                if kind[0] == "v":
                    dve.wait_ge(v_hi, 2 * g + (QB + i + 1))
                    V.tensor_tensor(vb[:, i, :, :, 1, :].rearrange("p t e d -> p (t e) d"),
                                    bank[:, b, :].rearrange("p (a d) -> p a d", d=HALF),
                                    vb[:, i, :, :, 0, :].rearrange("p t e d -> p (t e) d").bitcast(F32),
                                    ALU.subtract).then_inc(tile_read, 1)
                    return
                hi_t, lo_t = (q_h, q_l) if kind[0] == "q" else (k_h, k_l)
                order = [x for x in (FIRST_ORDER if isinstance(g, int) else NEXT_ORDER) if x[0] in "qk"]
                dve.wait_ge(b_hi, 8 * g + 2 * (order.index(kind) + 1))
                for e in range(2):
                    r = slice(HALF * e, HALF * e + HALF)
                    V.tensor_tensor(lo_t[r, 2 * i + e, :], bank[r, b, :], hi_t[r, 2 * i + e, :].bitcast(F32),
                                    ALU.subtract).then_inc((b_lo, tile_read)[e], 1)

            def rotate(g):
                n = place("r", g)[0]
                dve.wait_ge(tile_full, 7 * g + (T_B + n))
                if not isinstance(g, int):
                    for i in range(2):
                        dve.wait_ge(r_moved[i], 64 * g)
                V.tensor_tensor(rope_a[:], bank[:, 7, :], cosb[:], ALU.mult).then_inc(r_part, 1)
                V.stream_shuffle(rope_b[:], bank[:, 7, :], swap).then_inc(tile_read, 1)
                dve.wait_ge(tile_read, 7 * g + (T_B + n))
                V.tensor_tensor(rope_b[:], rope_b[:], sinb[:], ALU.mult).then_inc(r_part, 1)
                dve.wait_ge(r_part, 2 * g + 2)
                V.tensor_tensor(rope_a[:], rope_a[:], rope_b[:], ALU.add).then_inc(r_sum, 1)

            def rotate_lo(g):
                dve.wait_ge(r_hi, g + 1)
                V.tensor_tensor(rope_l[:], rope_a[:], rope_h[:].bitcast(F32), ALU.subtract).then_inc(r_lo, 1)

            def maximum_b(g, e):
                dve.wait_ge(s_full, 1 + 16 * g + (4 * A_HEADS + 4 * e + 4))
                V.tensor_reduce(small[:, 4:8], bank[:, 0:QB, :], AX_X, ALU.max).then_inc(a_max, 1)
                dve.wait_ge(a_max, 4 * g + (A_HEADS + e + 1))
                V.tensor_scalar(small[:, 8:12], small[:, 4:8], -B_SCALE, None, ALU.mult).then_inc(a_shift, 1)

            def normalise_b(g, e):
                dve.wait_ge(a_exp, 1 + 16 * g + (5 * A_HEADS + 4 * e + 4))
                if not (isinstance(g, int) and 4 * g + e == 0):
                    dve.wait_ge(p_ready2, 8 * g + 2 * e)
                V.reciprocal(small[:, 24:28], small[:, 12:16]).then_inc(a_den, 1)
                dve.wait_ge(a_den, 4 * g + (2 * A_HEADS + e + 1))
                for qb in range(2):
                    V.tensor_scalar(pB[e % 2][:, qb, :], pB[e % 2][:, qb, :], small[:, 24 + qb:25 + qb], None, ALU.mult).then_inc(p_ready, 1)

            def lo_b(g, e, kbs):
                turned_lo(16 * g + 4 * A_HEADS, e, kbs, lambda kb: S, pTB_h, pTB_l)

            def out_b(g, e):
                r = slice(HALF * (e % 2), HALF * (e % 2) + HALF)
                if isinstance(g, int):
                    dst = oB[r, 2 * g + e // 2, :]
                else:
                    dst = oB[r, bass.ds(2 * g + e // 2, 1), :].rearrange("p a s -> p (a s)")
                out_sum(dst, 4 * g + (A_HEADS + e), e)

            def b_group(g, more):
                for e in range(4):
                    following = (g, e + 1) if e < 3 else (g + 1, 0) if more else None
                    if following:
                        maximum_b(*following)
                    if e > 0:
                        out_b(g, e - 1)
                    lo_b(g, e, (0, 1))
                    if following:
                        normalise_b(*following)
                    if more and FILL_1[e] == "r":
                        rotate(g + 1)
                    elif more:
                        project_lo(FILL_1[e], g + 1)
                    lo_b(g, e, (2, 3))
                    if more and e == 1:
                        rotate_lo(g + 1)
                    if more and FILL_2[e]:
                        project_lo(FILL_2[e], g + 1)
                out_b(g, 3)
                if more:
                    project_lo("v1", g + 1)

            for kind in FIRST_ORDER:
                if kind == "r":
                    rotate(0)
                    rotate_lo(0)
                    lo_at(N_B, 0, 2, 1536)
                else:
                    project_lo(kind, 0)
            maximum_b(0, 0)
            normalise_b(0, 0)
            with dve.Fori(0, GROUPS - 1) as g:
                b_group(g, True)
            b_group(GROUPS - 1, False)

            for b, (o, oh, ol) in enumerate(((oA, oA_h, oA_l), (oB, oB_h, oB_l))):
                for k in range(8):
                    dve.wait_ge(o_hi, 8 * b + k + 1)
                    V.tensor_tensor(ol[:, k, :], o[:, k, :], oh[:, k, :].bitcast(F32), ALU.subtract).then_inc(o_lo, 1)
            with dve.Fori(0, 8) as p:
                for i in range(2):
                    dve.wait_ge(tile_full, 4 * p + (T_BR + i + 1))
                    dve.wait_ge(gate_sig, 2 * p + 1)
                    dve.wait_ge(mg_lo, 1 + 2 * p)
                    V.tensor_tensor(tmp[:, i, :], bank[:, i, :], sg[:, 0, i, :], ALU.mult).then_inc(tile_read, 1)
                lo_at(N_BR, 2 * p, 2)
                for i in range(2):
                    dve.wait_ge(tile_full, 4 * p + (T_BR + i + 3))
                    dve.wait_ge(gate_sig, 2 * p + 2)
                    V.tensor_tensor(mt[:], bank[:, 2 + i, :], sg[:, 1, i, :], ALU.mult).then_inc(tile_read, 1)
                    dve.wait_ge(tile_read, 4 * p + (T_BR + i + 3))
                    V.tensor_tensor(tmp[:, i, :], tmp[:, i, :], mt[:], ALU.add).then_inc(merged, 1)
                    dve.wait_ge(merged, 2 * p + (i + 1))
                    dve.wait_ge(mg_hi, 2 * p + (i + 1))
                    V.tensor_tensor(mg_l[:, bass.ds(2 * p + i, 1), :], tmp[:, i:i + 1, :],
                                    mg_h[:, bass.ds(2 * p + i, 1), :].bitcast(F32), ALU.subtract).then_inc(mg_lo, 1)
                lo_at(N_BR, 2 * p, 3)

            link(V.memset(ssum[:], 0.0))
            with dve.Fori(0, 8) as p:
                for i in range(2):
                    dve.wait_ge(tile_full, 2 * p + (T_OUT + i + 1))
                    if i == 0:
                        dve.wait_ge(xin_in, 16 * p + 16)
                    V.tensor_tensor(x2[:, bass.ds(2 * p + i, 1), :], bank[:, 4 + i:5 + i, :], xin[:, i:i + 1, :],
                                    ALU.add).then_inc(tile_read, 1)
                    lo_at(N_OUT, 2 * p, 2 + i)
                    dve.wait_ge(sq_done, 2 * p + (KD + KQ + KKV + i + 1))
                    dve.wait_ge(sq_added, 2 * p + (KD + KQ + KKV + i))
                    V.tensor_tensor(ssum[:], ssum[:], sq[:, i, :], ALU.add).then_inc(sq_added, 1)
            for k in range(KD):
                dve.wait_ge(tile_full, T_MLP)
                dve.wait_ge(h2_hi, k + 1)
                V.scalar_tensor_tensor(h2_l[:, k, :], x2[:, k, :], tab[:, C_GMLP + k:C_GMLP + k + 1],
                                       h2_h[:, k, :].bitcast(F32), ALU.mult, ALU.subtract).then_inc(h2_lo, 1)
            rms(4, D, rstd[:])

            def up(c, q):
                for i in range(2):
                    n = CH * c + 2 * q + (i + 1)
                    dve.wait_ge(tile_full, 24 * c + 2 * q + (T_MLP + i + 1))
                    V.scalar_tensor_tensor(ru[:], bank[:, i, :], 0.0, rstd[:], ALU.max, ALU.mult).then_inc(tile_read, 1)
                    dve.wait_ge(tile_read, 24 * c + 2 * q + (T_MLP + i + 1))
                    V.tensor_tensor(uu[:], ru[:], ru[:], ALU.mult).then_inc(u_sq, 1)
                    dve.wait_ge(u_sq, n)
                    dve.wait_ge(u_hi, n)
                    V.tensor_tensor(u_l[:, bass.ds(2 * q + i, 1), :], uu[:].rearrange("p (a s) -> p a s", a=1),
                                    u_h[:, bass.ds(2 * q + i, 1), :].bitcast(F32), ALU.subtract).then_inc(u_lo, 1)
                    lo_at(N_MLP, 16 * c + 2 * q, 2 + i)

            def down(c, q, last=False):
                for b in range(2):
                    for j in range(2):
                        i = 2 * b + j
                        dve.wait_ge(tile_full, 24 * c + 4 * q + (T_MLP + CH + i + 1))
                        at_m = x2[:, bass.ds(4 * q + i, 1), :]
                        V.tensor_tensor(at_m, bank[:, 2 + i:3 + i, :], at_m, ALU.add).then_inc(tile_read, 1)
                    if not (last and q == 3):
                        lo_at(N_MLP + CH, 16 * c + 2 * q, 2 + b)
                    if last:
                        for j in range(2):
                            m = 4 * q + 2 * b + j
                            add_square(ssum[:], sq[:, j, :], 2 * KD + KQ + KKV + m + 1, m == 0)

            with dve.Fori(0, CHUNKS - 1) as c:
                with dve.Fori(0, 4) as q:
                    up(c, q)
                with dve.Fori(0, 4) as q:
                    down(c, q)
            with dve.Fori(0, 4) as q:
                up(CHUNKS - 1, q)
            for q in range(4):
                down(CHUNKS - 1, q, True)
            rms(5, D, rstd[:])
            for m in range(KD):
                dve.wait_ge(fin_gain, m + 1)
                V.tensor_tensor(outT[:, m, :], outT[:, m, :], rstd[:], ALU.mult).then_inc(fin_ready, 1)


def layout(inputs):
    import numpy as np
    f = np.float32

    def rows(w, width):
        return w.reshape(w.shape[0] // P, P, w.shape[1] // width, width)

    w_in = np.asarray(inputs["w_in"])[0]
    cuts = np.cumsum([1024, 256, 256, Q_LORA, KV_LORA, ROPE, D])
    qa, ka, va, cq, ckv, kr, ga, gb = np.split(w_in, cuts, axis=1)
    W = np.zeros((N_END, P, BLK), f)

    def cols(w):
        return rows(w, P).transpose(2, 1, 0, 3).reshape(-1, P, BLK)

    W[0:2] = cols(ka)
    W[2:4] = va.reshape(2, 8, P, 256).transpose(0, 2, 1, 3).reshape(2, P, BLK)
    a = W[N_A:N_LAT].reshape(8, 5, P, BLK)
    a[:, 0] = cols(qa)
    a[:, 1:] = np.concatenate([cols(ga), cols(gb)]).reshape(8, 4, P, BLK)
    W[N_LAT:N_LAT + 4] = cols(cq)
    W[N_LAT + 4:N_LAT + 6] = cols(ckv)
    W[N_LAT + 6][:, :KD * ROPE] = kr.reshape(KD, P, ROPE).transpose(1, 0, 2).reshape(P, -1)
    uq, uk, uv = (np.asarray(inputs[n])[0] for n in ("b_w_uq", "b_w_uk", "b_w_uv"))
    for g in range(GROUPS):
        hs = slice(4 * g, 4 * g + 4)
        q = uq[:, hs].reshape(KQ, P, 4, NOPE + ROPE)
        q = np.concatenate([q[..., :NOPE].reshape(KQ, P, -1), q[..., NOPE:].reshape(KQ, P, -1)], axis=2)
        W[N_B + 2 * g][:, :KQ * 384] = q.transpose(1, 0, 2).reshape(P, -1)
        for i, u in enumerate((uk, uv)):
            W[N_B + 2 * g + 1][:, 512 * i:512 * i + 512] = u[:, hs].reshape(KKV, P, 256).transpose(1, 0, 2).reshape(P, -1)

    def halves(w):
        k, m = w.shape
        return w.reshape(k // 1024, 8, P, m // 256, 256).transpose(0, 3, 2, 1, 4).reshape(k // 1024, m // 256, P, BLK)

    br = W[N_BR:N_OUT].reshape(8, 2, P, BLK)
    br[:, 0] = halves(np.asarray(inputs["w_branch_a"])[0])[0]
    br[:, 1] = halves(np.asarray(inputs["w_branch_b"])[0])[0]
    W[N_OUT:N_MLP] = cols(np.asarray(inputs["w_out"])[0])
    mlp = W[N_MLP:].reshape(CHUNKS, 2, 8, P, BLK)
    mlp[:, 0] = cols(np.asarray(inputs["w_mlp_in"])[0]).reshape(CHUNKS, 8, P, BLK)
    mlp[:, 1] = halves(np.asarray(inputs["w_mlp_out"])[0])

    tab = np.zeros((P, C_ALL), f)
    tab[:, C_ONES:C_ONES + P] = 1.0
    tab[:, C_IDENT:C_IDENT + P] = np.eye(P, dtype=f)
    for c, n in ((C_GATTN, "attn_norm_g"), (C_GMLP, "mlp_norm_g"), (C_GFIN, "final_norm_g"), (C_GQ, "b_q_norm_g"),
                 (C_GKV, "b_kv_norm_g")):
        g = np.asarray(inputs[n]).reshape(-1, P).T
        tab[:, c:c + g.shape[1]] = g
    tab[:, C_SLOPE:C_SLOPE + A_HEADS] = -np.exp2(-8.0 * (np.arange(A_HEADS) + 1.0) / A_HEADS).astype(f) / A_SCALE
    tab[:, C_SINK:C_SINK + A_HEADS] = np.asarray(inputs["a_sink"])
    p = np.arange(P)
    tab[:, C_INVF] = (f(10000.0) ** (-(np.arange(16, dtype=f)) / f(16)))[p % 16]
    tab[:, C_SIGN] = np.where(p % ROPE < ROPE // 2, -1.0, 1.0)
    mask = np.zeros((P, QB, 3 * P), f)
    for qb in range(QB):
        k0, k1 = key_range(qb)
        d = np.abs(P * qb + np.arange(P)[:, None] - np.arange(k0, k1)[None])
        mask[:, qb, :k1 - k0] = np.where(d <= WINDOW, 0.0, 1e30)
    pos = np.asarray(inputs["positions"])[0]
    pos = np.concatenate([np.broadcast_to(pos, (P, S)), pos.reshape(QB, P).T], axis=1)
    xT = np.asarray(inputs["x"])[0].T.reshape(KD, P, S).transpose(1, 0, 2)
    return {"xT": xT, "tab": tab, "pos": pos, "mask": mask, "w": W}


def kernel(**inputs):
    import numpy as np
    import concourse.bacc as bacc
    from concourse.bass_utils import run_bass_kernel_spmd

    nc = bacc.Bacc("TRN2", target_bir_lowering=False, num_devices=1)
    arrays, args = {}, []
    for name, a in layout(inputs).items():
        a = np.ascontiguousarray(a)
        arrays["in_" + name] = a
        args.append(nc.dram_tensor("in_" + name, a.shape, mybir.dt.from_np(a.dtype), kind="ExternalInput").ap())
    args.append(nc.dram_tensor("out_t", (P, KD, S), F32, kind="ExternalOutput").ap())
    build(nc, *args)
    r = run_bass_kernel_spmd(nc, [arrays], core_ids=[0])
    return np.ascontiguousarray(r.results[0]["out_t"].transpose(2, 1, 0).reshape(1, S, D))
```

```python
from contextlib import ExitStack

import concourse.bass as bass
from concourse import mybir

F32 = mybir.dt.float32
F32R = mybir.dt.float32r
I32 = mybir.dt.int32
ALU = mybir.AluOpType
ACT = mybir.ActivationFunctionType
AX_X = mybir.AxisListType.X

P = 128
S = 512
D = 2048
KD = D // P
DFF = 4 * D
EPS = 1e-6
QB = S // P
HALF = 64
A_HEADS, A_KV, WINDOW = 16, 4, 128
B_HEADS, Q_LORA, KV_LORA, NOPE, ROPE = 16, 512, 256, 64, 32
KQ, KKV = Q_LORA // P, KV_LORA // P
GROUPS = B_HEADS // 4
A_SCALE = 0.125
B_SCALE = float((NOPE + ROPE) ** -0.5)
BLK = 2048
CH = 8
CHUNKS = DFF // (CH * P)

N_A, T_A = 4, 6
N_LAT, T_LAT = N_A + 40, T_A + 40
N_B, T_B = N_LAT + 7, T_LAT + 7
N_BR, T_BR = N_B + 2 * GROUPS, T_B + 7 * GROUPS
N_OUT, T_OUT = N_BR + 16, T_BR + 32
N_MLP, T_MLP = N_OUT + 16, T_OUT + 16
N_END, T_END = N_MLP + 16 * CHUNKS, T_MLP + 24 * CHUNKS

X_CUTS = (0, 2, 4, 8, 12, KD)

C_ONES, C_GATTN, C_GMLP, C_GFIN, C_GQ, C_GKV, C_SLOPE, C_SINK, C_INVF, C_SIGN, C_POS = (
    0, 128, 144, 160, 176, 180, 182, 198, 214, 215, 216)
C_IDENT = 220
A_ORDER = (0, 3, 1, 2)
A_BANK = ((0, 0), (1, 0), (2, 0), (0, 256))
C_ALL = C_IDENT + P

TWO_PI_PARTS = (6.283203125, -1.7821788787841797e-05, 3.9693904e-09)

FIRST_ORDER = ("k0", "k1", "v0", "r", "q0", "q1", "v1")
NEXT_ORDER = ("r", "k0", "q0", "k1", "q1", "v0", "v1")
FIRST_BANK = (0, 1, 2, 7, 3, 4, 7)
FILL_0 = (None, "k0", "k1", None)
FILL_1 = ("r", "q0", "q1", "v0")


def place(kind, g):
    if isinstance(g, int) and g == 0:
        return FIRST_ORDER.index(kind) + 1, FIRST_BANK[FIRST_ORDER.index(kind)]
    return NEXT_ORDER.index(kind) + 1, 7


def key_range(qb):
    return max(0, qb - 1) * P, min(QB, qb + 2) * P


def build(nc, xT_d, tab_d, pos_d, mask_d, w_d, out_d):
    gates_d = nc.dram_tensor("gates_scratch", (32, P, S), F32, kind="Internal").ap()

    KB = 1024
    BASE = 16512

    def at(name, kb, shape, dt):
        return nc.alloc_sbuf_tensor_at(name, shape, dt, offset=BASE + int(kb * KB))

    raw = at("raw", 0, [P, 2, BLK], F32)
    wsp = at("wsp", 16, [P, 2, 2, BLK], F32R)
    tab = at("tab", 48, [P, C_ALL], F32)
    rstd = at("rstd", 50, [P, S], F32)
    small = at("small", 52, [P, 64], F32)
    tmp = at("tmp", 52.5, [P, 2, S], F32)
    dist_t = at("dist_t", 154, [P, S], F32)
    otmp = at("otmp", 56.5, [HALF, S], F32)
    xg_h = at("xg_h", 60, [P, KD, S], F32R)
    xg_l = at("xg_l", 92, [P, KD, S], F32R)
    xT = at("xT", 124, [P, KD, S], F32)
    dist = at("dist", 124, [P, QB, 3 * P], F32)
    s_sb = at("s_sb", 130, [P, QB, 3 * P], F32)
    pA = at("pA", 136, [P, QB, 3 * P], F32)
    pTA_h = at("pTA_h", 142, [P, QB, 3 * P], F32R)
    pTA_l = at("pTA_l", 148, [P, QB, 3 * P], F32R)
    qf = at("qf", 154, [P, S], F32)
    kd_h = at("kd_h", 156, [P, A_KV, S], F32R)
    kd_l = at("kd_l", 164, [P, A_KV, S], F32R)
    va = at("va", 172, [P, QB, A_KV, 2, HALF], F32R)
    vc = at("vc", 180, [P, QB, 2, HALF], F32R)
    oA = at("oA", 182, [P, 8, S], F32)
    qs = at("qs", 198, [P, 2, S], F32R)
    pos_a = at("pos_a", 198, [P, S + QB], I32)
    gbuf = at("gbuf", 202, [P, 2, S], F32)
    cqf = at("cqf", 124, [P, KQ, S], F32)
    ckvf = at("ckvf", 132, [P, KKV, S], F32)
    cq_h = at("cq_h", 136, [P, KQ, S], F32R)
    cq_l = at("cq_l", 144, [P, KQ, S], F32R)
    ckv_h = at("ckv_h", 152, [P, KKV, S], F32R)
    ckv_l = at("ckv_l", 156, [P, KKV, S], F32R)
    cosb = at("cosb", 160, [P, S], F32)
    sinb = at("sinb", 162, [P, S], F32)
    oB = at("oB", 164, [P, 8, S], F32)
    sqL = [at("sqL0", 176, [P, S], F32), at("sqL1", 56.5, [P, S], F32)]
    lat_rstd = at("lat_rstd", 178, [P, S], F32)
    sumsq = at("sumsq", 180, [P, S], F32)
    rope_a = at("rope_a", 198, [P, S], F32)
    rope_b = at("rope_b", 200, [P, S], F32)
    rope_h = at("rope_h", 202, [P, S], F32R)
    rope_l = at("rope_l", 204, [P, S], F32R)
    q_h = at("q_h", 60, [P, 4, S], F32R)
    q_l = at("q_l", 68, [P, 4, S], F32R)
    k_h = at("k_h", 76, [P, 4, S], F32R)
    k_l = at("k_l", 84, [P, 4, S], F32R)
    vb = at("vb", 92, [P, QB, 4, 2, HALF], F32R)
    pB = [at("pB0", 100, [P, QB, S], F32), at("pB1", 124, [P, QB, S], F32)]
    pTB_h = at("pTB_h", 108, [P, QB, S], F32R)
    pTB_l = at("pTB_l", 116, [P, QB, S], F32R)
    oA_h = at("oA_h", 60, [P, 8, S], F32R)
    oA_l = at("oA_l", 76, [P, 8, S], F32R)
    oB_h = at("oB_h", 92, [P, 8, S], F32R)
    oB_l = at("oB_l", 108, [P, 8, S], F32R)
    mg_h = at("mg_h", 124, [P, KD, S], F32R)
    mg_l = at("mg_l", 156, [P, KD, S], F32R)
    sg = at("sg", 188, [P, 2, 2, S], F32)
    gl = at("gl", 198, [P, 2, 2, S], F32)
    mt = at("mt", 196, [P, S], F32)
    x2 = at("x2", 60, [P, KD, S], F32)
    h2_h = at("h2_h", 92, [P, KD, S], F32R)
    h2_l = at("h2_l", 124, [P, KD, S], F32R)
    u_h = at("u_h", 156, [P, CH, S], F32R)
    u_l = at("u_l", 172, [P, CH, S], F32R)
    xin = at("xin", 188, [P, 2, S], F32)
    ssum = at("ssum", 192, [P, S], F32)
    sq = at("sq", 194, [P, 2, S], F32)
    ru = at("ru", 198, [P, S], F32)
    uu = at("uu", 200, [P, S], F32)
    outT = at("outT", 92, [P, KD, S], F32)
    pos_i = at("pos_i", 172, [P, S], I32)
    posf = at("posf", 174, [P, S], F32)
    ang = at("ang", 164, [P, S], F32)
    turns = at("turns", 166, [P, S], F32)
    t_hi = at("t_hi", 168, [P, S], F32)
    t_lo = at("t_lo", 170, [P, S], F32)

    with ExitStack() as ctx:
        bank = ctx.enter_context(nc.psum_tensor("bank", [P, 8, S], F32))

        def sem(name):
            return ctx.enter_context(nc.semaphore(name))

        raw_full = [sem("raw_full0"), sem("raw_full1")]
        hi_done, lo_done = sem("hi_done"), sem("lo_done")
        tile_full, tile_read = sem("tile_full"), sem("tile_read")
        tab_in = sem("tab_in")
        x_in = [sem(f"x_in{c}") for c in range(len(X_CUTS) - 1)]
        mask_in, pos_in = sem("mask_in"), sem("pos_in")
        xh_done, xl_done = sem("xh_done"), sem("xl_done")
        sq_done, sq_added = sem("sq_done"), sem("sq_added")
        stat_full, stat_read, diag_ready, rstd_full = sem("stat_full"), sem("stat_read"), sem("diag_ready"), sem("rstd_full")
        sqrt_done, sin_done = sem("sqrt_done"), sem("sin_done")
        rstd_done = sem("rstd_done")
        chain, ang_ready = sem("chain"), sem("ang_ready")
        hi_half, lo_half = sem("hi_half"), sem("lo_half")
        raw_half = sem("raw_half")
        kv_hi, kv_ready = sem("kv_hi"), sem("kv_ready")
        v_half, v_hi, vc_ready = sem("v_half"), sem("v_hi"), sem("vc_ready")
        pad_set = sem("pad_set")
        q_hi, q_ready = sem("q_hi"), sem("q_ready")
        s_full, s_read = sem("s_full"), sem("s_read")
        neg_ready = sem("neg_ready")
        a_max, a_shift, a_exp, a_den, p_ready, p_ready2 = (
            sem("a_max"), sem("a_shift"), sem("a_exp"), sem("a_den"), sem("p_ready"), sem("p_ready2"))
        t_full, pt_hi, pt_lo = sem("t_full"), sem("pt_hi"), sem("pt_lo")
        pv_full, pv_half, o_done = sem("pv_full"), sem("pv_half"), sem("o_done")
        gate_out = [sem("gate_out0"), sem("gate_out1")]
        lat_norm, lat_hi, lat_lo = sem("lat_norm"), sem("lat_hi"), sem("lat_lo")
        kr_ready, kr_split, kr_spread = sem("kr_ready"), sem("kr_split"), sem("kr_spread")
        zero_set = sem("zero_set")
        r_part = sem("r_part")
        b_hi, b_lo, r_sum, r_hi, r_lo = sem("b_hi"), sem("b_lo"), sem("r_sum"), sem("r_hi"), sem("r_lo")
        r_first_hi, r_first_lo = sem("r_first_hi"), sem("r_first_lo")
        r_moved = [sem("r_moved0"), sem("r_moved1")]
        o_hi, o_lo = sem("o_hi"), sem("o_lo")
        gate_in = [sem("gate_inA"), sem("gate_inB")]
        gate_sig, merged, mg_hi, mg_lo = sem("gate_sig"), sem("merged"), sem("mg_hi"), sem("mg_lo")
        xin_in = sem("xin_in")
        h2_hi, h2_lo = sem("h2_hi"), sem("h2_lo")
        u_sq, u_hi, u_lo = sem("u_sq"), sem("u_hi"), sem("u_lo")
        fin_gain, fin_ready, stored = sem("fin_gain"), sem("fin_ready"), sem("stored")

        block = ctx.enter_context(nc.Block())
        ones = tab[:, C_ONES:C_ONES + P]
        ident = tab[:, C_IDENT:C_IDENT + P]

        @block.sync
        def _(sp):
            def x_part(c):
                rows = slice(X_CUTS[c], X_CUTS[c + 1])
                sp.dma_start(xT[:, rows, :], xT_d[:, rows, :]).then_inc(x_in[c], 16)
            sp.dma_start(raw[:, 0, 0:BLK // 2], w_d[0][:, 0:BLK // 2]).then_inc(raw_half, 16)
            sp.dma_start(tab[:], tab_d).then_inc(tab_in, 16)
            x_part(0)
            x_part(1)
            sp.dma_start(raw[:, 0, BLK // 2:], w_d[0][:, BLK // 2:]).then_inc(raw_full[0], 16)
            x_part(2)
            sp.dma_start(raw[:, 1, :], w_d[1]).then_inc(raw_full[1], 16)
            x_part(3)
            x_part(4)
            with sp.Fori(1, N_END // 2) as h:
                for slot in range(2):
                    sp.wait_ge(hi_done, h * 2 + slot - 1)
                    sp.wait_ge(lo_done, h * 2 + slot - 1)
                    sp.dma_start(raw[:, slot, :], w_d[bass.ds(h * 2 + slot, 1)].rearrange("a p k -> p (a k)")).then_inc(
                        raw_full[slot], 16)
            n = N_END - 1
            sp.wait_ge(hi_done, n - 1)
            sp.wait_ge(lo_done, n - 1)
            sp.dma_start(raw[:, n % 2, :], w_d[n]).then_inc(raw_full[n % 2], 16)
            for i in range(KD // 2):
                sp.wait_ge(fin_ready, 2 * i + 2)
                sp.dma_start(out_d[:, 2 * i:2 * i + 2, :], outT[:, 2 * i:2 * i + 2, :]).then_inc(stored, 16)
            sp.wait_ge(stored, 16 * (KD // 2))

        @block.gpsimd
        def _(pool):
            pool.dma_start(pos_a[:], pos_d).then_inc(pos_in, 16)
            pool.wait_ge(sq_done, KD)
            pool.wait_ge(xl_done, KD)
            pool.dma_start(dist[:], mask_d).then_inc(mask_in, 16)
            nc.gpsimd.memset(s_sb[:, 0, 2 * P:3 * P], -3e38).then_inc(pad_set, 1)
            nc.gpsimd.memset(s_sb[:, 3, 2 * P:3 * P], -3e38).then_inc(pad_set, 1)
            pool.wait_ge(tile_read, T_A)
            with pool.Fori(0, 4) as J:
                pool.wait_ge(pv_full, 1 + J * 4)
                nc.gpsimd.tensor_copy(vc[:].rearrange("p a b c -> p a (b c)"),
                                      va[:, :, bass.ds(J, 1), :, :].rearrange("p a g b c -> p a (g b c)")).then_inc(vc_ready, 1)
                for jj in range(2):
                    for i in range(4):
                        pool.wait_ge(tile_read, J * 10 + (T_A + 5 * jj + 1 + i + 1))
                        pool.dma_start(gates_d[bass.ds(J * 8 + 4 * jj + i, 1)].rearrange("a p k -> p (a k)"),
                                       gbuf[:, i % 2, :]).then_inc(gate_out[i % 2], 16)
            pool.wait_ge(gate_out[0], 16 * 16)
            pool.wait_ge(gate_out[1], 16 * 16)
            pool.wait_ge(pv_full, 1 + A_HEADS)
            pool.dma_start(pos_i[:], pos_d[:, 0:S]).then_inc(pos_in, 16)

            def block_lo(n, width):
                pool.wait_ge(hi_done, n + 1)
                pool.wait_ge(lo_done, n)
                nc.gpsimd.tensor_tensor(wsp[:, n % 2, 1, 0:width], raw[:, n % 2, 0:width],
                                        wsp[:, n % 2, 0, 0:width].bitcast(F32), ALU.subtract).then_inc(lo_done, 1)


            pool.wait_ge(tile_full, T_B)
            for t in (q_h, q_l, k_h, k_l):
                for e in (1, 3):
                    nc.gpsimd.memset(t[0:32, e, :].bitcast(F32), 0.0).then_inc(zero_set, 1)

            def rope_moves(g, pairs):
                pool.wait_ge(r_lo, g + 1)
                pool.wait_ge(r_hi, g + 1)
                for i in pairs:
                    if g > 0:
                        pool.wait_ge(s_full, 1 + 4 * A_HEADS + 16 * (g - 1) + 8 * (i + 1))
                    for e in (2 * i, 2 * i + 1):
                        to = HALF if e % 2 == 0 else 32
                        for src, dst in ((rope_h, q_h), (rope_l, q_l)):
                            pool.dma_start(dst[to:to + 32, e, :], src[32 * e:32 * e + 32, :]).then_inc(r_moved[i], 16)
            def normalise_part(h):
                pool.wait_ge(a_den, 2 * A_HEADS + h + 1)
                qb = QB - 1
                nc.gpsimd.tensor_scalar(pB[h % 2][:, qb, :], pB[h % 2][:, qb, :], small[:, 24 + qb:25 + qb], None,
                                        ALU.mult).then_inc(p_ready2, 1)

            rope_moves(0, (1,))
            normalise_part(0)
            block_lo(N_B + 2, 1536)
            for g in range(GROUPS):
                for e in range(4):
                    if e == 0:
                        block_lo(N_B + 2 * g + 3, 1024 if g < GROUPS - 1 else BLK)
                    if 4 * g + e + 1 < B_HEADS:
                        normalise_part(4 * g + e + 1)
                    if g < GROUPS - 1:
                        if e in (1, 2):
                            rope_moves(g + 1, (e - 1,))
                        if e == 3:
                            block_lo(N_B + 2 * g + 4, BLK)

            def gate_loads(p):
                for b in range(2):
                    if not (isinstance(p, int) and p == 0):
                        pool.wait_ge(gate_sig, p * 2 + b - 1)
                    pool.dma_start(gl[:, b], gates_d[bass.ds(p * 2 + 16 * b, 2)].rearrange("m p s -> p m s")).then_inc(
                        gate_in[b], 16)
            pool.wait_ge(r_moved[0], 64 * (GROUPS - 1))
            pool.wait_ge(r_moved[1], 64 * GROUPS)
            gate_loads(0)
            with pool.Fori(1, 8) as p:
                gate_loads(p)
            pool.wait_ge(merged, 16)
            pool.wait_ge(mg_lo, 1 + 16)
            with pool.Fori(0, 8) as p:
                pool.wait_ge(tile_read, p * 2 + T_OUT)
                pool.dma_start(xin[:], xT_d[:, bass.ds(p * 2, 2), :]).then_inc(xin_in, 16)

        @block.tensor
        def _(pe):
            for s in (pv_full, s_full, t_full):
                pe.sem_inc(s, 1)

            def split_ready(n):
                pe.wait_ge(hi_done, n + 1)
                pe.wait_ge(lo_done, n + 1)

            def mm3(out, w, sl, xh, xl, start, stop):
                wh, wl = wsp[:, sl, 0, w], wsp[:, sl, 1, w]
                nc.tensor.matmul(out, wh, xh, start=start, stop=False)
                nc.tensor.matmul(out, wh, xl, start=False, stop=False)
                return nc.tensor.matmul(out, wl, xh, start=False, stop=stop)

            def tile(b, sl, k0=0, k1=KD, xh=xg_h, xl=xg_l, kn=KD, off=0, width=P):
                for k in range(k0, k1):
                    c = off + width * k
                    last = mm3(bank[:, b, :], slice(c, c + P), sl, xh[:, k, :], xl[:, k, :], k == 0, k == kn - 1)
                return last

            def sums_of(squares):
                for tt in range(QB):
                    last = nc.tensor.matmul(bank[:, 7, tt:tt + 1], squares[:, P * tt:P * tt + P], ones[:, 0:1],
                                            start=True, stop=True)
                last.then_inc(stat_full, 1)

            def spread_rstd(i):
                pe.wait_ge(diag_ready, QB * i)
                nc.tensor.matmul(bank[:, 7, :], ones, tmp[:, 1, :], start=True, stop=True).then_inc(rstd_full, 1)

            pe.wait_ge(tab_in, 16)
            pe.wait_ge(hi_half, 1)
            pe.wait_ge(lo_half, 1)
            for k in range(KD):
                if k == KD // 2:
                    split_ready(0)
                pe.wait_ge(xh_done, k + 1)
                pe.wait_ge(xl_done, k + 1)
                last = mm3(bank[:, 0, :], slice(P * k, P * k + P), 0, xg_h[:, k, :], xg_l[:, k, :], k == 0, k == KD - 1)
            last.then_inc(tile_full, 1)
            split_ready(1)
            tile(1, 1).then_inc(tile_full, 1)
            for b in range(2):
                split_ready(2 + b)
                for tt in range(QB):
                    out = bank[:, 2 + tt, 0:256]
                    tok = slice(P * tt, P * tt + P)
                    for k in range(8):
                        wh, wl = (wsp[:, b, i, 256 * k:256 * k + 256] for i in range(2))
                        xh, xl = xg_h[:, 8 * b + k, tok], xg_l[:, 8 * b + k, tok]
                        nc.tensor.matmul(out, xh, wh, start=(b == 0 and k == 0), stop=False)
                        nc.tensor.matmul(out, xh, wl, start=False, stop=False)
                        last = nc.tensor.matmul(out, xl, wh, start=False, stop=(b == 1 and k == 7))
                    if b == 1:
                        last.then_inc(tile_full, 1)
                    if b == 1 and tt == 1:
                        spread_rstd(1)
                if b == 0:
                    last.then_inc(v_half, 1)
                    pe.wait_ge(sq_added, KD)
                    sums_of(tmp[:, 0, :])

            def a_scores(J, jj, e):
                h = 2 * jj + e
                for qb in A_ORDER:
                    k0, k1 = key_range(qb)
                    b, c = A_BANK[qb]
                    out = bank[:, b, c:c + k1 - k0]
                    lhs = qs[:, e, P * qb:P * qb + P]
                    if qb == 0:
                        pe.wait_ge(kv_hi, 3 * A_KV)
                        pe.wait_ge(q_ready, J * 4 + 2 * jj + 2)
                        pe.wait_ge(s_read, 1 + J * 16 + 4 * h)
                    nc.tensor.matmul(out, lhs, kd_h[:, bass.ds(J, 1), k0:k1].rearrange("p a k -> p (a k)"), start=True, stop=False)
                    nc.tensor.matmul(out, lhs, kd_l[:, bass.ds(J, 1), k0:k1].rearrange("p a k -> p (a k)"),
                                     start=False, stop=True).then_inc(s_full, 1)

            def a_turn(J, h, kbs):
                for kb in kbs:
                    if kb == 0:
                        pe.wait_ge(p_ready, J * 16 + 4 * h + 4)
                    pe.wait_ge(pt_lo, 1 + J * 16 + max(4 * h + kb - 1, 0))
                    q0, q1 = max(0, kb - 1), min(QB, kb + 2)
                    for qb in range(q0, q1):
                        c = P * kb - key_range(qb)[0]
                        last = nc.tensor.transpose(bank[:, 4 + kb % 2, P * (qb - q0):P * (qb - q0) + P],
                                                   pA[:, qb, c:c + P], ident)
                    last.then_inc(t_full, 1)

            def a_values(J, h, kbs):
                for kb in kbs:
                    if kb == 0:
                        pe.wait_ge(vc_ready, J + 1)
                        pe.wait_ge(o_done, 1 + J * 4 + h)
                    pe.wait_ge(pt_lo, 1 + J * 16 + 4 * h + kb + 1)
                    q0, q1 = key_range(kb)
                    n = q1 - q0
                    nc.tensor.matmul(bank[:, 6, q0:q1], vc[:, kb].rearrange("p a d -> p (a d)"), pTA_h[:, kb, 0:n],
                                     start=(kb == 0), stop=False, skip_group_check=True)
                    last = nc.tensor.matmul(bank[0:HALF, 6, q0:q1], vc[:, kb, 0, :], pTA_l[:, kb, 0:n],
                                            start=False, stop=(kb == QB - 1), skip_group_check=True)
                if kbs[-1] == QB - 1:
                    last.then_inc(pv_full, 1)

            with pe.Fori(0, 4) as J:
                for jj in range(2):
                    h0, h1 = 2 * jj, 2 * jj + 1

                    def piece(i, k0, k1):
                        b, sl = (3, 7)[(5 * jj + i) % 2], (5 * jj + i) % 2
                        if k0 == 0:
                            split_ready(J * 10 + (N_A + 5 * jj + i))
                            pe.wait_ge(tile_read, J * 10 + (T_A + 5 * jj + i - 1))
                        last = tile(b, sl, k0, k1)
                        if k1 == KD:
                            last.then_inc(tile_full, 1)
                    piece(0, 0, KD)
                    piece(1, 0, KD)
                    a_scores(J, jj, 0)
                    piece(2, 0, KD)
                    a_turn(J, h0, (0, 1))
                    piece(3, 0, 8)
                    a_values(J, h0, (0, 1))
                    a_turn(J, h0, (2, 3))
                    a_scores(J, jj, 1)
                    piece(3, 8, KD)
                    a_values(J, h0, (2, 3))
                    piece(4, 0, 8)
                    a_turn(J, h1, (0, 1))
                    piece(4, 8, 11)
                    a_values(J, h1, (0, 1))
                    a_turn(J, h1, (2, 3))
                    piece(4, 11, 14)
                    a_values(J, h1, (2, 3))
                    piece(4, 14, KD)

            pe.wait_ge(s_read, 1 + 4 * A_HEADS)
            pe.wait_ge(pt_lo, 1 + 4 * A_HEADS)
            pe.wait_ge(tile_read, T_A + 39)
            for t in range(KKV + KQ):
                split_ready(N_LAT + t)
                cut = 13 if t == KKV + 1 else KD // 2
                tile(t, (N_LAT + t) % 2, 0, cut)
                if t == KKV:
                    pe.wait_ge(tile_read, T_LAT)
                    pe.wait_ge(sq_added, KD + KKV)
                    sums_of(sumsq)
                if t == KKV + 1:
                    spread_rstd(2)
                tile(t, (N_LAT + t) % 2, cut, KD).then_inc(tile_full, 1)
            split_ready(N_LAT + KKV + KQ)
            pe.wait_ge(o_done, 1 + A_HEADS)
            for k in range(KD):
                if k == 5:
                    pe.wait_ge(sq_added, KD + KQ + KKV)
                    pe.wait_ge(rstd_done, 2)
                    sums_of(sumsq)
                if k == 13:
                    spread_rstd(3)
                last = mm3(bank[0:ROPE, 6, :], slice(ROPE * k, ROPE * k + ROPE), (N_LAT + KKV + KQ) % 2, xg_h[:, k, :],
                           xg_l[:, k, :], k == 0, k == KD - 1)
            last.then_inc(tile_full, 1)

            def b_project(kind, g):
                n, b = place(kind, g)
                first = isinstance(g, int) and g == 0
                q_block, kv_block = N_B, N_B + 1
                if kind == "r":
                    split_ready(2 * g + q_block)
                if kind == "k0":
                    split_ready(2 * g + kv_block)
                if first:
                    pe.wait_ge(lat_lo, KKV if kind[0] in "kv" else KQ + KKV)
                else:
                    pe.wait_ge(tile_read, 7 * g + (T_B + n - 1))
                if kind[0] in "qr":
                    part = ("q0", "q1", "r").index(kind)
                    last = tile(b, q_block % 2, 0, KQ, cq_h, cq_l, KQ, P * part, 3 * P)
                elif kind[0] == "k":
                    last = tile(b, kv_block % 2, 0, KKV, ckv_h, ckv_l, KKV, P * int(kind[1]), 2 * P)
                else:
                    for t in range(2):
                        tt = 2 * int(kind[1]) + t
                        tok = slice(P * tt, P * tt + P)
                        out = bank[:, b, 256 * t:256 * t + 256]
                        for k in range(KKV):
                            wh, wl = (wsp[:, kv_block % 2, v, 512 + 256 * k:768 + 256 * k] for v in range(2))
                            nc.tensor.matmul(out, ckv_h[:, k, tok], wh, start=(k == 0), stop=False)
                            nc.tensor.matmul(out, ckv_h[:, k, tok], wl, start=False, stop=False)
                            last = nc.tensor.matmul(out, ckv_l[:, k, tok], wh, start=False, stop=(k == KKV - 1))
                last.then_inc(tile_full, 1)

            def b_scores(g, e):
                first = isinstance(g, int) and g == 0
                rows = slice(0, NOPE + ROPE) if e % 2 == 0 else slice(0, P)
                if e % 2 == 0:
                    pe.wait_ge(b_lo, 3 if first and e == 0 else 4 * g + (2 * (e // 2) + 2))
                    if not (first and e == 0):
                        pe.wait_ge(tile_read, 7 * g + (T_B + place("q0q1"[e:e + 2], g)[0]))
                    if first and e == 0:
                        pe.wait_ge(r_first_hi, 2)
                        pe.wait_ge(r_first_lo, 2)
                    elif e == 0:
                        pe.wait_ge(r_moved[0], 64 * g)
                    else:
                        pe.wait_ge(r_moved[1], 64 * g + 64)
                for qb in range(QB):
                    if not (first and e == 0):
                        pe.wait_ge(a_exp, 16 * g + (1 + 5 * A_HEADS + 4 * e - 4 + qb + 1))
                    q = slice(P * qb, P * qb + P)
                    nc.tensor.matmul(bank[:, qb, :], q_h[rows, e, q], k_h[rows, e, :], start=True, stop=False)
                    nc.tensor.matmul(bank[:, qb, :], q_h[rows, e, q], k_l[rows, e, :], start=False, stop=False)
                    nc.tensor.matmul(bank[:, qb, :], q_l[rows, e, q], k_h[rows, e, :], start=False, stop=True).then_inc(
                        s_full, 1)

            def b_turn(g, e, kbs):
                for kb in kbs:
                    if kb == 0:
                        pe.wait_ge(p_ready, 12 * g + (4 * A_HEADS + 3 * e + 3))
                        pe.wait_ge(p_ready2, 4 * g + (e + 1))
                    pe.wait_ge(pt_lo, 1 + 16 * g + (4 * A_HEADS + 4 * e + kb - 1))
                    for qb in range(QB):
                        last = nc.tensor.transpose(bank[:, 4 + kb % 2, P * qb:P * qb + P], pB[e % 2][:, qb, P * kb:P * kb + P], ident)
                    last.then_inc(t_full, 1)

            def b_values(g, e):
                pe.wait_ge(o_done, 4 * g + (1 + A_HEADS + e))
                if e == 0:
                    pe.wait_ge(tile_read, 7 * g + (T_B + 7))
                for kb in range(QB):
                    pe.wait_ge(pt_lo, 16 * g + (1 + 4 * A_HEADS + 4 * e + kb + 1))
                    v = vb[:, kb, e]
                    nc.tensor.matmul(bank[:, 6, :], v.rearrange("p a d -> p (a d)"), pTB_h[:, kb, :],
                                     start=(kb == 0), stop=False, skip_group_check=True)
                    last = nc.tensor.matmul(bank[0:HALF, 6, :], v[:, 0, :], pTB_l[:, kb, :],
                                            start=False, stop=(kb == QB - 1), skip_group_check=True)
                last.then_inc(pv_full, 1)

            def b_group(g, more):
                for e in range(4):
                    if e < 3:
                        b_scores(g, e + 1)
                    elif more:
                        b_scores(g + 1, 0)
                    if more and FILL_0[e]:
                        b_project(FILL_0[e], g + 1)
                    if e > 0:
                        b_values(g, e - 1)
                    else:
                        b_project("v1", g)
                    b_turn(g, e, (0, 1))
                    if more:
                        b_project(FILL_1[e], g + 1)
                    b_turn(g, e, (2, 3))
                b_values(g, 3)

            pe.wait_ge(tile_read, T_B - 1)
            for kind in FIRST_ORDER[:-1]:
                if kind == "r":
                    pe.wait_ge(rstd_done, 3)
                b_project(kind, 0)
            pe.wait_ge(zero_set, 8)
            pe.wait_ge(kr_spread, 8)
            pe.wait_ge(tile_read, T_B + 5)
            b_scores(0, 0)
            with pe.Fori(0, GROUPS - 1) as g:
                b_group(g, True)
            b_group(GROUPS - 1, False)

            def branch_pair(p, first):
                for b, (oh, ol) in enumerate(((oA_h, oA_l), (oB_h, oB_l))):
                    split_ready(2 * p + N_BR + b)
                    for i in range(2):
                        pe.wait_ge(tile_read, 4 * p + (T_BR + 2 * b + i - 3))
                        for k in range(8):
                            if first and i == 0:
                                pe.wait_ge(o_lo, 8 * b + k + 1)
                            c = 256 * k + P * i
                            last = mm3(bank[:, 2 * b + i, :], slice(c, c + P), (N_BR + b) % 2, oh[:, k, :], ol[:, k, :],
                                       k == 0, k == 7)
                        last.then_inc(tile_full, 1)

            pe.wait_ge(tile_read, T_BR)
            pe.wait_ge(a_exp, 1 + 5 * A_HEADS + 4 * B_HEADS)
            branch_pair(0, True)
            with pe.Fori(1, 8) as p:
                branch_pair(p, False)

            def out_pair(p, first):
                for i in range(2):
                    split_ready(2 * p + N_OUT + i)
                    pe.wait_ge(tile_read, 2 * p + (T_OUT + i - 1))
                    for k in range(KD):
                        if first and i == 0:
                            pe.wait_ge(mg_lo, 1 + k + 1)
                        last = mm3(bank[:, 4 + i, :], slice(P * k, P * k + P), (N_OUT + i) % 2, mg_h[:, k, :], mg_l[:, k, :],
                                   k == 0, k == KD - 1)
                    last.then_inc(tile_full, 1)

            out_pair(0, True)
            with pe.Fori(1, 8) as p:
                out_pair(p, False)

            def up_pair(c, q):
                for i in range(2):
                    split_ready(16 * c + 2 * q + (N_MLP + i))
                    pe.wait_ge(tile_read, 24 * c + 2 * q + (T_MLP + i - 1))
                    for k in range(KD):
                        last = mm3(bank[:, i, :], slice(P * k, P * k + P), (N_MLP + i) % 2, h2_h[:, k, :], h2_l[:, k, :],
                                   k == 0, k == KD - 1)
                    last.then_inc(tile_full, 1)

            def first_up_pair():
                for i in range(2):
                    split_ready(N_MLP + i)
                    for k in range(KD):
                        if i == 0:
                            pe.wait_ge(h2_hi, k + 1)
                        wh, wl = (wsp[:, (N_MLP + i) % 2, v, P * k:P * k + P] for v in range(2))
                        nc.tensor.matmul(bank[:, i, :], wh, h2_h[:, k, :], start=(k == 0), stop=False)
                        nc.tensor.matmul(bank[:, i, :], wl, h2_h[:, k, :], start=False, stop=False)
                    if i == 0:
                        pe.wait_ge(sq_added, KD + KQ + KKV + KD)
                        sums_of(ssum)
                for i in range(2):
                    for k in range(KD):
                        if i == 0:
                            pe.wait_ge(h2_lo, k + 1)
                        if i == 1 and k == 3:
                            spread_rstd(4)
                        last = nc.tensor.matmul(bank[:, i, :], wsp[:, (N_MLP + i) % 2, 0, P * k:P * k + P], h2_l[:, k, :],
                                                start=False, stop=(k == KD - 1))
                    last.then_inc(tile_full, 1)

            def down_pair(c, q):
                for i in range(4):
                    b, j = i // 2, i % 2
                    if j == 0:
                        split_ready(16 * c + 2 * q + (N_MLP + CH + b))
                    pe.wait_ge(tile_read, 24 * c + 4 * q + (T_MLP + CH + i - 3))
                    for k in range(CH):
                        if i == 0 and k in (0, CH - 1):
                            pe.wait_ge(u_lo, CH * c + (CH - 1 if k == 0 else CH))
                        col = 256 * k + P * j
                        last = mm3(bank[:, 2 + i, :], slice(col, col + P), (N_MLP + b) % 2, u_h[:, k, :], u_l[:, k, :],
                                   k == 0, k == CH - 1)
                    last.then_inc(tile_full, 1)

            first_up_pair()
            with pe.Fori(1, 4) as q:
                up_pair(0, q)
            with pe.Fori(0, 4) as q:
                down_pair(0, q)
            with pe.Fori(1, CHUNKS) as c:
                with pe.Fori(0, 4) as q:
                    up_pair(c, q)
                with pe.Fori(0, 4) as q:
                    down_pair(c, q)
            pe.wait_ge(sq_added, KD + KQ + KKV + 2 * KD)
            pe.wait_ge(rstd_done, 4)
            sums_of(ssum)
            spread_rstd(5)

        @block.scalar
        def _(act):
            def hi(n, sl, hlf, done, width=BLK):
                act.wait_ge(raw_full[sl], hlf)
                if done is not None:
                    act.wait_ge(tile_full, done)
                nc.scalar.copy(wsp[:, sl, 0, 0:width], raw[:, sl, 0:width]).then_inc(hi_done, 1)

            def hi_at(base_n, per, i, done, width=BLK):
                n = base_n + i
                hi(None, n % 2, per * 8 + 16 * (n // 2 + 1), done, width)

            act.sem_inc(a_exp, 1)
            act.wait_ge(raw_half, 16)
            nc.scalar.copy(wsp[:, 0, 0, 0:BLK // 2], raw[:, 0, 0:BLK // 2]).then_inc(hi_half, 1)
            act.wait_ge(tab_in, 16)
            for k in range(KD):
                if k == 4:
                    act.wait_ge(raw_full[0], 16)
                    nc.scalar.copy(wsp[:, 0, 0, BLK // 2:], raw[:, 0, BLK // 2:]).then_inc(hi_done, 1)
                if k in X_CUTS:
                    act.wait_ge(x_in[X_CUTS.index(k)], 16)
                nc.scalar.activation(xg_h[:, k, :], xT[:, k, :], ACT.Copy,
                                     scale=tab[:, C_GATTN + k:C_GATTN + k + 1]).then_inc(xh_done, 1)
                if k == 7:
                    hi(1, 1, 16, None)
            for k in range(KD):
                if k >= 2:
                    act.wait_ge(sq_added, k - 1)
                nc.scalar.square(gbuf[:, k % 2, :], xT[:, k, :]).then_inc(sq_done, 1)
                if k == 7:
                    hi(2, 0, 32, 1)
            hi(3, 1, 32, 2)

            def sqrt_of(i):
                act.wait_ge(stat_read, i)
                nc.scalar.sqrt(small[:, 52:56], small[:, 48:52]).then_inc(sqrt_done, 1)
            sqrt_of(1)
            act.wait_ge(v_half, 1)
            hi(4, 0, 48, None)
            for g in range(A_KV):
                r = slice(HALF * (g % 2), HALF * (g % 2) + HALF)
                act.wait_ge(tile_read, g // 2 + 1)
                nc.scalar.copy(kd_h[r, g, :], gbuf[r, g // 2, :]).then_inc(kv_hi, 1)
            act.wait_ge(rstd_done, 1)
            for tt in range(QB):
                act.wait_ge(tile_full, 3 + tt)
                nc.scalar.activation(va[:, tt, :, 0, :], bank[:, 2 + tt, 0:256].rearrange("p (g d) -> p g d", g=A_KV), ACT.Copy,
                                     scale=small[:, 60 + tt:61 + tt]).then_inc(v_hi, 1)
            hi(5, 1, 48, T_A)
            for g in range(A_KV):
                r = slice(HALF * (g % 2), HALF * (g % 2) + HALF)
                o = slice(HALF * (1 - g % 2), HALF * (1 - g % 2) + HALF)
                act.wait_ge(kv_ready, g + 1)
                act.wait_ge(kv_hi, g + 1)
                nc.scalar.copy(kd_h[o, g, :], kd_h[r, g, :].bitcast(F32)).then_inc(kv_hi, 1)
                nc.scalar.copy(kd_l[o, g, :], kd_l[r, g, :].bitcast(F32)).then_inc(kv_hi, 1)

            def softmax_a(J, h):
                act.wait_ge(a_shift, J * 4 + h + 1)
                act.wait_ge(t_full, 1 + J * 16 + 4 * h)
                for qb in range(QB):
                    k0, k1 = key_range(qb)
                    nc.scalar.activation(pA[:, qb, 0:k1 - k0], s_sb[:, qb, 0:k1 - k0], ACT.Exp, scale=A_SCALE,
                                         bias=small[:, 8 + qb:9 + qb], accum_out=small[:, 12 + qb:13 + qb]).then_inc(a_exp, 1)
                nc.scalar.activation(small[:, 16:20], small[:, 8:12], ACT.Exp,
                                     bias=tab[:, bass.ds(J * 4 + (C_SINK + h), 1)]).then_inc(a_exp, 1)

            def turned_hi(base, h, kbs, src_n, dst):
                for kb in kbs:
                    act.wait_ge(t_full, 1 + base + (4 * h + kb + 1))
                    n = src_n(kb)
                    nc.scalar.copy(dst[:, kb, 0:n], bank[:, 4 + kb % 2, 0:n]).then_inc(pt_hi, 1)

            def a_n(kb):
                return key_range(kb)[1] - key_range(kb)[0]

            def turned_a(J, h, kbs):
                if kbs[0] == 0:
                    act.wait_ge(pv_full, 1 + J * 4 + h)
                turned_hi(J * 16, h, kbs, a_n, pTA_h)

            def half_out(count):
                act.wait_ge(pv_full, 1 + count + 1)
                act.wait_ge(o_done, 1 + count)
                nc.scalar.copy(otmp[:], bank[HALF:P, 6, :]).then_inc(pv_half, 1)

            with act.Fori(0, 4) as J:
                for jj in range(2):
                    def next_hi(i):
                        hi_at(N_A, J * 10, 5 * jj + i + 2, J * 10 + (T_A + 5 * jj + i + 1))
                    h0, h1 = 2 * jj, 2 * jj + 1
                    act.wait_ge(tile_read, J * 10 + (T_A + 5 * jj + 1))
                    act.wait_ge(s_full, 1 + J * 16 + 8 * jj)
                    nc.scalar.copy(qs[0:HALF, 0, :], qf[0:HALF, :]).then_inc(q_hi, 1)
                    nc.scalar.copy(qs[HALF:P, 1, :], qf[HALF:P, :]).then_inc(q_hi, 1)
                    next_hi(0)
                    next_hi(1)
                    softmax_a(J, h0)
                    next_hi(2)
                    turned_a(J, h0, (0, 1))
                    turned_a(J, h0, (2, 3))
                    softmax_a(J, h1)
                    next_hi(3)
                    half_out(J * 4 + h0)
                    turned_a(J, h1, (0, 1))
                    turned_a(J, h1, (2, 3))
                    half_out(J * 4 + h1)
                    next_hi(4)

            def latent_square(m, t, src):
                act.wait_ge(tile_read, T_LAT + t + 1)
                if m == 1:
                    act.wait_ge(o_done, 1 + A_HEADS)
                if m >= 2:
                    act.wait_ge(sq_added, KD + m - 1)
                nc.scalar.square(sqL[m % 2][:], src).then_inc(sq_done, 1)

            for m in range(KKV):
                latent_square(m, m, ckvf[:, m, :])
                hi_at(N_LAT, 0, m + 2, T_LAT + m + 1)
            for m in range(KQ):
                t = KKV + m
                latent_square(t, t, cqf[:, m, :])
                hi_at(N_LAT, 0, t + 2, T_LAT + t + 1)
                if m == 0:
                    sqrt_of(2)
                    for k in range(KKV):
                        act.wait_ge(lat_norm, k + 1)
                        nc.scalar.activation(ckv_h[:, k, :], ckvf[:, k, :], ACT.Copy,
                                             scale=tab[:, C_GKV + k:C_GKV + k + 1]).then_inc(lat_hi, 1)
                    act.wait_ge(ang_ready, 1)
                    nc.scalar.activation(t_hi[:], ang[:], ACT.Sin, scale=0.5).then_inc(sin_done, 1)
                    nc.scalar.activation(t_lo[:], turns[:], ACT.Sin).then_inc(sin_done, 1)
            sqrt_of(3)

            def project_hi(kind, g):
                n, b = place(kind, g)
                act.wait_ge(tile_full, 7 * g + (T_B + n))
                i = int(kind[1])
                if kind[0] == "v":
                    if not (isinstance(g, int) and g == 0):
                        act.wait_ge(pv_full, 4 * g + (1 + A_HEADS))
                    nc.scalar.copy(vb[:, 2 * i:2 * i + 2, :, 0, :].rearrange("p t e d -> p (t e) d"),
                                   bank[:, b, :].rearrange("p (a d) -> p a d", d=HALF)).then_inc(v_hi, 1)
                    return
                if not isinstance(g, int):
                    act.wait_ge(s_full, 16 * g + (1 + 4 * A_HEADS - 16 + 8 * i + 8))
                for e in range(2):
                    r = slice(HALF * e, HALF * e + HALF)
                    nc.scalar.copy((q_h if kind[0] == "q" else k_h)[r, 2 * i + e, :], bank[r, b, :]).then_inc(b_hi, 1)

            def rope_hi(g):
                act.wait_ge(r_sum, g + 1)
                nc.scalar.copy(rope_h[:], rope_a[:]).then_inc(r_hi, 1)

            def softmax_b(g, e):
                act.wait_ge(a_shift, 4 * g + (A_HEADS + e + 1))
                act.wait_ge(t_full, 16 * g + (1 + 4 * A_HEADS + 4 * e - 4))
                for qb in range(QB):
                    nc.scalar.activation(pB[e % 2][:, qb, :], bank[:, qb, :], ACT.Exp, scale=B_SCALE,
                                         bias=small[:, 8 + qb:9 + qb], accum_out=small[:, 12 + qb:13 + qb]).then_inc(a_exp, 1)

            def turned_b(g, e, kbs):
                if kbs[0] == 0:
                    act.wait_ge(pv_full, 4 * g + (1 + A_HEADS + e))
                turned_hi(16 * g + 4 * A_HEADS, e, kbs, lambda kb: S, pTB_h)

            def b_group(g, more):
                for e in range(4):
                    if more and FILL_0[e]:
                        project_hi(FILL_0[e], g + 1)
                    if e > 0:
                        half_out(4 * g + (A_HEADS + e - 1))
                    else:
                        project_hi("v1", g)
                    turned_b(g, e, (0, 1))
                    if e == 0:
                        hi_at(N_B, 2 * g, 3, 7 * g + (T_B + 7), 1024 if more else BLK)
                    if e < 3:
                        softmax_b(g, e + 1)
                    elif more:
                        softmax_b(g + 1, 0)
                    if more and e in (1, 2):
                        project_hi(FILL_1[e], g + 1)
                    turned_b(g, e, (2, 3))
                    if more and e == 0:
                        rope_hi(g + 1)
                    if more and e == 3:
                        hi_at(N_B, 2 * g, 4, 7 * g + (T_B + 7 + place("q1", g + 1)[0]))
                half_out(4 * g + (A_HEADS + 3))
                if more:
                    project_hi("v0", g + 1)

            hi_at(N_LAT, 0, KKV + KQ + 2, T_LAT + KKV + KQ + 1, 1024)
            for k in range(KQ):
                act.wait_ge(lat_norm, KKV + k + 1)
                nc.scalar.activation(cq_h[:, k, :], cqf[:, k, :], ACT.Copy,
                                     scale=tab[:, C_GQ + k:C_GQ + k + 1]).then_inc(lat_hi, 1)
            for kind in ("k0", "k1", "v0"):
                project_hi(kind, 0)
            act.wait_ge(kr_ready, 1)
            act.wait_ge(gate_out[0], 16 * 16)
            act.wait_ge(gate_out[1], 16 * 16)
            nc.scalar.copy(rope_h[0:ROPE, :], rope_a[0:ROPE, :]).then_inc(kr_split, 1)
            act.wait_ge(kr_split, 2)
            for e in range(4):
                to = HALF if e % 2 == 0 else 32
                nc.scalar.copy(k_l[to:to + ROPE, e, :], rope_l[0:ROPE, :].bitcast(F32)).then_inc(kr_spread, 1)
                nc.scalar.copy(k_h[to:to + ROPE, e, :], rope_h[0:ROPE, :].bitcast(F32)).then_inc(kr_spread, 1)
            act.wait_ge(kr_spread, 8)
            project_hi("q0", 0)
            rope_hi(0)
            act.wait_ge(r_hi, 1)
            for e in range(2):
                to = HALF if e % 2 == 0 else 32
                nc.scalar.copy(q_h[to:to + ROPE, e, :], rope_h[32 * e:32 * e + 32, :].bitcast(F32)).then_inc(r_first_hi, 1)
            project_hi("q1", 0)
            softmax_b(0, 0)
            hi_at(N_B, 0, 2, T_B + 6, 1536)
            with act.Fori(0, GROUPS - 1) as g:
                b_group(g, True)
            b_group(GROUPS - 1, False)

            for k in range(8):
                nc.scalar.copy(oA_h[:, k, :], oA[:, k, :]).then_inc(o_hi, 1)
            for k in range(8):
                act.wait_ge(o_done, 1 + A_HEADS + 2 * k + 2)
                nc.scalar.copy(oB_h[:, k, :], oB[:, k, :]).then_inc(o_hi, 1)

            def sig(p, b):
                act.wait_ge(gate_in[b], 16 * p + 16)
                act.wait_ge(tile_read, 4 * p + (T_BR - 2 + 2 * b))
                nc.scalar.activation(sg[:, b], gl[:, b], ACT.Sigmoid).then_inc(gate_sig, 1)

            act.wait_ge(o_lo, 8)
            with act.Fori(0, 8) as p:
                sig(p, 0)
                sig(p, 1)
                hi_at(N_BR, 2 * p, 2, 4 * p + (T_BR + 2))
                for i in range(2):
                    act.wait_ge(merged, 2 * p + (i + 1))
                    nc.scalar.copy(mg_h[:, bass.ds(2 * p + i, 1), :], tmp[:, i:i + 1, :]).then_inc(mg_hi, 1)
                hi_at(N_BR, 2 * p, 3, 4 * p + (T_BR + 4))

            with act.Fori(0, 8) as p:
                for i in range(2):
                    act.wait_ge(tile_read, 2 * p + (T_OUT + i + 1))
                    act.wait_ge(sq_added, 2 * p + (KD + KQ + KKV + i - 1))
                    nc.scalar.activation(h2_h[:, bass.ds(2 * p + i, 1), :].rearrange("p a s -> p (a s)"),
                                         x2[:, bass.ds(2 * p + i, 1), :].rearrange("p a s -> p (a s)"), ACT.Copy,
                                         scale=tab[:, bass.ds(2 * p + (C_GMLP + i), 1)]).then_inc(h2_hi, 1)
                    nc.scalar.square(sq[:, i, :].rearrange("p (a s) -> p a s", a=1), x2[:, bass.ds(2 * p + i, 1), :]).then_inc(sq_done, 1)
                    hi_at(N_OUT, 2 * p, 2 + i, 2 * p + (T_OUT + i + 1))

            def up(c, q, first=False):
                for i in range(2):
                    if first:
                        hi_at(N_MLP, 0, 2 + i, T_MLP + i + 1)
                    act.wait_ge(u_sq, CH * c + 2 * q + (i + 1))
                    nc.scalar.copy(u_h[:, bass.ds(2 * q + i, 1), :], uu[:].rearrange("p (a s) -> p a s", a=1)).then_inc(u_hi, 1)
                    if not first:
                        hi_at(N_MLP, 16 * c + 2 * q, 2 + i, 24 * c + 2 * q + (T_MLP + i + 1))

            def down(c, q, last=False):
                for b in range(2):
                    if last:
                        for j in range(2):
                            m = 4 * q + 2 * b + j
                            act.wait_ge(tile_read, T_END - KD + m + 1)
                            act.wait_ge(sq_added, KD + KQ + KKV + KD + m - 1)
                            nc.scalar.square(sq[:, j, :], x2[:, m, :]).then_inc(sq_done, 1)
                            nc.scalar.activation(outT[:, m, :], x2[:, m, :], ACT.Copy,
                                                 scale=tab[:, C_GFIN + m:C_GFIN + m + 1]).then_inc(fin_gain, 1)
                    if not (last and q == 3):
                        hi_at(N_MLP + CH, 16 * c + 2 * q, 2 + b, 24 * c + 4 * q + (T_MLP + CH + 2 * b + 2))

            sqrt_of(4)
            up(0, 0, True)
            with act.Fori(1, 4) as q:
                up(0, q)
            with act.Fori(0, 4) as q:
                down(0, q)
            with act.Fori(1, CHUNKS - 1) as c:
                with act.Fori(0, 4) as q:
                    up(c, q)
                with act.Fori(0, 4) as q:
                    down(c, q)
            with act.Fori(0, 4) as q:
                up(CHUNKS - 1, q)
            for q in range(4):
                down(CHUNKS - 1, q, True)
            sqrt_of(5)

        @block.vector
        def _(dve):
            V = nc.vector
            links = [0]

            def link(ins):
                links[0] += 1
                ins.then_inc(chain, 1)
                dve.wait_ge(chain, links[0])

            def lo_at(base_n, per, i, width=BLK):
                n = base_n + i
                dve.wait_ge(hi_done, per + (n + 1))
                if n > 0:
                    dve.wait_ge(lo_done, per + n)
                V.tensor_tensor(wsp[:, n % 2, 1, 0:width], raw[:, n % 2, 0:width], wsp[:, n % 2, 0, 0:width].bitcast(F32),
                                ALU.subtract).then_inc(lo_done, 1)

            def rms(i, count, dst, beside=None):
                mean, root, work, r = (small[:, c:c + QB] for c in (48, 52, 56, 60))
                dve.wait_ge(stat_full, i)
                V.tensor_scalar(mean, bank[:, 7, 0:QB], 1.0 / count, EPS, ALU.mult, ALU.add).then_inc(stat_read, 1)
                dve.wait_ge(sqrt_done, i)
                link(V.reciprocal(r, root))
                link(V.tensor_tensor(work, r, r, ALU.mult))
                dve.wait_ge(stat_read, i)
                link(V.tensor_tensor(work, work, mean, ALU.mult))
                link(V.tensor_scalar(work, work, -0.5, 1.5, ALU.mult, ALU.add))
                link(V.tensor_tensor(r, r, work, ALU.mult))
                for tt in range(QB):
                    V.tensor_scalar(tmp[:, 1, P * tt:P * tt + P], ident, small[:, 60 + tt:61 + tt], None, ALU.mult).then_inc(
                        diag_ready, 1)
                if beside:
                    beside()
                dve.wait_ge(rstd_full, i)
                V.tensor_copy(dst, bank[:, 7, :]).then_inc(rstd_done, 1)
                dve.wait_ge(rstd_done, i)

            def add_square(total, src, count, first):
                dve.wait_ge(sq_done, count)
                if first:
                    V.tensor_copy(total, src).then_inc(sq_added, 1)
                else:
                    dve.wait_ge(sq_added, count - 1)
                    V.tensor_tensor(total, total, src, ALU.add).then_inc(sq_added, 1)

            for s in (s_read, pt_lo, o_done, mg_lo):
                dve.sem_inc(s, 1)
            dve.wait_ge(hi_half, 1)
            V.tensor_tensor(wsp[:, 0, 1, 0:BLK // 2], raw[:, 0, 0:BLK // 2], wsp[:, 0, 0, 0:BLK // 2].bitcast(F32),
                            ALU.subtract).then_inc(lo_half, 1)
            dve.wait_ge(tab_in, 16)
            for k in range(KD):
                if k == 4:
                    dve.wait_ge(hi_done, 1)
                    V.tensor_tensor(wsp[:, 0, 1, BLK // 2:], raw[:, 0, BLK // 2:], wsp[:, 0, 0, BLK // 2:].bitcast(F32),
                                    ALU.subtract).then_inc(lo_done, 1)
                dve.wait_ge(xh_done, k + 1)
                V.scalar_tensor_tensor(xg_l[:, k, :], xT[:, k, :], tab[:, C_GATTN + k:C_GATTN + k + 1],
                                       xg_h[:, k, :].bitcast(F32), ALU.mult, ALU.subtract).then_inc(xl_done, 1)
                if k == 9:
                    lo_at(0, 0, 1)
            for k in range(KD):
                add_square(tmp[:, 0, :], gbuf[:, k % 2, :], k + 1, k == 0)
                if k == 9:
                    lo_at(0, 0, 2)
            lo_at(0, 0, 3)
            rms(1, D, rstd[:], lambda: lo_at(0, 0, 4))
            for i in range(2):
                dve.wait_ge(tile_full, i + 1)
                V.tensor_tensor(gbuf[:, i, :], bank[:, i, :], rstd[:], ALU.mult).then_inc(tile_read, 1)
            for g in range(A_KV):
                r = slice(HALF * (g % 2), HALF * (g % 2) + HALF)
                dve.wait_ge(kv_hi, g + 1)
                dve.wait_ge(tile_read, g // 2 + 1)
                V.tensor_tensor(kd_l[r, g, :], gbuf[r, g // 2, :], kd_h[r, g, :].bitcast(F32), ALU.subtract).then_inc(kv_ready, 1)
            for tt in range(QB):
                dve.wait_ge(v_hi, tt + 1)
                V.scalar_tensor_tensor(va[:, tt, :, 1, :], bank[:, 2 + tt, 0:256].rearrange("p (g d) -> p g d", g=A_KV),
                                       small[:, 60 + tt:61 + tt], va[:, tt, :, 0, :].bitcast(F32), ALU.mult, ALU.subtract).then_inc(
                    tile_read, 1)
            lo_at(0, 0, 5)
            dve.wait_ge(pos_in, 16)
            link(V.tensor_copy(small[:, 28:32], pos_a[:, S:S + QB]))
            V.tensor_scalar(small[:, 32:48], tab[:, C_SINK:C_SINK + A_HEADS], -1.0, None, ALU.mult).then_inc(neg_ready, 1)
            dve.wait_ge(mask_in, 16)
            for qb in range(QB):
                k0, k1 = key_range(qb)
                n = k1 - k0
                link(V.tensor_scalar(dist_t[:, 0:n], pos_a[:, k0:k1], small[:, 28 + qb:29 + qb], None, ALU.subtract))
                link(V.scalar_tensor_tensor(dist_t[:, 0:n], dist_t[:, 0:n], -1.0, dist_t[:, 0:n], ALU.mult, ALU.max))
                link(V.tensor_tensor(dist[:, qb, 0:n], dist[:, qb, 0:n], dist_t[:, 0:n], ALU.add))

            def gate_tile(J, jj, i):
                t = 5 * jj + i
                dve.wait_ge(tile_full, J * 10 + (T_A + t + 1))
                if jj or i > 2:
                    dve.wait_ge(gate_out[(i - 1) % 2], J * 64 + 16 * (2 * jj + (i - 1) // 2))
                V.tensor_tensor(gbuf[:, (i - 1) % 2, :], bank[:, (3, 7)[t % 2], :], rstd[:], ALU.mult).then_inc(tile_read, 1)

            def maximum(before, h):
                dve.wait_ge(s_read, 1 + before * 4 + (4 * h + 4))
                V.tensor_reduce(small[:, 4:8], s_sb[:], AX_X, ALU.max).then_inc(a_max, 1)
                dve.wait_ge(a_max, before + (h + 1))

            def biased(J, h):
                if h == 0:
                    dve.wait_ge(pad_set, 2)
                for n, qb in enumerate(A_ORDER):
                    dve.wait_ge(s_full, 1 + J * 16 + (4 * h + max(n + 1, 2)))
                    if n == 0:
                        dve.wait_ge(a_exp, 1 + J * 20 + 5 * h)
                    k0, k1 = key_range(qb)
                    b, c = A_BANK[qb]
                    V.scalar_tensor_tensor(s_sb[:, qb, 0:k1 - k0], dist[:, qb, 0:k1 - k0],
                                           tab[:, bass.ds(J * 4 + (C_SLOPE + h), 1)], bank[:, b, c:c + k1 - k0],
                                           ALU.mult, ALU.add).then_inc(s_read, 1)
                maximum(J * 4, h)
                V.tensor_scalar(small[:, 8:12], small[:, 4:8], -A_SCALE, small[:, bass.ds(J * 4 + (32 + h), 1)],
                                ALU.mult, ALU.min).then_inc(a_shift, 1)

            def normalise_a(J, h):
                dve.wait_ge(a_exp, 1 + J * 20 + (5 * h + 5))
                V.tensor_tensor(small[:, 20:24], small[:, 12:16], small[:, 16:20], ALU.add).then_inc(a_den, 1)
                dve.wait_ge(a_den, J * 8 + (2 * h + 1))
                V.reciprocal(small[:, 24:28], small[:, 20:24]).then_inc(a_den, 1)
                dve.wait_ge(a_den, J * 8 + (2 * h + 2))
                for qb in range(QB):
                    n = key_range(qb)[1] - key_range(qb)[0]
                    V.tensor_scalar(pA[:, qb, 0:n], pA[:, qb, 0:n], small[:, 24 + qb:25 + qb], None, ALU.mult).then_inc(p_ready, 1)

            def turned_lo(base, h, kbs, width, hi_t, lo_t):
                for kb in kbs:
                    dve.wait_ge(pt_hi, base + (4 * h + kb + 1))
                    n = width(kb)
                    V.tensor_tensor(lo_t[:, kb, 0:n], bank[:, 4 + kb % 2, 0:n], hi_t[:, kb, 0:n].bitcast(F32),
                                    ALU.subtract).then_inc(pt_lo, 1)

            def a_n(kb):
                return key_range(kb)[1] - key_range(kb)[0]

            def out_sum(dst, count, e):
                dve.wait_ge(pv_half, count + 1)
                V.tensor_tensor(dst, bank[0:HALF, 6, :], otmp[:], ALU.add).then_inc(o_done, 1)

            dve.wait_ge(neg_ready, 1)
            with dve.Fori(0, 4) as J:
                for jj in range(2):
                    h0, h1 = 2 * jj, 2 * jj + 1
                    dve.wait_ge(tile_full, J * 10 + (T_A + 5 * jj + 1))
                    V.tensor_tensor(qf[:], bank[:, (3, 7)[5 * jj % 2], :], rstd[:], ALU.mult).then_inc(tile_read, 1)
                    dve.wait_ge(q_hi, J * 4 + (2 * jj + 2))
                    dve.wait_ge(tile_read, J * 10 + (T_A + 5 * jj + 1))
                    V.tensor_tensor(qs[HALF:P, 0, :], qf[0:HALF, :], qs[0:HALF, 0, :].bitcast(F32), ALU.subtract).then_inc(q_ready, 1)
                    V.tensor_tensor(qs[0:HALF, 1, :], qf[HALF:P, :], qs[HALF:P, 1, :].bitcast(F32), ALU.subtract).then_inc(q_ready, 1)

                    def next_lo(i):
                        lo_at(N_A, J * 10, 5 * jj + i + 2)

                    def out_a(h):
                        out_sum(oA[HALF * (h % 2):HALF * (h % 2) + HALF, bass.ds(J * 2 + h // 2, 1), :].rearrange("p a s -> p (a s)"),
                                J * 4 + h, h)
                    next_lo(0)
                    gate_tile(J, jj, 1)
                    biased(J, h0)
                    next_lo(1)
                    normalise_a(J, h0)
                    gate_tile(J, jj, 2)
                    turned_lo(J * 16, h0, (0, 1), a_n, pTA_h, pTA_l)
                    next_lo(2)
                    turned_lo(J * 16, h0, (2, 3), a_n, pTA_h, pTA_l)
                    biased(J, h1)
                    gate_tile(J, jj, 3)
                    normalise_a(J, h1)
                    out_a(h0)
                    next_lo(3)
                    turned_lo(J * 16, h1, (0, 1), a_n, pTA_h, pTA_l)
                    turned_lo(J * 16, h1, (2, 3), a_n, pTA_h, pTA_l)
                    out_a(h1)
                    gate_tile(J, jj, 4)
                    next_lo(4)
                for b in range(2):
                    dve.wait_ge(gate_out[b], J * 64 + 64)

            def angles():
                magic = 1.5 * 2.0 ** 23
                dve.wait_ge(pos_in, 32)
                link(V.tensor_copy(posf[:], pos_i[:]))
                link(V.tensor_scalar(ang[:], posf[:], tab[:, C_INVF:C_INVF + 1], None, ALU.mult))
                link(V.tensor_scalar(turns[:], ang[:], 0.15915494309189535, magic, ALU.mult, ALU.add))
                link(V.tensor_scalar(turns[:], turns[:], magic, None, ALU.subtract))
                link(V.tensor_scalar(t_hi[:], turns[:], magic * 2048, None, ALU.add))
                link(V.tensor_scalar(t_hi[:], t_hi[:], magic * 2048, None, ALU.subtract))
                link(V.tensor_tensor(t_lo[:], turns[:], t_hi[:], ALU.subtract))
                for part in TWO_PI_PARTS:
                    for t in (t_hi, t_lo):
                        link(V.scalar_tensor_tensor(ang[:], t[:], -part, ang[:], ALU.mult, ALU.add))
                link(V.scalar_tensor_tensor(turns[:], ang[:], -1.0, ang[:], ALU.mult, ALU.max))
                V.tensor_scalar(turns[:], turns[:], -0.5, 1.5707963267948966, ALU.mult, ALU.add).then_inc(ang_ready, 1)

            def latent_read(dst, t, b):
                dve.wait_ge(tile_full, T_LAT + t + 1)
                V.tensor_tensor(dst, bank[:, b, :], rstd[:], ALU.mult).then_inc(tile_read, 1)

            def latent_split(x, hi_t, lo_t, gain, n, before, beside=None):
                for k in range(n):
                    V.tensor_tensor(x[:, k, :], x[:, k, :], lat_rstd[:], ALU.mult).then_inc(lat_norm, 1)
                if beside:
                    beside()
                for k in range(n):
                    dve.wait_ge(lat_norm, before + k + 1)
                    dve.wait_ge(lat_hi, before + k + 1)
                    V.scalar_tensor_tensor(lo_t[:, k, :], x[:, k, :], tab[:, gain + k:gain + k + 1],
                                           hi_t[:, k, :].bitcast(F32), ALU.mult, ALU.subtract).then_inc(lat_lo, 1)

            for m in range(KKV):
                latent_read(ckvf[:, m, :], m, m)
                lo_at(N_LAT, 0, m + 2)
                add_square(sumsq[:], sqL[m % 2][:], KD + m + 1, m == 0)
            angles()
            for m in range(KQ):
                t = KKV + m
                latent_read(cqf[:, m, :], t, t)
                if m < KQ - 1:
                    lo_at(N_LAT, 0, t + 2)
                if m == 0:
                    dve.wait_ge(stat_full, 2)
                add_square(sumsq[:], sqL[t % 2][:], KD + t + 1, m == 0)
                if m == 0:
                    rms(2, KV_LORA, lat_rstd[:])
                    latent_split(ckvf, ckv_h, ckv_l, C_GKV, KKV, 0)
                if m == 1:
                    dve.wait_ge(sin_done, 2)
                    link(V.tensor_tensor(cosb[:], t_hi[:], t_hi[:], ALU.mult))
                    link(V.tensor_scalar(cosb[:], cosb[:], -2.0, 1.0, ALU.mult, ALU.add))
                    link(V.tensor_tensor(sinb[:], t_hi[:], t_lo[:], ALU.mult))
                    link(V.tensor_scalar(sinb[:], sinb[:], tab[:, C_SIGN:C_SIGN + 1], 2.0, ALU.mult, ALU.mult))
            lo_at(N_LAT, 0, KKV + KQ + 1)
            rms(3, Q_LORA, lat_rstd[:])
            latent_split(cqf, cq_h, cq_l, C_GQ, KQ, KKV, lambda: lo_at(N_LAT, 0, KKV + KQ + 2, 1024))
            dve.wait_ge(tile_full, T_B)
            r0 = slice(0, ROPE)
            swap = [(i + 16) % 32 for i in range(32)]
            V.tensor_tensor(rope_a[r0, :], bank[r0, 6, :], rstd[r0, :], ALU.mult).then_inc(tile_read, 1)
            dve.wait_ge(tile_read, T_B)
            link(V.stream_shuffle(rope_b[r0, :], rope_a[r0, :], swap))
            link(V.tensor_tensor(rope_b[r0, :], rope_b[r0, :], sinb[r0, :], ALU.mult))
            link(V.tensor_tensor(rope_a[r0, :], rope_a[r0, :], cosb[r0, :], ALU.mult))
            V.tensor_tensor(rope_a[r0, :], rope_a[r0, :], rope_b[r0, :], ALU.add).then_inc(kr_ready, 1)
            dve.wait_ge(kr_split, 1)
            V.tensor_tensor(rope_l[r0, :], rope_a[r0, :], rope_h[r0, :].bitcast(F32), ALU.subtract).then_inc(kr_split, 1)

            def project_lo(kind, g):
                n, b = place(kind, g)
                i = int(kind[1])
                if kind[0] == "v":
                    dve.wait_ge(v_hi, 2 * g + (QB + i + 1))
                    V.tensor_tensor(vb[:, 2 * i:2 * i + 2, :, 1, :].rearrange("p t e d -> p (t e) d"),
                                    bank[:, b, :].rearrange("p (a d) -> p a d", d=HALF),
                                    vb[:, 2 * i:2 * i + 2, :, 0, :].rearrange("p t e d -> p (t e) d").bitcast(F32),
                                    ALU.subtract).then_inc(tile_read, 1)
                    return
                hi_t, lo_t = (q_h, q_l) if kind[0] == "q" else (k_h, k_l)
                order = [x for x in (FIRST_ORDER if isinstance(g, int) else NEXT_ORDER) if x[0] in "qk"]
                dve.wait_ge(b_hi, 8 * g + 2 * (order.index(kind) + 1))
                for e in range(2):
                    r = slice(HALF * e, HALF * e + HALF)
                    V.tensor_tensor(lo_t[r, 2 * i + e, :], bank[r, b, :], hi_t[r, 2 * i + e, :].bitcast(F32),
                                    ALU.subtract).then_inc((b_lo, tile_read)[e], 1)

            def rotate(g):
                n = place("r", g)[0]
                dve.wait_ge(tile_full, 7 * g + (T_B + n))
                if not isinstance(g, int):
                    dve.wait_ge(r_moved[1], 64 * g)
                V.tensor_tensor(rope_a[:], bank[:, 7, :], cosb[:], ALU.mult).then_inc(r_part, 1)
                V.stream_shuffle(rope_b[:], bank[:, 7, :], swap).then_inc(tile_read, 1)
                dve.wait_ge(tile_read, 7 * g + (T_B + (1 if isinstance(g, int) else n)))
                V.tensor_tensor(rope_b[:], rope_b[:], sinb[:], ALU.mult).then_inc(r_part, 1)
                dve.wait_ge(r_part, 2 * g + 2)
                V.tensor_tensor(rope_a[:], rope_a[:], rope_b[:], ALU.add).then_inc(r_sum, 1)

            def rotate_lo(g):
                dve.wait_ge(r_hi, g + 1)
                V.tensor_tensor(rope_l[:], rope_a[:], rope_h[:].bitcast(F32), ALU.subtract).then_inc(r_lo, 1)

            def maximum_b(g, e):
                dve.wait_ge(s_full, 1 + 16 * g + (4 * A_HEADS + 4 * e + 4))
                V.tensor_reduce(small[:, 4:8], bank[:, 0:QB, :], AX_X, ALU.max).then_inc(a_max, 1)
                dve.wait_ge(a_max, 4 * g + (A_HEADS + e + 1))
                V.tensor_scalar(small[:, 8:12], small[:, 4:8], -B_SCALE, None, ALU.mult).then_inc(a_shift, 1)

            def normalise_b(g, e):
                dve.wait_ge(a_exp, 1 + 16 * g + (5 * A_HEADS + 4 * e + 4))
                if not (isinstance(g, int) and 4 * g + e == 0):
                    dve.wait_ge(p_ready2, 4 * g + e)
                V.reciprocal(small[:, 24:28], small[:, 12:16]).then_inc(a_den, 1)
                dve.wait_ge(a_den, 4 * g + (2 * A_HEADS + e + 1))
                for qb in range(QB - 1):
                    V.tensor_scalar(pB[e % 2][:, qb, :], pB[e % 2][:, qb, :], small[:, 24 + qb:25 + qb], None, ALU.mult).then_inc(p_ready, 1)

            def lo_b(g, e, kbs):
                turned_lo(16 * g + 4 * A_HEADS, e, kbs, lambda kb: S, pTB_h, pTB_l)

            def out_b(g, e):
                r = slice(HALF * (e % 2), HALF * (e % 2) + HALF)
                if isinstance(g, int):
                    dst = oB[r, 2 * g + e // 2, :]
                else:
                    dst = oB[r, bass.ds(2 * g + e // 2, 1), :].rearrange("p a s -> p (a s)")
                out_sum(dst, 4 * g + (A_HEADS + e), e)

            def b_group(g, more):
                for e in range(4):
                    following = (g, e + 1) if e < 3 else (g + 1, 0) if more else None
                    if more and e == 1:
                        project_lo(FILL_0[e], g + 1)
                    if following:
                        maximum_b(*following)
                    if more and e == 2:
                        project_lo(FILL_0[e], g + 1)
                    if more and e == 1:
                        rotate_lo(g + 1)
                    if e > 0:
                        out_b(g, e - 1)
                    else:
                        project_lo("v1", g)
                    lo_b(g, e, (0, 1))
                    if more and e == 0:
                        rotate(g + 1)
                    if following:
                        normalise_b(*following)
                    if more and e in (1, 2):
                        project_lo(FILL_1[e], g + 1)
                    lo_b(g, e, (2, 3))
                out_b(g, 3)
                if more:
                    project_lo("v0", g + 1)

            dve.wait_ge(kr_split, 2)
            rotate(0)
            for kind in ("k0", "k1", "v0", "q0"):
                project_lo(kind, 0)
            dve.wait_ge(kr_spread, 8)
            rotate_lo(0)
            dve.wait_ge(r_lo, 1)
            for e in range(2):
                to = HALF if e % 2 == 0 else 32
                V.tensor_copy(q_l[to:to + ROPE, e, :], rope_l[32 * e:32 * e + 32, :].bitcast(F32)).then_inc(r_first_lo, 1)
            project_lo("q1", 0)
            maximum_b(0, 0)
            normalise_b(0, 0)
            with dve.Fori(0, GROUPS - 1) as g:
                b_group(g, True)
            b_group(GROUPS - 1, False)

            for b, (o, oh, ol) in enumerate(((oA, oA_h, oA_l), (oB, oB_h, oB_l))):
                for k in range(8):
                    dve.wait_ge(o_hi, 8 * b + k + 1)
                    V.tensor_tensor(ol[:, k, :], o[:, k, :], oh[:, k, :].bitcast(F32), ALU.subtract).then_inc(o_lo, 1)
            with dve.Fori(0, 8) as p:
                for i in range(2):
                    dve.wait_ge(tile_full, 4 * p + (T_BR + i + 1))
                    dve.wait_ge(gate_sig, 2 * p + 1)
                    dve.wait_ge(mg_lo, 1 + 2 * p)
                    V.tensor_tensor(tmp[:, i, :], bank[:, i, :], sg[:, 0, i, :], ALU.mult).then_inc(tile_read, 1)
                lo_at(N_BR, 2 * p, 2)
                for i in range(2):
                    dve.wait_ge(tile_full, 4 * p + (T_BR + i + 3))
                    dve.wait_ge(gate_sig, 2 * p + 2)
                    V.tensor_tensor(mt[:], bank[:, 2 + i, :], sg[:, 1, i, :], ALU.mult).then_inc(tile_read, 1)
                    dve.wait_ge(tile_read, 4 * p + (T_BR + i + 3))
                    V.tensor_tensor(tmp[:, i, :], tmp[:, i, :], mt[:], ALU.add).then_inc(merged, 1)
                    dve.wait_ge(merged, 2 * p + (i + 1))
                    dve.wait_ge(mg_hi, 2 * p + (i + 1))
                    V.tensor_tensor(mg_l[:, bass.ds(2 * p + i, 1), :], tmp[:, i:i + 1, :],
                                    mg_h[:, bass.ds(2 * p + i, 1), :].bitcast(F32), ALU.subtract).then_inc(mg_lo, 1)
                lo_at(N_BR, 2 * p, 3)

            link(V.memset(ssum[:], 0.0))
            with dve.Fori(0, 8) as p:
                for i in range(2):
                    dve.wait_ge(tile_full, 2 * p + (T_OUT + i + 1))
                    if i == 0:
                        dve.wait_ge(xin_in, 16 * p + 16)
                    V.tensor_tensor(x2[:, bass.ds(2 * p + i, 1), :], bank[:, 4 + i:5 + i, :], xin[:, i:i + 1, :],
                                    ALU.add).then_inc(tile_read, 1)
                    lo_at(N_OUT, 2 * p, 2 + i)
                    dve.wait_ge(sq_done, 2 * p + (KD + KQ + KKV + i + 1))
                    dve.wait_ge(sq_added, 2 * p + (KD + KQ + KKV + i))
                    V.tensor_tensor(ssum[:], ssum[:], sq[:, i, :], ALU.add).then_inc(sq_added, 1)
            for k in range(KD):
                dve.wait_ge(tile_full, T_MLP)
                dve.wait_ge(h2_hi, k + 1)
                V.scalar_tensor_tensor(h2_l[:, k, :], x2[:, k, :], tab[:, C_GMLP + k:C_GMLP + k + 1],
                                       h2_h[:, k, :].bitcast(F32), ALU.mult, ALU.subtract).then_inc(h2_lo, 1)
            rms(4, D, rstd[:])

            def up(c, q, first=False):
                for i in range(2):
                    n = CH * c + 2 * q + (i + 1)
                    dve.wait_ge(tile_full, 24 * c + 2 * q + (T_MLP + i + 1))
                    V.scalar_tensor_tensor(ru[:], bank[:, i, :], 0.0, rstd[:], ALU.max, ALU.mult).then_inc(tile_read, 1)
                    dve.wait_ge(tile_read, 24 * c + 2 * q + (T_MLP + i + 1))
                    V.tensor_tensor(uu[:], ru[:], ru[:], ALU.mult).then_inc(u_sq, 1)
                    if first:
                        lo_at(N_MLP, 0, 2 + i)
                    dve.wait_ge(u_sq, n)
                    dve.wait_ge(u_hi, n)
                    V.tensor_tensor(u_l[:, bass.ds(2 * q + i, 1), :], uu[:].rearrange("p (a s) -> p a s", a=1),
                                    u_h[:, bass.ds(2 * q + i, 1), :].bitcast(F32), ALU.subtract).then_inc(u_lo, 1)
                    if not first:
                        lo_at(N_MLP, 16 * c + 2 * q, 2 + i)

            def down(c, q, last=False):
                for b in range(2):
                    for j in range(2):
                        i = 2 * b + j
                        dve.wait_ge(tile_full, 24 * c + 4 * q + (T_MLP + CH + i + 1))
                        at_m = x2[:, bass.ds(4 * q + i, 1), :]
                        V.tensor_tensor(at_m, bank[:, 2 + i:3 + i, :], at_m, ALU.add).then_inc(tile_read, 1)
                    if not (last and q == 3):
                        lo_at(N_MLP + CH, 16 * c + 2 * q, 2 + b)
                    if last:
                        for j in range(2):
                            m = 4 * q + 2 * b + j
                            add_square(ssum[:], sq[:, j, :], 2 * KD + KQ + KKV + m + 1, m == 0)

            up(0, 0, True)
            with dve.Fori(1, 4) as q:
                up(0, q)
            with dve.Fori(0, 4) as q:
                down(0, q)
            with dve.Fori(1, CHUNKS - 1) as c:
                with dve.Fori(0, 4) as q:
                    up(c, q)
                with dve.Fori(0, 4) as q:
                    down(c, q)
            with dve.Fori(0, 4) as q:
                up(CHUNKS - 1, q)
            for q in range(4):
                down(CHUNKS - 1, q, True)
            rms(5, D, rstd[:])
            for m in range(KD):
                dve.wait_ge(fin_gain, m + 1)
                V.tensor_tensor(outT[:, m, :], outT[:, m, :], rstd[:], ALU.mult).then_inc(fin_ready, 1)


def layout(inputs):
    import numpy as np
    f = np.float32

    def rows(w, width):
        return w.reshape(w.shape[0] // P, P, w.shape[1] // width, width)

    w_in = np.asarray(inputs["w_in"])[0]
    cuts = np.cumsum([1024, 256, 256, Q_LORA, KV_LORA, ROPE, D])
    qa, ka, va, cq, ckv, kr, ga, gb = np.split(w_in, cuts, axis=1)
    W = np.zeros((N_END, P, BLK), f)

    def cols(w):
        return rows(w, P).transpose(2, 1, 0, 3).reshape(-1, P, BLK)

    W[0:2] = cols(ka)
    W[2:4] = va.reshape(2, 8, P, 256).transpose(0, 2, 1, 3).reshape(2, P, BLK)
    a = W[N_A:N_LAT].reshape(8, 5, P, BLK)
    a[:, 0] = cols(qa)
    a[:, 1:] = np.concatenate([cols(ga), cols(gb)]).reshape(8, 4, P, BLK)
    W[N_LAT:N_LAT + KKV] = cols(ckv)
    W[N_LAT + KKV:N_B - 1] = cols(cq)
    W[N_B - 1][:, :KD * ROPE] = kr.reshape(KD, P, ROPE).transpose(1, 0, 2).reshape(P, -1)
    uq, uk, uv = (np.asarray(inputs[n])[0] for n in ("b_w_uq", "b_w_uk", "b_w_uv"))
    for g in range(GROUPS):
        hs = slice(4 * g, 4 * g + 4)
        q = uq[:, hs].reshape(KQ, P, 4, NOPE + ROPE)
        q = np.concatenate([q[..., :NOPE].reshape(KQ, P, -1), q[..., NOPE:].reshape(KQ, P, -1)], axis=2)
        nq, nkv = N_B + 2 * g, N_B + 2 * g + 1
        W[nq][:, :KQ * 384] = q.transpose(1, 0, 2).reshape(P, -1)
        for i, u in enumerate((uk, uv)):
            W[nkv][:, 512 * i:512 * i + 512] = u[:, hs].reshape(KKV, P, 256).transpose(1, 0, 2).reshape(P, -1)

    def halves(w):
        k, m = w.shape
        return w.reshape(k // 1024, 8, P, m // 256, 256).transpose(0, 3, 2, 1, 4).reshape(k // 1024, m // 256, P, BLK)

    br = W[N_BR:N_OUT].reshape(8, 2, P, BLK)
    br[:, 0] = halves(np.asarray(inputs["w_branch_a"])[0])[0]
    br[:, 1] = halves(np.asarray(inputs["w_branch_b"])[0])[0]
    W[N_OUT:N_MLP] = cols(np.asarray(inputs["w_out"])[0])
    mlp = W[N_MLP:].reshape(CHUNKS, 2, 8, P, BLK)
    mlp[:, 0] = cols(np.asarray(inputs["w_mlp_in"])[0]).reshape(CHUNKS, 8, P, BLK)
    mlp[:, 1] = halves(np.asarray(inputs["w_mlp_out"])[0])

    tab = np.zeros((P, C_ALL), f)
    tab[:, C_ONES:C_ONES + P] = 1.0
    tab[:, C_IDENT:C_IDENT + P] = np.eye(P, dtype=f)
    for c, n in ((C_GATTN, "attn_norm_g"), (C_GMLP, "mlp_norm_g"), (C_GFIN, "final_norm_g"), (C_GQ, "b_q_norm_g"),
                 (C_GKV, "b_kv_norm_g")):
        g = np.asarray(inputs[n]).reshape(-1, P).T
        tab[:, c:c + g.shape[1]] = g
    tab[:, C_SLOPE:C_SLOPE + A_HEADS] = -np.exp2(-8.0 * (np.arange(A_HEADS) + 1.0) / A_HEADS).astype(f) / A_SCALE
    tab[:, C_SINK:C_SINK + A_HEADS] = np.asarray(inputs["a_sink"])
    p = np.arange(P)
    tab[:, C_INVF] = (f(10000.0) ** (-(np.arange(16, dtype=f)) / f(16)))[p % 16]
    tab[:, C_SIGN] = np.where(p % ROPE < ROPE // 2, -1.0, 1.0)
    mask = np.zeros((P, QB, 3 * P), f)
    for qb in range(QB):
        k0, k1 = key_range(qb)
        d = np.abs(P * qb + np.arange(P)[:, None] - np.arange(k0, k1)[None])
        mask[:, qb, :k1 - k0] = np.where(d <= WINDOW, 0.0, 1e30)
    pos = np.asarray(inputs["positions"])[0]
    pos = np.concatenate([np.broadcast_to(pos, (P, S)), pos.reshape(QB, P).T], axis=1)
    xT = np.asarray(inputs["x"])[0].T.reshape(KD, P, S).transpose(1, 0, 2)
    return {"xT": xT, "tab": tab, "pos": pos, "mask": mask, "w": W}


def kernel(**inputs):
    import numpy as np
    import concourse.bacc as bacc
    from concourse.bass_utils import run_bass_kernel_spmd

    nc = bacc.Bacc("TRN2", target_bir_lowering=False, num_devices=1)
    arrays, args = {}, []
    for name, a in layout(inputs).items():
        a = np.ascontiguousarray(a)
        arrays["in_" + name] = a
        args.append(nc.dram_tensor("in_" + name, a.shape, mybir.dt.from_np(a.dtype), kind="ExternalInput").ap())
    args.append(nc.dram_tensor("out_t", (P, KD, S), F32, kind="ExternalOutput").ap())
    build(nc, *args)
    r = run_bass_kernel_spmd(nc, [arrays], core_ids=[0])
    return np.ascontiguousarray(r.results[0]["out_t"].transpose(2, 1, 0).reshape(1, S, D))
```
